# Optimizing a Trainium2 kernel written in Bass

```python
import math
import jax, jax.numpy as jnp
from jax import lax
import numpy as np

D_MODEL = 1024
BATCH = 1
SEQ = 512
DEPTH = 1
DEC_BATCH = 1
DEC_SEQ = 256
PAST_LEN = 128

ATT_HEADS = 16
ATT_KV_HEADS = 4
ATT_HEAD_DIM = 64
ATT_GROUP = ATT_HEADS // ATT_KV_HEADS
WINDOW = 128
ATT_BLOCK = 128
ATT_Q = ATT_HEADS * ATT_HEAD_DIM
ATT_KV = ATT_KV_HEADS * ATT_HEAD_DIM

HGRN_HEADS = 8
HGRN_DK = 128
HGRN_DV = 128
HGRN_CHUNK = 32
HG_K = HGRN_HEADS * HGRN_DK
HG_V = HGRN_HEADS * HGRN_DV

IN_SIZES = (ATT_Q, ATT_KV, ATT_KV, HG_K, HG_K, HG_K, HG_V, HG_V, D_MODEL, D_MODEL)
IN_COLS = ATT_Q + 2 * ATT_KV + 3 * HG_K + 2 * HG_V + 2 * D_MODEL

PEER_HEADS = 8
PEER_NKEYS = 128
PEER_EXPERTS = PEER_NKEYS * PEER_NKEYS
PEER_QDIM = 256
PEER_HALF = PEER_QDIM // 2
PEER_TOPK = 16
PEER_CHUNK = 128

EPS = 1e-6

kernel_name = "hybrid_swa_hgrn2_peer_adaln_encoder"

def rmsnorm(x, g):
    xf = x.astype(jnp.float32)
    y = xf * lax.rsqrt(jnp.mean(xf * xf, axis=-1, keepdims=True) + EPS)
    return (y * g.astype(jnp.float32)).astype(x.dtype)

def alibi_slopes():
    h = jnp.arange(1, ATT_HEADS + 1, dtype=jnp.float32)
    return jnp.exp2(-8.0 * h / ATT_HEADS)

def windowed_attention(q, k, v, sink):
    B, S = q.shape[0], q.shape[1]
    nblk = S // ATT_BLOCK
    span = ATT_BLOCK + 2 * WINDOW
    kp = jnp.pad(k, ((0, 0), (WINDOW, WINDOW), (0, 0), (0, 0)))
    vp = jnp.pad(v, ((0, 0), (WINDOW, WINDOW), (0, 0), (0, 0)))
    slopes = alibi_slopes().reshape(ATT_KV_HEADS, ATT_GROUP)
    sinkg = sink.astype(jnp.float32).reshape(ATT_KV_HEADS, ATT_GROUP)[None, :, :, None]
    scale = 1.0 / math.sqrt(ATT_HEAD_DIM)

    def block(j):
        start = j * ATT_BLOCK
        qb = lax.dynamic_slice_in_dim(q, start, ATT_BLOCK, axis=1)
        kb = lax.dynamic_slice_in_dim(kp, start, span, axis=1)
        vb = lax.dynamic_slice_in_dim(vp, start, span, axis=1)
        qpos = start + jnp.arange(ATT_BLOCK)
        kpos = start - WINDOW + jnp.arange(span)
        dist = jnp.abs(qpos[:, None] - kpos[None, :])
        valid = (dist <= WINDOW) & (kpos >= 0)[None, :] & (kpos < S)[None, :]
        s = jnp.einsum('bqhgd,bkhd->bhgqk', qb, kb, preferred_element_type=jnp.float32) * scale
        s = s - slopes[:, :, None, None] * dist.astype(jnp.float32)
        s = jnp.where(valid, s, -jnp.inf)
        m = jnp.maximum(jnp.max(s, axis=-1), sinkg)
        p = jnp.exp(s - m[..., None])
        denom = jnp.sum(p, axis=-1) + jnp.exp(sinkg - m)
        o = jnp.einsum('bhgqk,bkhd->bqhgd', p, vb.astype(jnp.float32))
        o = o / jnp.transpose(denom, (0, 3, 1, 2))[..., None]
        return o.astype(q.dtype)

    out = lax.map(block, jnp.arange(nblk))
    return jnp.moveaxis(out, 0, 1).reshape(B, S, ATT_Q)

def hgrn2_scan(q, logf, kk, v):
    B, S, H, _ = q.shape
    C = HGRN_CHUNK
    nC = S // C

    def to_chunks(a):
        return jnp.transpose(a.reshape(B, nC, C, H, a.shape[-1]), (1, 0, 3, 2, 4))

    mask = jnp.tril(jnp.ones((C, C), dtype=bool))[None, None, :, :, None]

    def step(state, inp):
        qc, lfc, kc, vc = inp
        b = jnp.cumsum(lfc, axis=2)
        o_inter = jnp.einsum('bhtk,bhkv->bhtv', qc * jnp.exp(b), state)
        diff = jnp.where(mask, b[:, :, :, None, :] - b[:, :, None, :, :], -jnp.inf)
        A = jnp.einsum('bhtk,bhtsk,bhsk->bhts', qc, jnp.exp(diff), kc)
        o = o_inter + jnp.einsum('bhts,bhsv->bhtv', A, vc)
        b_last = b[:, :, -1:, :]
        new_state = jnp.exp(b_last[:, :, 0, :])[..., None] * state + jnp.einsum(
            'bhsk,bhsv->bhkv', kc * jnp.exp(b_last - b), vc)
        return new_state, o

    s0 = jnp.zeros((B, H, q.shape[-1], v.shape[-1]), jnp.float32)
    _, o = lax.scan(step, s0, (to_chunks(q), to_chunks(logf), to_chunks(kk), to_chunks(v)))
    return jnp.transpose(o, (1, 0, 3, 2, 4)).reshape(B, S, H, v.shape[-1])

def lower_bound(p_lb, layer):
    lb = jnp.cumsum(jax.nn.softmax(p_lb.astype(jnp.float32), axis=0), axis=0)[layer]
    return lb.reshape(HGRN_HEADS, HGRN_DK)

def hgrn2_direction(qh, z, ih, lb, reverse):
    zf = z.astype(jnp.float32)
    f = lb + (1.0 - lb) * jax.nn.sigmoid(zf)
    kk = (1.0 - lb) * jax.nn.sigmoid(-zf)
    logf = jnp.log(f)
    if reverse:
        o = hgrn2_scan(jnp.flip(qh, 1), jnp.flip(logf, 1), jnp.flip(kk, 1), jnp.flip(ih, 1))
        return jnp.flip(o, 1)
    return hgrn2_scan(qh, logf, kk, ih)

def peer(h, w_pq, keys, u, v):
    B, S, D = h.shape
    hc = h.reshape(-1, PEER_CHUNK, D)
    T = PEER_CHUNK

    def chunk(xc):
        q = (xc @ w_pq).reshape(T, PEER_HEADS, 2, PEER_HALF)
        s = jnp.einsum('thpd,hpnd->thpn', q, keys, preferred_element_type=jnp.float32)
        sv, si = lax.top_k(s, PEER_TOPK)
        cand = sv[:, :, 0, :, None] + sv[:, :, 1, None, :]
        cand_id = si[:, :, 0, :, None] * PEER_NKEYS + si[:, :, 1, None, :]
        top_s, pos = lax.top_k(cand.reshape(T, PEER_HEADS, PEER_TOPK * PEER_TOPK), PEER_TOPK)
        eid = jnp.take_along_axis(cand_id.reshape(T, PEER_HEADS, PEER_TOPK * PEER_TOPK), pos, axis=-1)
        gate = jax.nn.softmax(top_s, axis=-1)
        ue = u[eid]
        act = jax.nn.gelu(jnp.einsum('thkd,td->thk', ue, xc, preferred_element_type=jnp.float32),
                          approximate=False)
        ve = v[eid]
        return jnp.einsum('thk,thkd->td', (gate * act).astype(xc.dtype), ve)

    return lax.map(chunk, hc).reshape(B, S, D)

def encoder_layer(x, c, layer, w_mod, b_mod, g_norm1, w_in, att_sink, p_lb_fwd, p_lb_bwd,
                  g_hnorm, w_o_att, w_o_hgrn, w_out, g_norm2, w_pq, peer_keys, peer_u, peer_v):
    B, S, D = x.shape
    mod = jax.nn.silu(c) @ w_mod + b_mod
    shift1, scale1, gate1, shift2, scale2, gate2 = [m[:, None, :] for m in jnp.split(mod, 6, axis=-1)]

    h = rmsnorm(x, g_norm1) * (1.0 + scale1) + shift1
    proj = h @ w_in
    cuts = np.cumsum(IN_SIZES)[:-1].tolist()
    qa, ka, va, qh, zf, zb, ih, gh, ga, gb = jnp.split(proj, cuts, axis=-1)

    att = windowed_attention(qa.reshape(B, S, ATT_KV_HEADS, ATT_GROUP, ATT_HEAD_DIM),
                             ka.reshape(B, S, ATT_KV_HEADS, ATT_HEAD_DIM),
                             va.reshape(B, S, ATT_KV_HEADS, ATT_HEAD_DIM), att_sink)
    y_att = att @ w_o_att

    qf = jax.nn.silu(qh.astype(jnp.float32)).reshape(B, S, HGRN_HEADS, HGRN_DK)
    iv = ih.astype(jnp.float32).reshape(B, S, HGRN_HEADS, HGRN_DV)
    o = (hgrn2_direction(qf, zf.reshape(B, S, HGRN_HEADS, HGRN_DK), iv, lower_bound(p_lb_fwd, layer), False)
         + hgrn2_direction(qf, zb.reshape(B, S, HGRN_HEADS, HGRN_DK), iv, lower_bound(p_lb_bwd, layer), True))
    o = o * lax.rsqrt(jnp.mean(o * o, axis=-1, keepdims=True) + EPS)
    o = o * g_hnorm.astype(jnp.float32).reshape(HGRN_HEADS, HGRN_DV)
    o = o * jax.nn.silu(gh.astype(jnp.float32)).reshape(B, S, HGRN_HEADS, HGRN_DV)
    y_hg = o.reshape(B, S, HG_V).astype(x.dtype) @ w_o_hgrn

    merged = jax.nn.sigmoid(ga) * y_att + jax.nn.sigmoid(gb) * y_hg
    x = x + gate1 * (merged @ w_out)

    h2 = rmsnorm(x, g_norm2) * (1.0 + scale2) + shift2
    x = x + gate2 * peer(h2, w_pq, peer_keys, peer_u, peer_v)
    return x

def setup_inputs(seed: int = 0) -> dict:
    key = jax.random.key(seed)
    ks = jax.random.split(key, 21)
    f32 = jnp.float32
    nrm = lambda k, shape, s: jax.random.normal(k, shape, f32) * s
    D = D_MODEL
    return {
        "x_prompt": nrm(ks[0], (BATCH, SEQ, D), 1.0),
        "x_sample": nrm(ks[1], (DEC_BATCH, DEC_SEQ, D), 1.0),
        "c_prompt": nrm(ks[2], (BATCH, D), 1.0),
        "c_sample": nrm(ks[3], (DEC_BATCH, D), 1.0),
        "w_mod": nrm(ks[4], (DEPTH, D, 6 * D), 0.5 * D ** -0.5),
        "b_mod": nrm(ks[5], (DEPTH, 6 * D), 0.02),
        "g_norm1": 1.0 + nrm(ks[6], (DEPTH, D), 0.02),
        "w_in": nrm(ks[7], (DEPTH, D, IN_COLS), D ** -0.5),
        "att_sink": nrm(ks[8], (DEPTH, ATT_HEADS), 0.5),
        "p_lb_fwd": nrm(ks[9], (DEPTH + 1, HG_K), 0.1),
        "p_lb_bwd": nrm(ks[10], (DEPTH + 1, HG_K), 0.1),
        "g_hnorm": 1.0 + nrm(ks[11], (DEPTH, HG_V), 0.02),
        "w_o_att": nrm(ks[12], (DEPTH, ATT_Q, D), ATT_Q ** -0.5),
        "w_o_hgrn": nrm(ks[13], (DEPTH, HG_V, D), HG_V ** -0.5),
        "w_out": nrm(ks[14], (DEPTH, D, D), D ** -0.5),
        "g_norm2": 1.0 + nrm(ks[15], (DEPTH, D), 0.02),
        "w_pq": nrm(ks[16], (DEPTH, D, PEER_HEADS * PEER_QDIM), D ** -0.5),
        "peer_keys": nrm(ks[17], (DEPTH, PEER_HEADS, 2, PEER_NKEYS, PEER_HALF), PEER_HALF ** -0.5),
        "peer_u": nrm(ks[18], (DEPTH, PEER_EXPERTS, D), D ** -0.5),
        "peer_v": nrm(ks[19], (DEPTH, PEER_EXPERTS, D), PEER_HEADS ** -0.5),
        "g_final": 1.0 + nrm(ks[20], (D,), 0.02),
    }

def reference(x_prompt, x_sample, c_prompt, c_sample, w_mod, b_mod, g_norm1, w_in, att_sink,
              p_lb_fwd, p_lb_bwd, g_hnorm, w_o_att, w_o_hgrn, w_out, g_norm2, w_pq, peer_keys,
              peer_u, peer_v, g_final):
    def run(x, c):
        for l in range(DEPTH):
            x = encoder_layer(x, c, l, w_mod[l], b_mod[l], g_norm1[l], w_in[l], att_sink[l],
                              p_lb_fwd, p_lb_bwd, g_hnorm[l], w_o_att[l], w_o_hgrn[l], w_out[l],
                              g_norm2[l], w_pq[l], peer_keys[l], peer_u[l], peer_v[l])
        return rmsnorm(x, g_final)

    y_prompt = run(x_prompt, c_prompt)
    y_sample = run(x_sample, c_sample)
    return (y_prompt, y_sample)


_drawn_inputs = setup_inputs


def setup_inputs(seed=0):
    import zlib

    import numpy as np

    out = dict(_drawn_inputs(seed))
    spreads = {}
    factors = {'b_mod': 3.517,
     'g_norm1': 8.0,
     'att_sink': 8.0,
     'p_lb_fwd': 8.0,
     'p_lb_bwd': 8.0,
     'g_hnorm': 21.819,
     'g_norm2': 52.4,
     'g_final': 8.438}
    for name, (base, spread) in spreads.items():
        noise = np.random.default_rng([zlib.crc32(name.encode()), seed]).standard_normal(out[name].shape)
        drawn = base * np.exp(spread * noise) if base else spread * noise
        out[name] = __import__('jax').numpy.asarray(drawn.astype(out[name].dtype))
    for name, factor in factors.items():
        out[name] = (out[name] * factor).astype(out[name].dtype)
    return out
```

```python
from contextlib import ExitStack

import concourse.bass as bass
import numpy as np
from concourse import mybir

F32 = mybir.dt.float32
F32R = mybir.dt.float32r
U32 = mybir.dt.uint32
ALU = mybir.AluOpType
ACT = mybir.ActivationFunctionType
AX_X = mybir.AxisListType.X
ds = bass.ds

P = 128
D = 1024
DC = D // P
T_PROMPT, T_SAMPLE = 512, 256
T = T_PROMPT + T_SAMPLE
TT = T // P
HALF = T // 2
GROUPS = ((0, T_PROMPT), (T_PROMPT, T))
EPS = 1e-6
KV_HEADS, Q_PER_KV, HD = 4, 4, 64
HEADS = KV_HEADS * Q_PER_KV
H_HEADS = 8
LEVELS = 7
PH, NKEYS, TOPK = 8, 128, 16
EXPERTS = NKEYS * NKEYS
ROW_LEN = [TOPK // (a + 1) for a in range(TOPK)]
CAND = sum(ROW_LEN)

N_ATT = KV_HEADS * 3
N_GATT = 2 * DC
N_HG = H_HEADS * 5
N_GHG = 2 * DC
N_OUT = DC
N_PQ = 2 * PH
U_ATT = 0
U_GATT = U_ATT + N_ATT
U_HG = U_GATT + N_GATT
U_GHG = U_HG + N_HG
U_OUT = U_GHG + N_GHG
U_PQ = U_OUT + N_OUT
UNITS = U_PQ + N_PQ
LEAD = 4
N_MOD = 6 * DC
MOD_LOT = 4

V_BMOD, V_G1, V_G2, V_GF, V_GH = 0, 48, 56, 64, 72
V_LB = 80
V_C = 112
V_SINK = 128
V_N = V_SINK + HEADS
C_ID, C_ONE, C_IOTA, C_SLOPE, C_MASK = 0, 128, 256, 384, 400
C_DIST = C_MASK + LEVELS * P
C_N = C_DIST + 3 * P
C_KEEP = C_MASK

BLOCKS = []
for g0, g1 in ((0, T_PROMPT // P), (T_PROMPT // P, TT)):
    for q in range(g0, g1):
        k0, k1 = max(g0, q - 1), min(g1 - 1, q + 1)
        BLOCKS.append((q, k0, k1 - k0 + 1, (k0 - q + 1) * P))
B_OFF = [P * sum(b[2] for b in BLOCKS[:i]) for i in range(TT + 1)]
N_KT = sum(b[2] for b in BLOCKS)


def encoder_kernel(nc, x_t, vecs, consts, w_mod, w_str, keys_t, u_t, v_t, out):
    with ExitStack() as ctx:
        def sb(name, shape, dt=F32):
            return ctx.enter_context(nc.sbuf_tensor(name, shape, dt))

        def sem(name):
            return ctx.enter_context(nc.semaphore(name))

        acts_a = sb("acts_a", [P, 2, DC, T], F32R)
        acts_b = sb("acts_b", [P, 2, DC, T], F32R)
        w_split = sb("w_split", [P, 2, 2, DC, P], F32R)
        w_raw = sb("w_raw", [P, 2, DC, P])
        cst = sb("cst", [P, C_KEEP])
        vec = sb("vec", [P, V_N])
        mod = sb("mod", [P, 6 * DC, 2])
        lb = sb("lb", [P, 2, 2, H_HEADS])
        ARENA = 19200
        g_more = sb("g_more", [P, 3 * T], F32R)
        arena = sb("arena", [P, ARENA])
        psum = ctx.enter_context(nc.psum_tensor("psum", [P, 8, 512], F32))
        m_dram = nc.dram_tensor("m_scratch", (DC, P, T), F32, kind="Internal").ap()
        x1_dram = nc.dram_tensor("x1_scratch", (P, DC * T), F32, kind="Internal").ap()

        class Arena:
            def __init__(self):
                self.at = 0

            def take(self, *shape):
                n = int(np.prod(shape))
                ap = arena[:, self.at:self.at + n]
                self.at += n
                assert self.at <= ARENA, self.at
                if len(shape) == 2:
                    ap = ap.rearrange("p (a b) -> p a b", a=shape[0])
                elif len(shape) == 3:
                    ap = ap.rearrange("p (a b c) -> p a b c", a=shape[0], b=shape[1])
                return ap

        ident, ones = cst[:, C_ID:C_ID + P], cst[:, C_ONE:C_ONE + P]
        iota = cst[:, C_IOTA:C_IOTA + P]

        def modcol(which, d, g):
            return mod[:, which * DC + d, g:g + 1]
        SHIFT1, SCALE1, GATE1, SHIFT2, SCALE2, GATE2 = range(6)

        raw_ready = [sem("raw_ready0"), sem("raw_ready1")]
        hi_ready, lo_ready = sem("hi_ready"), sem("lo_ready")
        w_used = sem("w_used")
        proj_free = [sem("proj_free0"), sem("proj_free1")]

        def load_unit(sp, n, s):
            sp.dma_start(w_raw[:, s], w_str[ds(n, 1)].rearrange("o p (c k) -> p (o c) k", c=DC)
                         ).then_inc(raw_ready[s], 16)

        def load_ahead(sp, n, u):
            sp.wait_ge(lo_ready, n + 3)
            load_unit(sp, n + LEAD, u % 2)

        def split_lo(dve, n, u):
            dve.wait_ge(hi_ready, n + 3)
            nc.vector.tensor_tensor(w_split[:, u % 2, 1], w_raw[:, u % 2],
                                    w_split[:, u % 2, 0].bitcast(F32), ALU.subtract).then_inc(lo_ready, 1)

        class Unit:
            def __init__(self, base, it=None, per=0):
                assert base % 2 == 0 and per % 2 == 0
                self.base, self.it, self.per = base, it, per

            def at(self, u):
                return self.base + u if self.it is None else self.it * self.per + (self.base + u)

            def half(self, u):
                h = (self.base + u) // 2
                return h if self.it is None else self.it * (self.per // 2) + h

        def do_load(sp, U, u):
            load_ahead(sp, U.at(u), u)

        def do_hi(act, U, u):
            act.wait_ge(raw_ready[u % 2], U.half(u) * 16 + 32)
            act.wait_ge(w_used, U.at(u) + 1)
            nc.scalar.activation(w_split[:, u % 2, 0], w_raw[:, u % 2], ACT.Copy).then_inc(hi_ready, 1)

        def do_lo(dve, U, u):
            split_lo(dve, U.at(u), u)

        def project(pe, U, u, a, tokens_out=False):
            s = u % 2
            pe.wait_ge(lo_ready, U.at(u) + 1)
            pe.wait_ge(proj_free[s], U.half(u) + 1)
            passes = ((0, 0), (0, 1), (1, 0))
            n_tiles = TT if tokens_out else 2
            for t in range(n_tiles):
                for d in range(DC):
                    for i, (wh, ah) in enumerate(passes):
                        if tokens_out:
                            o = psum[:, 2 * s + t // 3, t % 3 * P:t % 3 * P + P]
                            l, r = a[:, ah, d, t * P:(t + 1) * P], w_split[:, s, wh, d, :]
                        else:
                            o = psum[:, 2 * s + t, 0:HALF]
                            l, r = w_split[:, s, wh, d, :], a[:, ah, d, t * HALF:(t + 1) * HALF]
                        last = nc.tensor.matmul(o, l, r, start=(d == 0 and i == 0),
                                                stop=(d == DC - 1 and i == 2))
            last.then_inc(w_used, 1)

        def proj_out(u, parts=slice(0, P)):
            return psum[parts, 2 * (u % 2):2 * (u % 2) + 2, 0:HALF]

        def two(ap):
            return ap.rearrange("p (a b) -> p a b", a=2)

        A = Arena()
        wm = A.take(2, MOD_LOT, D)
        cs, cg = A.take(16), A.take(16)
        lbt = A.take(4, 8)
        d_vec, d_cst, d_wm = sem("d_vec"), sem("d_cst"), [sem("d_wm0"), sem("d_wm1")]
        mod_a, mod_v, mod_used, mod_done = sem("mod_a"), sem("mod_v"), sem("mod_used"), sem("mod_done")
        with nc.Block() as block:
            @block.sync
            def _(sp):
                sp.dma_start(vec[:], vecs).then_inc(d_vec, 16)
                sp.dma_start(cst[:], consts[:, 0:C_KEEP]).then_inc(d_cst, 16)
                for lot in range(N_MOD // MOD_LOT):
                    if lot >= 2:
                        sp.wait_ge(mod_used, lot - 1)
                    sp.dma_start(wm[:, lot % 2], w_mod[lot * MOD_LOT:(lot + 1) * MOD_LOT]
                                 .rearrange("u p k -> p u k")).then_inc(d_wm[lot % 2], 16)
                for n in range(2):
                    load_unit(sp, n, n)

            @block.scalar
            def _(act):
                act.wait_ge(d_vec, 16)
                nc.scalar.activation(cg, vec[:, V_C:V_C + 16], ACT.Sigmoid).then_inc(mod_a, 1)
                act.wait_ge(mod_v, 2)
                nc.scalar.activation(lbt, lbt, ACT.Exp).then_inc(mod_a, 1)

            @block.vector
            def _(dve):
                p_lb = vec[:, V_LB:V_LB + 32].rearrange("p (d l h) -> p d l h", d=2, l=2)
                e_lb = lbt.rearrange("p (d l) h -> p d l h", d=2)
                dve.wait_ge(d_vec, 16)
                nc.vector.tensor_tensor(lb[:, 0], p_lb[:, :, 0], p_lb[:, :, 1], ALU.max).then_inc(mod_v, 1)
                dve.wait_ge(mod_v, 1)
                for l in range(2):
                    m = nc.vector.tensor_tensor(e_lb[:, :, l], p_lb[:, :, l], lb[:, 0], ALU.subtract)
                m.then_inc(mod_v, 1)
                dve.wait_ge(mod_a, 1)
                nc.vector.tensor_tensor(cs, cg, vec[:, V_C:V_C + 16], ALU.mult).then_inc(mod_v, 1)
                dve.wait_ge(mod_a, 2)
                nc.vector.tensor_tensor(lb[:, 1], e_lb[:, :, 0], e_lb[:, :, 1], ALU.add).then_inc(mod_v, 1)
                dve.wait_ge(mod_v, 4)
                nc.vector.reciprocal(lb[:, 1], lb[:, 1]).then_inc(mod_v, 1)
                dve.wait_ge(mod_v, 5)
                nc.vector.tensor_tensor(lb[:, 0], e_lb[:, :, 0], lb[:, 1], ALU.mult).then_inc(mod_v, 1)
                dve.wait_ge(mod_v, 6)
                nc.vector.tensor_scalar(lb[:, 1], lb[:, 0], -1.0, 1.0, ALU.mult, ALU.add).then_inc(mod_v, 1)
                dve.wait_ge(mod_used, N_MOD // MOD_LOT)
                for g in range(2):
                    m = nc.vector.tensor_tensor(mod[:, :, g],
                                                psum[:, 0, 0:2 * N_MOD].rearrange("p (n g) -> p n g", g=2)[:, :, g],
                                                vec[:, V_BMOD:V_BMOD + N_MOD], ALU.add)
                m.then_inc(mod_v, 1)
                dve.wait_ge(mod_v, 8)
                for which, v in ((SCALE1, V_G1), (SCALE2, V_G2)):
                    for g in range(2):
                        col = mod[:, which * DC:(which + 1) * DC, g]
                        nc.vector.scalar_tensor_tensor(out=col, in0=col, scalar=1.0, in1=vec[:, v:v + DC],
                                                       op0=ALU.add, op1=ALU.mult).then_inc(mod_done, 1)

            @block.tensor
            def _(pe):
                pe.wait_ge(mod_v, 3)
                for lot in range(N_MOD // MOD_LOT):
                    pe.wait_ge(d_wm[lot % 2], 16 * (lot // 2 + 1))
                    for k in range(MOD_LOT):
                        n = lot * MOD_LOT + k
                        for d in range(DC):
                            last = nc.tensor.matmul(psum[:, 0, 2 * n:2 * n + 2], wm[:, lot % 2, k, d * P:(d + 1) * P],
                                                    cs[:, 2 * d:2 * d + 2], start=(d == 0), stop=(d == DC - 1))
                    last.then_inc(mod_used, 1)

        def norm_phase(name, x, load, scale_of, shift_of, dest=None, first=False, work=None,
                       wait_load=True, store=None):
            A = work
            sq, r, hx, hf = A.take(2, T), A.take(T), A.take(2, T), A.take(2, T)
            n_x, n_sq, n_ps = sem(name + "_x"), sem(name + "_sq"), sem(name + "_ps")
            n_r, n_root, n_hx, n_hf = sem(name + "_r"), sem(name + "_root"), sem(name + "_hx"), sem(name + "_hf")
            n_hi, n_lo = sem(name + "_hi"), sem(name + "_lo")
            with nc.Block() as block:
                @block.sync
                def _(sp):
                    if load is not None:
                        load(sp, n_x)
                        if not wait_load:
                            sp.wait_ge(n_x, 16)
                    if store is not None:
                        for d in range(DC):
                            sp.wait_ge(n_hf, 2 * d + 2)
                            sp.dma_start(store[:, d * T:(d + 1) * T], x[:, d]).then_inc(n_x, 16)
                        sp.wait_ge(n_x, 16 * DC)
                    if first:
                        for n in range(2, 4):
                            sp.wait_ge(lo_ready, n - 1)
                            load_unit(sp, n, n % 2)

                @block.scalar
                def _(act):
                    if first:
                        for s in range(2):
                            act.wait_ge(raw_ready[s], 16)
                            nc.scalar.activation(w_split[:, s, 0], w_raw[:, s], ACT.Copy).then_inc(hi_ready, 1)
                    if load is not None and wait_load:
                        act.wait_ge(n_x, 16)
                    for d in range(DC):
                        if d >= 2:
                            act.wait_ge(n_ps, d - 1)
                        nc.scalar.activation(sq[:, d % 2], x[:, d], ACT.Square).then_inc(n_sq, 1)
                    act.wait_ge(n_r, 1)
                    nc.scalar.activation(r, r, ACT.Sqrt).then_inc(n_root, 1)
                    if dest is not None:
                        for d in range(DC):
                            act.wait_ge(n_hf, 2 * d + 2)
                            nc.scalar.activation(dest[:, 0, d], hf[:, d % 2], ACT.Copy).then_inc(n_hi, 1)

                @block.tensor
                def _(pe):
                    for d in range(DC):
                        pe.wait_ge(n_sq, d + 1)
                        for t in range(2):
                            m = nc.tensor.matmul(psum[:, 4 + t, 0:HALF], ones, sq[:, d % 2, t * HALF:(t + 1) * HALF],
                                                 start=(d == 0), stop=(d == DC - 1))
                        m.then_inc(n_ps, 1)

                @block.vector
                def _(dve):
                    if first:
                        for s in range(2):
                            dve.wait_ge(hi_ready, s + 1)
                            nc.vector.tensor_tensor(w_split[:, s, 1], w_raw[:, s], w_split[:, s, 0].bitcast(F32),
                                                    ALU.subtract).then_inc(lo_ready, 1)
                        for s in range(2):
                            dve.sem_inc(proj_free[s], 1)
                    dve.wait_ge(n_ps, DC)
                    nc.vector.tensor_scalar(two(r), psum[:, 4:6, 0:HALF], 1.0 / D, EPS, ALU.mult, ALU.add
                                            ).then_inc(n_r, 1)
                    dve.wait_ge(n_root, 1)
                    nc.vector.reciprocal(r, r).then_inc(n_r, 1)
                    dve.wait_ge(n_r, 2)
                    for d in range(DC):
                        if d >= 2:
                            dve.wait_ge(n_hf, 2 * d - 2)
                        nc.vector.tensor_tensor(hx[:, d % 2], x[:, d], r, ALU.mult).then_inc(n_hx, 1)
                        dve.wait_ge(n_hx, d + 1)
                        if dest is not None and d >= 2:
                            dve.wait_ge(n_lo, d - 1)
                        for g, (t0, t1) in enumerate(GROUPS):
                            o = x[:, d, t0:t1] if dest is None else hf[:, d % 2, t0:t1]
                            if shift_of is None:
                                m = nc.vector.tensor_scalar(o, hx[:, d % 2, t0:t1], scale_of(d, g), None, ALU.mult)
                            else:
                                m = nc.vector.tensor_scalar(o, hx[:, d % 2, t0:t1], scale_of(d, g), shift_of(d, g),
                                                            ALU.mult, ALU.add)
                            m.then_inc(n_hf, 1)
                        if dest is not None and d >= 1:
                            dve.wait_ge(n_hi, d)
                            nc.vector.tensor_tensor(dest[:, 1, d - 1], hf[:, (d - 1) % 2],
                                                    dest[:, 0, d - 1].bitcast(F32), ALU.subtract).then_inc(n_lo, 1)
                    if dest is not None:
                        dve.wait_ge(n_hi, DC)
                        nc.vector.tensor_tensor(dest[:, 1, DC - 1], hf[:, (DC - 1) % 2],
                                                dest[:, 0, DC - 1].bitcast(F32), ALU.subtract).then_inc(n_lo, 1)

        A = Arena()
        x_sb = A.take(DC, T)
        norm_phase("n1", x_sb, lambda sp, s: sp.dma_start(x_sb, x_t).then_inc(s, 16),
                   lambda d, g: modcol(SCALE1, d, g), lambda d, g: modcol(SHIFT1, d, g), acts_a, first=True, work=A)


        A = Arena()
        dist = A.take(3 * P)
        kT, vT, qT = A.take(2, T), A.take(T), A.take(2, T)
        vN = A.take(2, TT, HD)
        sc = A.take(2, 2, N_KT * P)
        pT = A.take(2, N_KT, P)
        st = A.take(4, 6 * TT)
        d_dist = sem("d_dist")
        kv_ready, q_ready, v_ready = sem("kv_ready"), sem("q_ready"), sem("v_ready")
        score_ready, work_free = sem("score_ready"), [sem("work_free0"), sem("work_free1")]
        max_done, nmax_ready, sinkd_ready, exp_ready = sem("max_done"), sem("nmax_ready"), sem("sinkd_ready"), sem("exp_ready")
        den_step, prob_ready = sem("den_step"), sem("prob_ready")
        tr_ready, tr_taken, pv_ready, pv_hi = sem("tr_ready"), sem("tr_taken"), sem("pv_ready"), sem("pv_hi")
        TRIPS = KV_HEADS // 2
        PAIR_UNIT = (1, 2, 4, 5)
        SEQ = ["P0", "P1", "V0", "S0", "P2", "S1", "F0", "P3", "F1", "T0", "V1", "P4", "S2", "T1", "P5", "S3",
               "F2", "F3", "T2", "T3"]
        W_PAIR, W_TRIP = 2 * TT + 4, 4 * (2 * TT + 4)
        TR_GROUPS = [(a, min(a + 4, N_KT)) for a in range(0, N_KT, 4)]
        TR_TRIP = 2 + 4 * 2 * len(TR_GROUPS)
        PV_PARTS = ((0, T_PROMPT), (T_PROMPT, T))

        def walk(it):
            w = t = 0
            for step in SEQ:
                kind, k = step[0], int(step[1:])
                yield kind, k, w, t
                w += {"S": 2 * TT, "T": 4}.get(kind, 0)
                t += {"V": 1, "T": 2 * len(TR_GROUPS)}.get(kind, 0)
            assert w == W_TRIP and t == TR_TRIP

        def stat(p, e, k, n=TT):
            return st[:, (p % 2) * 2 + e, k * TT:k * TT + n]

        with nc.Block() as block:
            @block.sync
            def _(sp):
                sp.dma_start(dist, consts[:, C_DIST:C_DIST + 3 * P]).then_inc(d_dist, 16)
                with sp.Fori(0, TRIPS) as it:
                    U = Unit(U_ATT, it, 6)
                    for u in range(6):
                        do_load(sp, U, u)

            @block.tensor
            def _(pe):
                with pe.Fori(0, TRIPS) as it:
                    U = Unit(U_ATT, it, 6)
                    for kind, k, w, t in walk(it):
                        if kind == "P":
                            project(pe, U, k, acts_a)
                        elif kind == "V":
                            pe.wait_ge(kv_ready, it * 2 + (k + 1))
                            pe.wait_ge(tr_taken, it * TR_TRIP + (t + 1))
                            for i in range(TT):
                                m = nc.tensor.matmul(psum[:, 6 + t % 2, i * HD:(i + 1) * HD], vT[:, i * P:(i + 1) * P],
                                                     ident[:, HD:P], start=True, stop=True)
                            m.then_inc(tr_ready, 1)
                        elif kind == "S":
                            kv = k // 2
                            pe.wait_ge(kv_ready, it * 2 + (kv + 1))
                            pe.wait_ge(q_ready, it * 4 + (k + 1))
                            for e in range(2):
                                for i, (q, k0, nk, _) in enumerate(BLOCKS):
                                    wi = w + e * TT + i
                                    pe.wait_ge(work_free[wi % 2], it * (W_TRIP // 2) + (wi // 2 + 1))
                                    hd = slice(e * HD, (e + 1) * HD)
                                    nc.tensor.matmul(psum[:, 4 + wi % 2, 0:nk * P], qT[hd, k % 2, q * P:(q + 1) * P],
                                                     kT[hd, kv, k0 * P:(k0 + nk) * P], start=True, stop=True
                                                     ).then_inc(score_ready, 1)
                        elif kind == "T":
                            kv = k // 2
                            pe.wait_ge(v_ready, it * 2 + (kv + 1))
                            for e in range(2):
                                pe.wait_ge(prob_ready, it * 8 + (2 * k + e + 1))
                                for j, (a, b) in enumerate(TR_GROUPS):
                                    ti = t + e * len(TR_GROUPS) + j
                                    pe.wait_ge(tr_taken, it * TR_TRIP + (ti + 1))
                                    for c in range(a, b):
                                        m = nc.tensor.transpose(psum[:, 6 + ti % 2, (c - a) * P:(c - a + 1) * P],
                                                                sc[:, k % 2, e, c * P:(c + 1) * P], ident)
                                    m.then_inc(tr_ready, 1)
                            for e in range(2):
                                pe.wait_ge(tr_taken, it * TR_TRIP + (t + (e + 1) * len(TR_GROUPS) + 2))
                                for g, (t0, t1) in enumerate(PV_PARTS):
                                    wi = w + 2 * e + g
                                    pe.wait_ge(work_free[wi % 2], it * (W_TRIP // 2) + (wi // 2 + 1))
                                    for i, (q, k0, nk, _) in enumerate(BLOCKS):
                                        if not t0 <= q * P < t1:
                                            continue
                                        for j in range(nk):
                                            m = nc.tensor.matmul(
                                                psum[e * HD:(e + 1) * HD, 4 + wi % 2, q * P - t0:(q + 1) * P - t0],
                                                vN[:, kv, k0 + j, :], pT[:, e, B_OFF[i] // P + j, :],
                                                start=(j == 0), stop=(j == nk - 1))
                                    m.then_inc(pv_ready, 1)

            @block.scalar
            def _(act):
                act.sem_inc(tr_taken, 2)
                with act.Fori(0, TRIPS) as it:
                    U = Unit(U_ATT, it, 6)
                    for kind, k, w, t in walk(it):
                        if kind == "P":
                            act.wait_ge(w_used, U.at(k) + 1)
                            if k in (0, 3):
                                kv = k // 3
                                nc.scalar.activation(two(kT[0:HD, kv]), proj_out(k, slice(0, HD)), ACT.Copy)
                                nc.scalar.activation(two(kT[HD:P, kv]), proj_out(k, slice(0, HD)), ACT.Copy)
                                nc.scalar.activation(two(vT), proj_out(k), ACT.Copy
                                                     ).then_inc(proj_free[k % 2], 1)
                                act.wait_ge(proj_free[k % 2], U.half(k) + 2)
                                act.sem_inc(kv_ready, 1)
                            else:
                                p = PAIR_UNIT.index(k)
                                nc.scalar.activation(two(qT[:, p % 2]), proj_out(k), ACT.Copy, scale=HD ** -0.5
                                                     ).then_inc(proj_free[k % 2], 1)
                                act.wait_ge(proj_free[k % 2], U.half(k) + 2)
                                act.sem_inc(q_ready, 1)
                            do_hi(act, U, k)
                        elif kind == "V":
                            act.wait_ge(tr_ready, it * TR_TRIP + (t + 1))
                            nc.scalar.activation(vN[:, k].rearrange("p a b -> p (a b)"), psum[:, 6 + t % 2, 0:TT * HD],
                                                 ACT.Copy).then_inc(tr_taken, 1)
                            act.wait_ge(tr_taken, it * TR_TRIP + (t + 3))
                            act.sem_inc(v_ready, 1)
                        elif kind == "S":
                            for e in range(2):
                                act.wait_ge(sinkd_ready, it * 8 + (2 * k + e + 1))
                                for i, (q, k0, nk, _) in enumerate(BLOCKS):
                                    s = sc[:, k % 2, e, B_OFF[i]:B_OFF[i + 1]]
                                    nc.scalar.activation(s, s, ACT.Exp, bias=stat(k, e, 1)[:, i:i + 1],
                                                         accum_out=stat(k, e, 3)[:, i:i + 1])
                                nc.scalar.activation(stat(k, e, 4), stat(k, e, 2), ACT.Exp).then_inc(exp_ready, 1)
                        elif kind == "T":
                            for e in range(2):
                                for j, (a, b) in enumerate(TR_GROUPS):
                                    ti = t + e * len(TR_GROUPS) + j
                                    act.wait_ge(tr_ready, it * TR_TRIP + (ti + 1))
                                    nc.scalar.activation(pT[:, e, a:b].rearrange("p a b -> p (a b)"),
                                                         psum[:, 6 + ti % 2, 0:(b - a) * P], ACT.Copy).then_inc(tr_taken, 1)
                            for e in range(2):
                                for g, (t0, t1) in enumerate(PV_PARTS):
                                    wi = w + 2 * e + g
                                    act.wait_ge(pv_ready, it * 16 + (4 * k + 2 * e + g + 1))
                                    dst = acts_b[e * HD:(e + 1) * HD, 0, ds(it * 4 + k, 1), t0:t1]
                                    nc.scalar.activation(dst.rearrange("p o n -> p (o n)"),
                                                         psum[e * HD:(e + 1) * HD, 4 + wi % 2, 0:t1 - t0], ACT.Copy
                                                         ).then_inc(pv_hi, 1)

            @block.vector
            def _(dve):
                for b in range(2):
                    dve.sem_inc(work_free[b], 1)
                dve.wait_ge(d_dist, 16)
                with dve.Fori(0, TRIPS) as it:
                    U = Unit(U_ATT, it, 6)
                    steps = 0
                    for kind, k, w, t in walk(it):
                        if kind == "P":
                            do_lo(dve, U, k)
                        elif kind == "S":
                            for e in range(2):
                                head = it * 8 + (2 * k + e)
                                for i, (q, k0, nk, wc) in enumerate(BLOCKS):
                                    wi = w + e * TT + i
                                    dve.wait_ge(score_ready, it * (8 * TT) + ((2 * k + e) * TT + i + 1))
                                    nc.vector.scalar_tensor_tensor(
                                        out=sc[:, k % 2, e, B_OFF[i]:B_OFF[i + 1]], in0=dist[:, wc:wc + nk * P],
                                        scalar=cst[:, ds(head + C_SLOPE, 1)], in1=psum[:, 4 + wi % 2, 0:nk * P],
                                        op0=ALU.mult, op1=ALU.add).then_inc(work_free[wi % 2], 1)
                                for b in range(2):
                                    dve.wait_ge(work_free[b], it * (W_TRIP // 2) + ((w + e * TT + TT) // 2 + 1))
                                for i in range(TT):
                                    m = nc.vector.reduce_max(stat(k, e, 0)[:, i:i + 1],
                                                             sc[:, k % 2, e, B_OFF[i]:B_OFF[i + 1]], AX_X)
                                m.then_inc(max_done, 1)
                                sink = vec[:, ds(head + V_SINK, 1)]
                                dve.wait_ge(max_done, head + 1)
                                nc.vector.tensor_scalar(stat(k, e, 1), stat(k, e, 0), sink, -1.0, ALU.max, ALU.mult
                                                        ).then_inc(nmax_ready, 1)
                                dve.wait_ge(nmax_ready, head + 1)
                                nc.vector.tensor_scalar(stat(k, e, 2), stat(k, e, 1), sink, None, ALU.add
                                                        ).then_inc(sinkd_ready, 1)
                        elif kind == "F":
                            for e in range(2):
                                dve.wait_ge(exp_ready, it * 8 + (2 * k + e + 1))
                                nc.vector.tensor_tensor(stat(k, e, 5), stat(k, e, 3), stat(k, e, 4), ALU.add
                                                        ).then_inc(den_step, 1)
                                dve.wait_ge(den_step, it * 16 + (steps + 1))
                                nc.vector.reciprocal(stat(k, e, 5), stat(k, e, 5)).then_inc(den_step, 1)
                                dve.wait_ge(den_step, it * 16 + (steps + 2))
                                steps += 2
                                for i in range(TT):
                                    s = sc[:, k % 2, e, B_OFF[i]:B_OFF[i + 1]]
                                    m = nc.vector.tensor_scalar(s, s, stat(k, e, 5)[:, i:i + 1], None, ALU.mult)
                                m.then_inc(prob_ready, 1)
                        elif kind == "T":
                            for e in range(2):
                                for g, (t0, t1) in enumerate(PV_PARTS):
                                    wi = w + 2 * e + g
                                    dve.wait_ge(pv_hi, it * 16 + (4 * k + 2 * e + g + 1))
                                    hd = slice(e * HD, (e + 1) * HD)
                                    hi = acts_b[hd, 0, ds(it * 4 + k, 1), t0:t1].rearrange("p o n -> p (o n)")
                                    lo = acts_b[hd, 1, ds(it * 4 + k, 1), t0:t1].rearrange("p o n -> p (o n)")
                                    nc.vector.tensor_tensor(lo, psum[hd, 4 + wi % 2, 0:t1 - t0], hi.bitcast(F32),
                                                            ALU.subtract).then_inc(work_free[wi % 2], 1)

        def gate_phase(name, u0, last_phase):
            A = Arena()
            sg, m_sb, y = A.take(DC, T), A.take(DC, T), A.take(2, T)
            g_m, g_st, g_y, g_sum, g_hi = (sem(name + k) for k in ("_m", "_st", "_y", "_sum", "_hi"))
            with nc.Block() as block:
                @block.sync
                def _(sp):
                    if last_phase:
                        sp.dma_start(m_sb, m_dram.rearrange("c p t -> p c t")).then_inc(g_m, 16)
                    with sp.Fori(0, DC // 2) as it:
                        for u in range(2):
                            do_load(sp, Unit(u0, it, 2), u)
                    with sp.Fori(0, DC // 2) as it:
                        for u in range(2):
                            do_load(sp, Unit(u0 + DC, it, 2), u)
                            if not last_phase:
                                sp.wait_ge(g_y, it * 2 + (u + 1))
                                sp.dma_start(m_dram[ds(it * 2 + u, 1)].rearrange("o p t -> p (o t)"),
                                             m_sb[:, ds(it * 2 + u, 1)].rearrange("p o t -> p (o t)")
                                             ).then_inc(g_st, 16)
                    if not last_phase:
                        sp.wait_ge(g_st, 16 * DC)

                @block.tensor
                def _(pe):
                    for base, a in ((u0, acts_a), (u0 + DC, acts_b)):
                        with pe.Fori(0, DC // 2) as it:
                            for u in range(2):
                                project(pe, Unit(base, it, 2), u, a)

                @block.scalar
                def _(act):
                    with act.Fori(0, DC // 2) as it:
                        U = Unit(u0, it, 2)
                        for u in range(2):
                            act.wait_ge(w_used, U.at(u) + 1)
                            nc.scalar.activation(sg[:, ds(it * 2 + u, 1)].rearrange("p o (a b) -> p (o a) b", a=2),
                                                 proj_out(u), ACT.Sigmoid).then_inc(proj_free[u], 1)
                            do_hi(act, U, u)
                    with act.Fori(0, DC // 2) as it:
                        U = Unit(u0 + DC, it, 2)
                        for u in range(2):
                            do_hi(act, U, u)
                            if last_phase:
                                act.wait_ge(g_sum, it * 2 + (u + 1))
                                nc.scalar.activation(acts_a[:, 0, ds(it * 2 + u, 1)].rearrange("p o t -> p (o t)"),
                                                     y[:, u], ACT.Copy).then_inc(g_hi, 1)

                @block.vector
                def _(dve):
                    with dve.Fori(0, DC // 2) as it:
                        for u in range(2):
                            do_lo(dve, Unit(u0, it, 2), u)
                    if last_phase:
                        dve.wait_ge(g_m, 16)
                    with dve.Fori(0, DC // 2) as it:
                        U = Unit(u0 + DC, it, 2)
                        for u in range(2):
                            c = it * 2 + u
                            dve.wait_ge(w_used, U.at(u) + 1)
                            dve.wait_ge(proj_free[u], (u0 + DC) // 2 + 1)
                            gate = sg[:, ds(c, 1)].rearrange("p o (a b) -> p (o a) b", a=2)
                            if not last_phase:
                                nc.vector.tensor_tensor(m_sb[:, ds(c, 1)].rearrange("p o (a b) -> p (o a) b", a=2),
                                                        proj_out(u), gate, ALU.mult).then_inc(proj_free[u], 1)
                                dve.wait_ge(proj_free[u], U.half(u) + 2)
                                dve.sem_inc(g_y, 1)
                            else:
                                nc.vector.tensor_tensor(two(y[:, u]), proj_out(u), gate, ALU.mult
                                                        ).then_inc(proj_free[u], 1)
                                dve.wait_ge(proj_free[u], U.half(u) + 2)
                                nc.vector.tensor_tensor(y[:, u], y[:, u], m_sb[:, ds(c, 1)].rearrange("p o t -> p (o t)"),
                                                        ALU.add).then_inc(g_sum, 1)
                            do_lo(dve, U, u)
                            if last_phase:
                                dve.wait_ge(g_hi, c + 1)
                                hi, lo = (acts_a[:, k, ds(c, 1)].rearrange("p o t -> p (o t)") for k in range(2))
                                nc.vector.tensor_tensor(lo, y[:, u], hi.bitcast(F32), ALU.subtract
                                                        ).then_inc(g_y, 1)

        gate_phase("ga", U_GATT, False)

        A = Arena()
        hq, hv, gs = A.take(2, T), A.take(2, T), A.take(2, T)
        Pf, Pb, kf, kb = (A.take(2, T) for _ in range(4))
        Xf, Xb = A.take(T), A.take(T)
        Qs, Ks = A.take(2, T), A.take(2, T)
        At = A.take(T)
        kx, S = A.take(2, 4, P), A.take(2, 4, P)
        masks = A.take(LEVELS, P)
        ksum, sq, rr = Ks[:, 1], Ks[:, 0], Xf
        N_CH = T_PROMPT // P
        ENTER = ({1: 0, 2: 1, 3: 2, 5: 3}, {2: 0, 1: 1, 0: 2, 4: 3})
        MAKE = ((0, 1, 2, 4), (3, 2, 1, 5))
        d_mask, z_ready, f_ready, in_ready = sem("d_mask"), sem("z_ready"), sem("f_ready"), sem("in_ready")
        sum_ready, lev_ready, lev_done = sem("sum_ready"), sem("lev_ready"), sem("lev_done")
        bank_taken, upd_done, upd_step = [sem("bank_taken0"), sem("bank_taken1")], sem("upd_done"), sem("upd_step")
        end_ready, kx_tr, kx_ready, kv_done, st_ready = sem("end_ready"), sem("kx_tr"), sem("kx_ready"), sem("kv_done"), sem("st_ready")
        o_ready, sq_ready, ss_ready, ms_ready, root_ready = sem("o_ready"), sem("sq_ready"), sem("ss_ready"), sem("ms_ready"), sem("root_ready")
        r_step, of_ready, oh_ready, ol_ready = sem("r_step"), sem("of_ready"), sem("oh_ready"), sem("ol_ready")
        HU = 5
        ZF, ZB, QH, GH, IH = range(HU)
        SEQ_H = ["P0", "D0", "L0", "L1", "P1", "L2", "L3", "P2", "L4", "L5", "L6", "P3", "E0", "P4", "E1", "E2", "E3"]

        def halves(ap, B):
            return ap.rearrange("p (n h b) -> p n h b", h=2, b=B)

        def tot(Pr, B, half, direction):
            j = B - 1 if direction == 0 else 0
            a = halves(Pr, B)[:, :, half, j:j + 1]
            return a.broadcast_to([P, T // (2 * B), B]) if B > 1 else a

        def in_unit_act(act, U, u, i, b):
            act.wait_ge(w_used, U.at(u) + 1)
            s = u % 2
            if i in (ZF, ZB):
                Pr, kr = (Pf, kf) if i == ZF else (Pb, kb)
                nc.scalar.activation(two(Pr[:, b]), proj_out(u), ACT.Sigmoid)
                nc.scalar.activation(two(kr[:, b]), proj_out(u), ACT.Sigmoid, scale=-1.0).then_inc(proj_free[s], 1)
            elif i == IH:
                nc.scalar.activation(two(hv[:, b]), proj_out(u), ACT.Copy).then_inc(proj_free[s], 1)
            else:
                nc.scalar.activation(two((hq if i == QH else gs)[:, b]), proj_out(u), ACT.Sigmoid).then_inc(z_ready, 1)
            do_hi(act, U, u)

        def in_unit_dve(dve, U, u, i, b, hd_next):
            s = u % 2
            if i in (ZF, ZB):
                Pr, kr = (Pf, kf) if i == ZF else (Pb, kb)
                lbc, omc = (lb[:, k, i, ds(hd_next, 1)] for k in range(2))
                dve.wait_ge(proj_free[s], U.half(u) + 2)
                nc.vector.tensor_scalar(Pr[:, b], Pr[:, b], omc, lbc, ALU.mult, ALU.add).then_inc(f_ready, 1)
                nc.vector.tensor_scalar(kr[:, b], kr[:, b], omc, None, ALU.mult).then_inc(f_ready, 1)
            elif i in (QH, GH):
                dst = (hq if i == QH else gs)[:, b]
                dve.wait_ge(z_ready, hd_next * 2 + (1 if i == QH else 2))
                nc.vector.tensor_tensor(two(dst), two(dst), proj_out(u), ALU.mult).then_inc(proj_free[s], 1)
            do_lo(dve, U, u)

        BANKS = ((4, 0, T_PROMPT), (5, T_PROMPT, T))
        USES = LEVELS + 2

        def head_pe(pe, hd, b, kind, k):
            def free(bank, use):
                pe.wait_ge(bank_taken[bank], hd * USES + (use + 1))

            if kind in "DL":
                use = 0 if kind == "D" else k + 1
                l, r = (ksum, hq[:, b]) if kind == "D" else (Ks[:, k % 2], Qs[:, k % 2])
                if kind == "D":
                    pe.wait_ge(sum_ready, hd + 1)
                else:
                    pe.wait_ge(lev_ready, hd * LEVELS + (k + 1))
                for bank, (bk, t0, t1) in enumerate(BANKS):
                    free(bank, use)
                    for t in range(t0, t1, P):
                        m = nc.tensor.matmul(psum[:, bk, t - t0:t - t0 + P], l[:, t:t + P], r[:, t:t + P],
                                             start=True, stop=True)
                    m.then_inc(lev_done, 1)
            elif k == 0:
                pe.wait_ge(end_ready, hd + 1)
                for d in range(2):
                    if d == 0:
                        pe.wait_ge(ms_ready, hd + 1)
                    for j, c in enumerate(MAKE[d]):
                        m = nc.tensor.transpose(psum[:, 6 + d, j * P:(j + 1) * P], Ks[:, d, c * P:(c + 1) * P], ident)
                    m.then_inc(kx_tr, 1)
            elif k == 1:
                for d in range(2):
                    pe.wait_ge(kx_ready, hd * 2 + (d + 1))
                    for j, c in enumerate(MAKE[d]):
                        m = nc.tensor.matmul(psum[:, 6 + d, j * P:(j + 1) * P], kx[:, d, j], hv[:, b, c * P:(c + 1) * P],
                                             start=True, stop=True)
                    m.then_inc(kv_done, 1)
            elif k == 2:
                pe.wait_ge(st_ready, hd * 6 + 6)
                for bank, (bk, t0, t1) in enumerate(BANKS):
                    free(bank, LEVELS + 1)
                    for t in range(t0, t1, P):
                        c = t // P
                        o = psum[:, bk, t - t0:t - t0 + P]
                        parts = [(hv[:, b, t:t + P], At[:, t:t + P])]
                        parts += [(S[:, d, ENTER[d][c]], Qs[:, d, t:t + P]) for d in range(2) if c in ENTER[d]]
                        for n, (l, r) in enumerate(parts):
                            m = nc.tensor.matmul(o, l, r, start=(n == 0), stop=(n == len(parts) - 1))
                    m.then_inc(o_ready, 1)
            else:
                for bank, (bk, t0, t1) in enumerate(BANKS):
                    pe.wait_ge(sq_ready, hd * 2 + (bank + 1))
                    nc.tensor.matmul(psum[:, bk + 2, 0:t1 - t0], ones, sq[:, t0:t1], start=True, stop=True
                                     ).then_inc(ss_ready, 1)

        def head_act(act, hd, b, kind, k):
            if kind == "D":
                for bank, (bk, t0, t1) in enumerate(BANKS):
                    act.wait_ge(lev_done, hd * 2 * (LEVELS + 1) + (bank + 1))
                    nc.scalar.activation(At[:, t0:t1], psum[:, bk, 0:t1 - t0], ACT.Copy).then_inc(bank_taken[bank], 1)
            elif kind == "E" and k == 0:
                for d in range(2):
                    act.wait_ge(kx_tr, hd * 2 + (d + 1))
                    nc.scalar.activation(kx[:, d].rearrange("p a b -> p (a b)"), psum[:, 6 + d, :], ACT.Copy
                                         ).then_inc(kx_ready, 1)
            elif kind == "E" and k == 3:
                for bank, (bk, t0, t1) in enumerate(BANKS):
                    act.wait_ge(o_ready, hd * 2 + (bank + 1))
                    nc.scalar.activation(sq[:, t0:t1], psum[:, bk, 0:t1 - t0], ACT.Square).then_inc(sq_ready, 1)
                act.wait_ge(ms_ready, hd + 2)
                nc.scalar.activation(rr, rr, ACT.Sqrt).then_inc(root_ready, 1)
                act.wait_ge(of_ready, hd * 2 + 2)
                nc.scalar.activation(acts_b[:, 0, ds(hd, 1)].rearrange("p o t -> p (o t)"), At, ACT.Copy
                                     ).then_inc(oh_ready, 1)

        def head_dve(dve, hd, b, kind, k):
            q, pf, pb, kf_, kb_ = hq[:, b], Pf[:, b], Pb[:, b], kf[:, b], kb[:, b]
            if kind == "D":
                dve.wait_ge(f_ready, hd * 4 + 4)
                nc.vector.tensor_tensor(ksum, kf_, kb_, ALU.add).then_inc(sum_ready, 1)
                nc.vector.memset(Xf, 1.0).then_inc(upd_step, 1)
                nc.vector.memset(Xb, 1.0).then_inc(upd_step, 1)
            elif kind == "L":
                B = 1 << k
                if k >= 1:
                    dve.wait_ge(lev_done, hd * 2 * (LEVELS + 1) + 2 * k)
                dve.wait_ge(upd_step, hd * (2 + 4 * LEVELS) + 2 + 4 * k)
                Q, K = halves(Qs[:, k % 2], B), halves(Ks[:, k % 2], B)
                for o, a, x, h in ((Q, q, pf, 1), (K, kf_, Xf, 0), (Q, q, pb, 0), (K, kb_, Xb, 1)):
                    m = nc.vector.tensor_tensor(o[:, :, h], halves(a, B)[:, :, h], halves(x, B)[:, :, h], ALU.mult)
                m.then_inc(lev_ready, 1)
                dve.wait_ge(lev_ready, hd * LEVELS + (k + 1))
                for x, pr, h, o, d in ((Xf, pf, 0, 1, 0), (Xb, pb, 1, 0, 1)):
                    xv = halves(x, B)[:, :, h]
                    nc.vector.tensor_tensor(xv, xv, tot(pr, B, o, d), ALU.mult).then_inc(upd_step, 1)
                if k >= 1:
                    dve.wait_ge(lev_done, hd * 2 * (LEVELS + 1) + 2 * k + 2)
                dve.wait_ge(upd_step, hd * (2 + 4 * LEVELS) + 4 + 4 * k)
                for pr, h, o, d in ((pf, 1, 0, 0), (pb, 0, 1, 1)):
                    pv = halves(pr, B)[:, :, h]
                    nc.vector.tensor_tensor(pv, pv, tot(pr, B, o, d), ALU.mult).then_inc(upd_step, 1)
                if k == LEVELS - 1:
                    keep(dve, hd, k - 1)
                    dve.wait_ge(lev_done, hd * 2 * (LEVELS + 1) + 2 * (LEVELS + 1))
                    dve.wait_ge(upd_step, (hd + 1) * (2 + 4 * LEVELS))
                    for o, a, x in ((Qs[:, 0], q, pf), (Qs[:, 1], q, pb), (Ks[:, 0], kf_, Xf), (Ks[:, 1], kb_, Xb)):
                        m = nc.vector.tensor_tensor(o, a, x, ALU.mult)
                    m.then_inc(end_ready, 1)
                    keep(dve, hd, k)
                elif k >= 1:
                    keep(dve, hd, k - 1)
            elif k == 1:
                n = hd * 6
                for d in range(2):
                    dve.wait_ge(kv_done, hd * 2 + (d + 1))
                    D4 = psum[:, 6 + d, :].rearrange("p (a b) -> p a b", a=4)
                    nc.vector.tensor_copy(S[:, d, 0:4:3], D4[:, 0:4:3]).then_inc(st_ready, 1)
                    for j in (1, 2):
                        c = MAKE[d][j]
                        total = pf[:, (c + 1) * P - 1:(c + 1) * P] if d == 0 else pb[:, c * P:c * P + 1]
                        dve.wait_ge(st_ready, n + 3 * d + j)
                        nc.vector.scalar_tensor_tensor(out=S[:, d, j], in0=S[:, d, j - 1], scalar=total, in1=D4[:, j],
                                                       op0=ALU.mult, op1=ALU.add).then_inc(st_ready, 1)
            elif k == 3:
                for bank, (bk, t0, t1) in enumerate(BANKS):
                    dve.wait_ge(ss_ready, hd * 2 + (bank + 1))
                    m = nc.vector.tensor_scalar(rr[:, t0:t1], psum[:, bk + 2, 0:t1 - t0], 1.0 / P, EPS, ALU.mult, ALU.add)
                m.then_inc(ms_ready, 1)
                dve.wait_ge(root_ready, hd + 1)
                nc.vector.reciprocal(rr, rr).then_inc(r_step, 1)
                dve.wait_ge(r_step, hd + 1)
                for bank, (bk, t0, t1) in enumerate(BANKS):
                    nc.vector.tensor_tensor(rr[:, t0:t1], rr[:, t0:t1], psum[:, bk, 0:t1 - t0], ALU.mult
                                            ).then_inc(bank_taken[bank], 1)
                for bank, (bk, t0, t1) in enumerate(BANKS):
                    dve.wait_ge(bank_taken[bank], hd * USES + (USES + 1))
                    nc.vector.scalar_tensor_tensor(out=At[:, t0:t1], in0=rr[:, t0:t1], scalar=vec[:, ds(hd + V_GH, 1)],
                                                   in1=gs[:, b, t0:t1], op0=ALU.mult, op1=ALU.mult).then_inc(of_ready, 1)
                dve.wait_ge(oh_ready, hd + 1)
                hi, lo = (acts_b[:, j, ds(hd, 1)].rearrange("p o t -> p (o t)") for j in range(2))
                nc.vector.tensor_tensor(lo, At, hi.bitcast(F32), ALU.subtract).then_inc(ol_ready, 1)

        def keep(dve, hd, l):
            for bank, (bk, t0, t1) in enumerate(BANKS):
                n = (t1 - t0) // P
                mask = masks[:, l:l + 1].bitcast(U32).broadcast_to([P, n, P])
                nc.vector.copy_predicated(At[:, t0:t1].rearrange("p (n b) -> p n b", n=n), mask,
                                          psum[:, bk, 0:t1 - t0].rearrange("p (n b) -> p n b", n=n)
                                          ).then_inc(bank_taken[bank], 1)

        def run_heads(eng, head_fn, unit_fn, after=None):
            for i in range(HU):
                unit_fn(Unit(U_HG), i, i, 0, 0)
            with eng.Fori(0, H_HEADS // 2 - 1) as it:
                for b in range(2):
                    for step in SEQ_H:
                        kind, k = step[0], int(step[1:])
                        if kind == "P":
                            unit_fn(Unit(U_HG, it, 2 * HU), (b + 1) * HU + k, k, 1 - b, it * 2 + (b + 1))
                        else:
                            head_fn(eng, it * 2 + b, b, kind, k)
            for hd in range(H_HEADS - 2, H_HEADS):
                for step in SEQ_H:
                    kind, k = step[0], int(step[1:])
                    if kind == "P":
                        if hd + 1 < H_HEADS:
                            unit_fn(Unit(U_HG), (hd + 1) * HU + k, k, (hd + 1) % 2, hd + 1)
                    else:
                        head_fn(eng, hd, hd % 2, kind, k)

        with nc.Block() as block:
            @block.sync
            def _(sp):
                sp.dma_start(masks, consts[:, C_MASK:C_MASK + LEVELS * P].rearrange("p (a b) -> p a b", a=LEVELS)
                             ).then_inc(d_mask, 16)
                with sp.Fori(0, N_HG // 2) as it:
                    for u in range(2):
                        do_load(sp, Unit(U_HG, it, 2), u)

            @block.tensor
            def _(pe):
                run_heads(pe, head_pe, lambda U, u, i, b, h: project(pe, U, u, acts_a, tokens_out=(i == IH)))

            @block.scalar
            def _(act):
                run_heads(act, head_act, lambda U, u, i, b, h: in_unit_act(act, U, u, i, b))

            @block.vector
            def _(dve):
                for b in range(2):
                    dve.sem_inc(bank_taken[b], 1)
                dve.sem_inc(ms_ready, 1)
                dve.wait_ge(d_mask, 16)
                run_heads(dve, head_dve, lambda U, u, i, b, h: in_unit_dve(dve, U, u, i, b, h))

        gate_phase("gb", U_GHG, True)

        A = Arena()
        x1 = A.take(DC, T)
        x1_flat = arena[:, 0:DC * T]
        d_x1, x1_done = sem("d_x1"), sem("x1_done")
        PIECES = ((0, 0, HALF, 0), (1, HALF, T_PROMPT, 0), (1, T_PROMPT, T, 1))
        with nc.Block() as block:
            @block.sync
            def _(sp):
                sp.dma_start(x1_flat, x_t).then_inc(d_x1, 16)
                with sp.Fori(0, DC // 2) as it:
                    for u in range(2):
                        do_load(sp, Unit(U_OUT, it, 2), u)

            @block.tensor
            def _(pe):
                with pe.Fori(0, DC // 2) as it:
                    for u in range(2):
                        project(pe, Unit(U_OUT, it, 2), u, acts_a)

            @block.scalar
            def _(act):
                with act.Fori(0, DC // 2) as it:
                    for u in range(2):
                        do_hi(act, Unit(U_OUT, it, 2), u)

            @block.vector
            def _(dve):
                dve.wait_ge(d_x1, 16)
                with dve.Fori(0, DC // 2) as it:
                    U = Unit(U_OUT, it, 2)
                    for u in range(2):
                        dve.wait_ge(w_used, U.at(u) + 1)
                        for bank, t0, t1, g in PIECES:
                            x = x1[:, ds(it * 2 + u, 1), t0:t1].rearrange("p o t -> p (o t)")
                            gate = mod[:, ds(it * 2 + (GATE1 * DC + u), 1), g:g + 1].rearrange("p o t -> p (o t)")
                            m = nc.vector.scalar_tensor_tensor(
                                out=x, in0=psum[:, 2 * u + bank, t0 - bank * HALF:t1 - bank * HALF], scalar=gate,
                                in1=x, op0=ALU.mult, op1=ALU.add)
                        m.then_inc(proj_free[u], 1)
                        do_lo(dve, U, u)
        norm_phase("n2", x1, lambda sp, s: sp.dma_start(x1_dram, x1_flat).then_inc(s, 16),
                   lambda d, g: modcol(SCALE2, d, g), lambda d, g: modcol(SHIFT2, d, g), acts_a, work=A,
                   wait_load=False)

        A = Arena()
        KH = TOPK // 2
        keys = A.take(2 * PH * NKEYS)
        qh_sb, s_sb, s_cut = A.take(2, T), A.take(2, TT, NKEYS), A.take(TT, NKEYS)
        sv = A.take(2, TT, TOPK)
        si = A.take(2, TT, TOPK).bitcast(U32)
        sf = A.take(2, TT, TOPK)
        cv, cid, cv_cut = A.take(TT, CAND), A.take(TT, CAND), A.take(TT, CAND)
        tv = A.take(TT, TOPK)
        tp = A.take(TT, TOPK).bitcast(U32)
        tpf, te, tsum = A.take(TT, TOPK), A.take(TT, TOPK), A.take(TT)
        onehot = A.take(TOPK, CAND)
        eid, gate = A.take(TT, PH * TOPK), A.take(TT, PH * TOPK)
        ei = A.take(TT, PH * TOPK).bitcast(U32)
        te_ji, te_j = A.take(TT, PH * TOPK).bitcast(U32), A.take(TT, PH * TOPK)
        pad = A.take(2)
        gate_t, i_t = w_raw[:].rearrange("p a b c -> p (a b c)")[:, 0:T], w_raw[:].rearrange("p a b c -> p (a b c)")[:, T:2 * T]
        j_t = arena[:, ARENA - T:ARENA]
        d_keys, qh_ready, s_done, s_ready = sem("d_keys"), sem("qh_ready"), sem("s_done"), sem("s_ready")
        s_bank = [sem("s_bank0"), sem("s_bank1")]
        k_step, sf_ready, cid_ready, ts_ready, te_ready, head_done = (
            sem(n) for n in ("k_step", "sf_ready", "cid_ready", "ts_ready", "te_ready", "head_done"))
        tab_tr, tab_done, slot_free = sem("tab_tr"), sem("tab_done"), sem("slot_free")
        STEPS = 35
        rows = []
        at = 0
        for a in range(TOPK):
            rows.append((a, at, ROW_LEN[a]))
            at += ROW_LEN[a]
        SINGLE = TOPK // 2

        def pair_sums(eng_tt, out, first, second):
            for a, o, n in rows[:SINGLE]:
                m = eng_tt(out[:, :, o:o + n], second[:, :, 0:n], first[:, :, a:a + 1].broadcast_to([P, TT, n]), ALU.add)
            o = rows[SINGLE][1]
            return eng_tt(out[:, :, o:o + TOPK - SINGLE], first[:, :, SINGLE:TOPK],
                          second[:, :, 0:1].broadcast_to([P, TT, TOPK - SINGLE]), ALU.add)

        with nc.Block() as block:
            @block.sync
            def _(sp):
                sp.dma_start(keys, keys_t).then_inc(d_keys, 16)
                with sp.Fori(0, PH) as it:
                    for u in range(2):
                        do_load(sp, Unit(U_PQ, it, 2), u)

            @block.tensor
            def _(pe):
                def scores(n, u, hp):
                    pe.wait_ge(qh_ready, n + 1)
                    pe.wait_ge(s_bank[0], n + 1)
                    for t in range(TT):
                        m = nc.tensor.matmul(psum[:, 4 + t // 4, t % 4 * P:t % 4 * P + P],
                                             qh_sb[:, u, t * P:(t + 1) * P], keys[:, ds(hp, NKEYS)],
                                             start=True, stop=True)
                    m.then_inc(s_done, 1)
                pe.wait_ge(d_keys, 16)
                with pe.Fori(0, PH) as it:
                    project(pe, Unit(U_PQ, it, 2), 0, acts_a)
                    project(pe, Unit(U_PQ, it, 2), 1, acts_a)
                    for u in range(2):
                        scores(it * 2 + u, u, (it * 2 + u) * NKEYS)
                pe.wait_ge(tab_done, 1)
                for k, tab in enumerate((gate, eid, te_j)):
                    for t in range(TT):
                        m = nc.tensor.transpose(psum[:, 2 * k + t // 4, t % 4 * P:t % 4 * P + P], tab[:, t], ident)
                    m.then_inc(tab_tr, 1)

            @block.scalar
            def _(act):
                with act.Fori(0, PH) as it:
                    U = Unit(U_PQ, it, 2)
                    for u in range(2):
                        act.wait_ge(w_used, U.at(u) + 1)
                        nc.scalar.activation(two(qh_sb[:, u]), proj_out(u), ACT.Copy).then_inc(proj_free[u], 1)
                        act.wait_ge(proj_free[u], U.half(u) + 2)
                        act.sem_inc(qh_ready, 1)
                        do_hi(act, U, u)
                    for u in range(2):
                        n = it * 2 + u
                        act.wait_ge(s_done, n + 1)
                        act.wait_ge(slot_free, n + 1)
                        flat = s_sb[:, u].rearrange("p a b -> p (a b)")
                        nc.scalar.activation(flat[:, 0:512], psum[:, 4, :], ACT.Copy)
                        nc.scalar.activation(flat[:, 512:T], psum[:, 5, 0:T - 512], ACT.Copy).then_inc(s_bank[0], 1)
                    act.wait_ge(ts_ready, it + 1)
                    nc.scalar.activation(te, te, ACT.Exp).then_inc(te_ready, 1)
                for s in range(2):
                    act.wait_ge(raw_ready[s], 16 * (UNITS + LEAD) // 2)
                for k, dst in enumerate((gate_t, i_t, j_t)):
                    act.wait_ge(tab_tr, k + 1)
                    nc.scalar.activation(dst[:, 0:512], psum[:, 2 * k, :], ACT.Copy)
                    nc.scalar.activation(dst[:, 512:T], psum[:, 2 * k + 1, 0:T - 512], ACT.Copy).then_inc(te_ready, 1)

            @block.gpsimd
            def _(pool):
                with pool.Fori(0, PH) as it:
                    pool.wait_ge(sf_ready, it + 1)
                    pair_sums(nc.gpsimd.tensor_tensor, cid, sf[:, 0], sf[:, 1]).then_inc(cid_ready, 1)

            @block.vector
            def _(dve):
                dve.sem_inc(s_bank[0], 1)
                dve.sem_inc(slot_free, 2)
                nc.vector.memset(pad, 0.0).then_inc(k_step, 1)
                dve.wait_ge(k_step, 1)
                with dve.Fori(0, PH) as it:
                    U = Unit(U_PQ, it, 2)
                    count = [0]

                    def step(ins):
                        count[0] += 1
                        ins.then_inc(k_step, 1)
                        dve.wait_ge(k_step, it * STEPS + (count[0] + 1))

                    def carry():
                        nc.vector.tensor_copy(pad[:, 0:1], pad[:, 1:2])

                    def best16(src, cut, val, idx):
                        for t in range(TT):
                            m = nc.vector.max(val[:, t, 0:KH], src[:, t])
                        step(m)
                        carry()
                        for t in range(TT):
                            nc.vector.max_index(idx[:, t, 0:KH], val[:, t, 0:KH], src[:, t])
                            m = nc.vector.match_replace(cut[:, t], val[:, t, 0:KH], src[:, t], -3.0e38)
                        step(m)
                        carry()
                        for t in range(TT):
                            m = nc.vector.max(val[:, t, KH:TOPK], cut[:, t])
                        step(m)
                        carry()
                        for t in range(TT):
                            m = nc.vector.max_index(idx[:, t, KH:TOPK], val[:, t, KH:TOPK], cut[:, t])
                        step(m)
                    for u in range(2):
                        do_lo(dve, U, u)
                    for u in range(2):
                        dve.wait_ge(s_bank[0], it * 2 + (u + 2))
                        carry()
                        best16(s_sb[:, u], s_cut, sv[:, u], si[:, u])
                        dve.sem_inc(slot_free, 1)
                        if u == 0:
                            step(nc.vector.tensor_scalar(sf[:, 0], si[:, 0], float(NKEYS), None, ALU.mult))
                        else:
                            nc.vector.tensor_copy(sf[:, 1], si[:, 1]).then_inc(sf_ready, 1)
                    step(pair_sums(nc.vector.tensor_tensor, cv, sv[:, 0], sv[:, 1]))
                    carry()
                    best16(cv, cv_cut, tv, tp)
                    nc.vector.tensor_copy(tpf, tp).then_inc(k_step, 1)
                    nc.vector.tensor_tensor(te, tv, tv[:, :, 0:1].broadcast_to([P, TT, TOPK]), ALU.subtract
                                            ).then_inc(ts_ready, 1)
                    count[0] += 1
                    dve.wait_ge(k_step, it * STEPS + (count[0] + 1))
                    dve.wait_ge(cid_ready, it + 1)
                    for t in range(TT):
                        step(nc.vector.tensor_tensor(onehot, iota[:, 0:CAND].rearrange("p (o c) -> p o c", o=1)
                                                     .broadcast_to([P, TOPK, CAND]),
                                                     tpf[:, t].rearrange("p (k o) -> p k o", o=1)
                                                     .broadcast_to([P, TOPK, CAND]), ALU.is_equal))
                        step(nc.vector.tensor_tensor(onehot, onehot, cid[:, t:t + 1].broadcast_to([P, TOPK, CAND]),
                                                     ALU.mult))
                        step(nc.vector.reduce_sum(eid[:, t, ds(it * TOPK, TOPK)], onehot, AX_X))
                    dve.wait_ge(te_ready, it + 1)
                    step(nc.vector.reduce_sum(tsum, te, AX_X))
                    step(nc.vector.reciprocal(tsum, tsum))
                    nc.vector.tensor_tensor(gate[:, :, ds(it * TOPK, TOPK)], te,
                                            tsum.rearrange("p (t o) -> p t o", o=1).broadcast_to([P, TT, TOPK]),
                                            ALU.mult).then_inc(head_done, 1)
                    assert count[0] == STEPS, count
                dve.wait_ge(head_done, PH)
                nc.vector.tensor_copy(ei, eid).then_inc(head_done, 1)
                dve.wait_ge(head_done, PH + 1)
                nc.vector.tensor_scalar(te_ji, ei, NKEYS - 1, None, ALU.bitwise_and)
                nc.vector.tensor_scalar(ei, ei, 7, None, ALU.logical_shift_right).then_inc(head_done, 1)
                dve.wait_ge(head_done, PH + 2)
                nc.vector.tensor_copy(eid, ei)
                nc.vector.tensor_copy(te_j, te_ji).then_inc(tab_done, 1)


        TB = 64
        NB = T // TB
        c_dram = nc.dram_tensor("gates_scratch", (NB, P, NKEYS * TB), F32, kind="Internal").ap()
        A = Arena()
        c_sb = A.take(2, NKEYS, TB)
        RING = 8
        oh_i, oh_j = A.take(RING, NKEYS), A.take(RING, NKEYS)
        onehot_ready, onehot_used, c_bank, c_stored = sem("onehot_ready"), sem("onehot_used"), sem("c_bank"), [sem("c_stored0"), sem("c_stored1")]
        Q4 = 4
        with nc.Block() as block:
            @block.vector
            def _(dve):
                dve.sem_inc(onehot_used, RING // Q4)
                with dve.Fori(0, T // RING) as it:
                    for q in range(RING // Q4):
                        dve.wait_ge(onehot_used, it * 2 + (q + 1))
                        for k in range(q * Q4, (q + 1) * Q4):
                            t = it * RING + k
                            nc.vector.tensor_scalar(oh_i[:, k], iota, i_t[:, ds(t, 1)], None, ALU.is_equal)
                            m = nc.vector.tensor_scalar(oh_j[:, k], iota, j_t[:, ds(t, 1)], gate_t[:, ds(t, 1)],
                                                        ALU.is_equal, ALU.mult)
                        m.then_inc(onehot_ready, 1)

            @block.tensor
            def _(pe):
                with pe.Fori(0, T // RING) as it:
                    for q in range(RING // Q4):
                        pe.wait_ge(onehot_ready, it * 2 + (q + 1))
                        pe.wait_ge(c_bank, it * 2 + (q + 1))
                        for k in range(Q4):
                            m = nc.tensor.matmul(psum[:, q, k * P:(k + 1) * P], oh_i[:, q * Q4 + k], oh_j[:, q * Q4 + k],
                                                 start=True, stop=True)
                        m.then_inc(onehot_used, 1)

            @block.scalar
            def _(act):
                act.sem_inc(c_bank, 2)
                for s in range(2):
                    act.sem_inc(c_stored[s], 16)
                with act.Fori(0, NB // 2) as blk:
                    for s in range(2):
                        act.wait_ge(c_stored[s], blk * 16 + 16)
                        with act.Fori(0, TB // RING) as it:
                            for q in range(RING // Q4):
                                n = blk * (2 * TB // Q4) + it * 2 + (s * (TB // Q4) + q)
                                act.wait_ge(onehot_used, n + 3)
                                dst = c_sb[:, s, :, ds(it * RING + q * Q4, Q4)].rearrange("p j t -> p t j")
                                nc.scalar.activation(dst, psum[:, q, :].rearrange("p (t j) -> p t j", t=Q4), ACT.Copy
                                                     ).then_inc(c_bank, 1)

            @block.sync
            def _(sp):
                with sp.Fori(0, NB // 2) as blk:
                    for s in range(2):
                        sp.wait_ge(c_bank, blk * (2 * TB // Q4) + ((s + 1) * (TB // Q4) + 2))
                        sp.dma_start(c_dram[ds(blk * 2 + s, 1)].rearrange("o p n -> p (o n)"),
                                     c_sb[:, s].rearrange("p j t -> p (j t)")).then_inc(c_stored[s], 16)
                for s in range(2):
                    sp.wait_ge(c_stored[s], 16 * (NB // 2 + 1))

        A = Arena()
        y_sb = A.take(TT, D)
        v_raw = A.take(2, D)
        c_lot = A.take(2, NB, TB)
        gl = A.take(2, T)
        b_flat = acts_b[:].rearrange("p a b c -> p (a b c)")
        v_split = b_flat[:, 0:8 * D].rearrange("p (b j h n) -> p b j h n", b=2, j=2, h=2)
        pieces = [b_flat[:, 8 * D + k * T:8 * D + (k + 1) * T] for k in range(5)] + [g_more[:, k * T:(k + 1) * T] for k in range(3)]
        g_split = [[[pieces[4 * b + 2 * j + h] for h in range(2)] for j in range(2)] for b in range(2)]
        LOTS, PAIRS = NKEYS, NKEYS // 2
        u_in, v_in, c_in = ([sem(n + str(s)) for s in range(2)] for n in ("u_in", "v_in", "c_in"))
        uh, ul, vh, vl = sem("uh"), sem("ul"), sem("vh"), sem("vl")
        act_done, gelu_done, g_mul, gh_done, gl_done = (sem(n) for n in ("act_done", "gelu_done", "g_mul", "gh_done", "gl_done"))
        y_done, y_free, y_zero = sem("y_done"), [sem("y_free%d" % k) for k in range(4)], sem("y_zero")
        YH = 6

        def u_lot(s):
            return w_split[:, s]

        with nc.Block() as block:
            @block.gpsimd
            def _(pool):
                nc.gpsimd.memset(y_sb, 0.0).then_inc(y_zero, 1)

            @block.sync
            def _(sp):
                def loads(j, s, wait):
                    if wait:
                        sp.wait_ge(ul, j - 1)
                    sp.dma_start(w_raw[:, s], u_t[ds(j, 1)].rearrange("o p (c k) -> p (o c) k", c=DC)).then_inc(u_in[s], 16)
                    if wait:
                        sp.wait_ge(g_mul, j - 1)
                    sp.dma_start(c_lot[:, s], c_dram[:, :, ds(j * TB, TB)].rearrange("b p t -> p b t")).then_inc(c_in[s], 16)
                    if wait:
                        sp.wait_ge(vl, j - 1)
                    sp.dma_start(v_raw[:, s], v_t[ds(j, 1)].rearrange("o p n -> p (o n)")).then_inc(v_in[s], 16)
                loads(0, 0, False)
                loads(1, 1, False)
                with sp.Fori(0, LOTS // 2 - 1) as it:
                    for s in range(2):
                        loads(it * 2 + (2 + s), s, True)

            @block.tensor
            def _(pe):
                def a_lot(j, s, first=False):
                    pe.wait_ge(ul, j + 1)
                    if not first:
                        pe.wait_ge(gelu_done, j - 1)
                    for t in range(2):
                        for d in range(DC):
                            for i, (wh, ah) in enumerate(((0, 0), (0, 1), (1, 0))):
                                m = nc.tensor.matmul(psum[:, 2 * s + t, 0:HALF], u_lot(s)[:, wh, d, :],
                                                     acts_a[:, ah, d, t * HALF:(t + 1) * HALF],
                                                     start=(d == 0 and i == 0), stop=(d == DC - 1 and i == 2))
                    m.then_inc(act_done, 1)

                def y_half(p, b, half):
                    if half == 0:
                        pe.wait_ge(gl_done, p * 2 + 2)
                        pe.wait_ge(vl, p * 2 + 2)
                    for n in range(half * YH, (half + 1) * YH):
                        t, c = n // 2, n % 2
                        pe.wait_ge(y_free[n % 4], p * 3 + (n // 4 + 1))
                        k = 0
                        for j in range(2):
                            for gh, vh_ in ((0, 0), (0, 1), (1, 0)):
                                m = nc.tensor.matmul(psum[:, 4 + n % 4, :], g_split[b][j][gh][:, t * P:(t + 1) * P],
                                                     v_split[:, b, j, vh_, c * 512:(c + 1) * 512],
                                                     start=(k == 0), stop=(k == 5))
                                k += 1
                        m.then_inc(y_done, 1)
                a_lot(0, 0, True)
                a_lot(1, 1, True)
                with pe.Fori(0, PAIRS // 2 - 1) as it:
                    for b in range(2):
                        p = it * 2 + b
                        for half in range(2):
                            a_lot(p * 2 + (2 + half), half)
                            y_half(p, b, half)
                p = PAIRS - 2
                for half in range(2):
                    a_lot(p * 2 + 2 + half, half)
                    y_half(p, 0, half)
                for half in range(2):
                    y_half(PAIRS - 1, 1, half)

            @block.scalar
            def _(act):
                def u_hi(j, s, h, first=False):
                    act.wait_ge(u_in[s], h * 16 + 16)
                    if not first:
                        act.wait_ge(act_done, j - 1)
                    nc.scalar.activation(u_lot(s)[:, 0], w_raw[:, s], ACT.Copy).then_inc(uh, 1)

                def v_hi(j, s, h, b, first=False):
                    act.wait_ge(v_in[s], h * 16 + 16)
                    if not first:
                        act.wait_ge(y_done, (h - 1) * 12)
                    nc.scalar.activation(v_split[:, b, s, 0], v_raw[:, s], ACT.Copy).then_inc(vh, 1)

                def gelu(j, s):
                    act.wait_ge(act_done, j + 1)
                    nc.scalar.activation(two(gl[:, s]), psum[:, 2 * s:2 * s + 2, 0:HALF], ACT.Gelu).then_inc(gelu_done, 1)

                def g_hi(j, s, b):
                    act.wait_ge(g_mul, j + 1)
                    nc.scalar.activation(g_split[b][s][0], gl[:, s], ACT.Copy).then_inc(gh_done, 1)
                for j in range(2):
                    u_hi(j, j, 0, True)
                for j in range(2):
                    v_hi(j, j, 0, 0, True)
                for j in range(2):
                    gelu(j, j)
                    u_hi(j + 2, j, 1)
                    g_hi(j, j, 0)
                for j in range(2):
                    v_hi(j + 2, j, 1, 1, True)

                def pair(p, b, last=False):
                    for s in range(2):
                        j = p * 2 + (2 + s)
                        gelu(j, s)
                        if not last:
                            u_hi(j + 2, s, p + 2)
                        g_hi(j, s, 1 - b)
                    if not last:
                        for s in range(2):
                            v_hi(p * 2 + (4 + s), s, p + 2, b)
                with act.Fori(0, PAIRS // 2 - 1) as it:
                    for b in range(2):
                        pair(it * 2 + b, b)
                pair(PAIRS - 2, 0, True)

            @block.vector
            def _(dve):
                def u_lo(j, s):
                    dve.wait_ge(uh, j + 1)
                    nc.vector.tensor_tensor(u_lot(s)[:, 1], w_raw[:, s], u_lot(s)[:, 0].bitcast(F32), ALU.subtract
                                            ).then_inc(ul, 1)

                def v_lo(j, s, b):
                    dve.wait_ge(vh, j + 1)
                    nc.vector.tensor_tensor(v_split[:, b, s, 1], v_raw[:, s], v_split[:, b, s, 0].bitcast(F32),
                                            ALU.subtract).then_inc(vl, 1)

                def times_gates(j, s, h):
                    dve.wait_ge(gelu_done, j + 1)
                    dve.wait_ge(c_in[s], h * 16 + 16)
                    nc.vector.tensor_tensor(gl[:, s], gl[:, s], c_lot[:, s].rearrange("p b t -> p (b t)"), ALU.mult
                                            ).then_inc(g_mul, 1)

                def g_lo(j, s, b):
                    dve.wait_ge(gh_done, j + 1)
                    nc.vector.tensor_tensor(g_split[b][s][1], gl[:, s], g_split[b][s][0].bitcast(F32), ALU.subtract
                                            ).then_inc(gl_done, 1)

                def adds(p, half):
                    for n in range(half * YH, (half + 1) * YH):
                        t, c = n // 2, n % 2
                        dve.wait_ge(y_done, p * 12 + (n + 1))
                        dve.wait_ge(y_free[n % 4], p * 3 + (n // 4 + 1))
                        y = y_sb[:, t, c * 512:(c + 1) * 512]
                        nc.vector.tensor_tensor(y, y, psum[:, 4 + n % 4, :], ALU.add).then_inc(y_free[n % 4], 1)
                for k in range(4):
                    dve.sem_inc(y_free[k], 1)
                dve.wait_ge(y_zero, 1)
                for j in range(2):
                    u_lo(j, j)
                for j in range(2):
                    v_lo(j, j, 0)
                for j in range(2):
                    u_lo(j + 2, j)
                    times_gates(j, j, 0)
                    g_lo(j, j, 0)
                for j in range(2):
                    v_lo(j + 2, j, 1)

                def pair(p, b, last=False):
                    for s in range(2):
                        j = p * 2 + (2 + s)
                        if not last:
                            u_lo(j + 2, s)
                        times_gates(j, s, p + 1)
                        g_lo(j, s, 1 - b)
                        adds(p, s)
                    if not last:
                        for s in range(2):
                            v_lo(p * 2 + (4 + s), s, b)
                with dve.Fori(0, PAIRS // 2 - 1) as it:
                    for b in range(2):
                        pair(it * 2 + b, b)
                pair(PAIRS - 2, 0, True)
                for half in range(2):
                    adds(PAIRS - 1, half)

        A = Arena()
        y_in = A.take(TT, D)
        x2 = A.take(DC, T)
        d_x2, yt_done, yt_free = sem("d_x2"), sem("yt_done"), sem("yt_free")
        with nc.Block() as block:
            @block.sync
            def _(sp):
                sp.dma_start(arena[:, TT * D:TT * D + DC * T], x1_dram).then_inc(d_x2, 16)

            @block.tensor
            def _(pe):
                for d in range(DC):
                    if d >= 2:
                        pe.wait_ge(yt_free, d - 1)
                    for t in range(TT):
                        b = 2 * (d % 2) + t // 4
                        m = nc.tensor.transpose(psum[:, b, t % 4 * P:t % 4 * P + P], y_in[:, t, d * P:(d + 1) * P], ident)
                    m.then_inc(yt_done, 1)

            @block.vector
            def _(dve):
                dve.wait_ge(d_x2, 16)
                for d in range(DC):
                    dve.wait_ge(yt_done, d + 1)
                    for g, (t0, t1) in enumerate(GROUPS):
                        x = x2[:, d, t0:t1]
                        m = nc.vector.scalar_tensor_tensor(out=x, in0=psum[:, 2 * (d % 2) + g, 0:t1 - t0],
                                                           scalar=modcol(GATE2, d, g), in1=x, op0=ALU.mult, op1=ALU.add)
                    m.then_inc(yt_free, 1)
        norm_phase("n3", x2, None, lambda d, g: vec[:, V_GF + d:V_GF + d + 1], None, None, work=A, store=out)


def _constants():
    c = np.zeros((P, C_N), np.float32)
    row, col = np.arange(P)[:, None], np.arange(P)[None, :]
    c[:, C_ID:C_ID + P] = row == col
    c[:, C_ONE:C_ONE + P] = 1.0
    c[:, C_IOTA:C_IOTA + P] = col
    c[:, C_SLOPE:C_SLOPE + HEADS] = np.exp2(-8.0 * np.arange(1, HEADS + 1) / HEADS)
    for l in range(LEVELS):
        m = (((row ^ col) >> l) == 1).astype(np.uint32)
        c[:, C_MASK + l * P:C_MASK + (l + 1) * P] = m.view(np.float32)
    d = np.abs(row - np.arange(3 * P)[None, :] + P)
    c[:, C_DIST:C_DIST + 3 * P] = np.where(d <= P, -d, -1e30)
    return c


def _columns(v):
    return np.reshape(v, (-1, P)).T


def _units(w):
    k, n = w.shape
    return w.reshape(DC, P, n // P, P).transpose(2, 1, 0, 3).reshape(n // P, P, D)


def arrays_of(i):
    i = {k: np.asarray(v) for k, v in i.items()}
    x = np.concatenate([i["x_prompt"][0], i["x_sample"][0]], 0)
    x_t = x.T.reshape(DC, P, T).transpose(1, 0, 2)
    c = np.stack([_columns(i["c_prompt"][0]), _columns(i["c_sample"][0])], -1).reshape(P, 16)
    vecs = np.concatenate(
        [_columns(i["b_mod"][0]), _columns(i["g_norm1"][0]), _columns(i["g_norm2"][0]), _columns(i["g_final"]),
         _columns(i["g_hnorm"][0]), _columns(i["p_lb_fwd"][0]), _columns(i["p_lb_fwd"][1]),
         _columns(i["p_lb_bwd"][0]), _columns(i["p_lb_bwd"][1]), c,
         np.broadcast_to(i["att_sink"][0][None, :], (P, HEADS))], 1)
    w = i["w_in"][0]
    qa, kv = _units(w[:, 0:D]), w[:, D:D + 512]
    n0 = D + 512
    qh, zf, zb, ih, gh, ga, gb = (_units(w[:, n0 + k * D:n0 + (k + 1) * D]) for k in range(7))
    order = []
    for g in range(KV_HEADS):
        pair = np.concatenate([kv[:, g * HD:(g + 1) * HD], kv[:, 256 + g * HD:256 + (g + 1) * HD]], 1)
        order += [_units(pair)[0], qa[2 * g], qa[2 * g + 1]]
    order += list(ga) + list(_units(i["w_o_att"][0]))
    for h in range(H_HEADS):
        order += [zf[h], zb[h], qh[h], gh[h], ih[h]]
    order += list(gb) + list(_units(i["w_o_hgrn"][0])) + list(_units(i["w_out"][0])) + list(_units(i["w_pq"][0]))
    order += [order[k] for k in range(LEAD)]
    keys_t = i["peer_keys"][0].reshape(2 * PH, NKEYS, P).transpose(2, 0, 1).reshape(P, 2 * PH * NKEYS)
    u_t = i["peer_u"][0].reshape(NKEYS, NKEYS, DC, P).transpose(1, 3, 2, 0).reshape(NKEYS, P, D)
    v_t = i["peer_v"][0].reshape(NKEYS, NKEYS, D).transpose(1, 0, 2)
    return {"x_t": x_t.reshape(P, DC * T), "vecs": vecs, "consts": _constants(), "w_mod": _units(i["w_mod"][0]),
            "w_str": np.stack(order), "keys_t": keys_t, "u_t": u_t, "v_t": v_t}


def kernel(**inputs):
    import concourse.bacc as _bacc
    from concourse.bass_utils import run_bass_kernel_spmd as _run

    nc = _bacc.Bacc("TRN2", target_bir_lowering=False, num_devices=1)
    arrays = {k: np.ascontiguousarray(v) for k, v in arrays_of(inputs).items()}
    args = [nc.dram_tensor(k, v.shape, F32, kind="ExternalInput").ap() for k, v in arrays.items()]
    out = nc.dram_tensor("y_t", (P, DC * T), F32, kind="ExternalOutput").ap()
    encoder_kernel(nc, *args, out)
    y = _run(nc, [arrays], core_ids=[0]).results[0]["y_t"]
    y = np.asarray(y).reshape(P, DC, T).transpose(2, 1, 0).reshape(T, D)
    return y[None, 0:T_PROMPT], y[None, T_PROMPT:T]
```

```python
from contextlib import ExitStack

import concourse.bass as bass
import numpy as np
from concourse import mybir

F32 = mybir.dt.float32
F32R = mybir.dt.float32r
U32 = mybir.dt.uint32
ALU = mybir.AluOpType
ACT = mybir.ActivationFunctionType
AX_X = mybir.AxisListType.X
ds = bass.ds

P = 128
D = 1024
DC = D // P
T_PROMPT, T_SAMPLE = 512, 256
T = T_PROMPT + T_SAMPLE
TT = T // P
HALF = T // 2
GROUPS = ((0, T_PROMPT), (T_PROMPT, T))
EPS = 1e-6
KV_HEADS, Q_PER_KV, HD = 4, 4, 64
HEADS = KV_HEADS * Q_PER_KV
H_HEADS = 8
LEVELS = 7
PH, NKEYS, TOPK = 8, 128, 16
EXPERTS = NKEYS * NKEYS
ROW_LEN = [TOPK // (a + 1) for a in range(TOPK)]
CAND = sum(ROW_LEN)

N_ATT = KV_HEADS * 3
N_GATT = 2 * DC
N_HG = H_HEADS * 5
N_GHG = 2 * DC
N_OUT = DC
N_PQ = 2 * PH
U_ATT = 0
U_GATT = U_ATT + N_ATT
U_HG = U_GATT + N_GATT
U_GHG = U_HG + N_HG
U_OUT = U_GHG + N_GHG
U_PQ = U_OUT + N_OUT
UNITS = U_PQ + N_PQ
LEAD = 4
EARLY = EXPERTS // P // 2
EARLY_PQ = 5
EARLY_LEAD = 2
N_MOD = 6 * DC
MOD_LOT = 4

V_BMOD, V_G1, V_G2, V_GF, V_GH = 0, 48, 56, 64, 72
V_LB = 80
V_C = 112
V_SINK = 128
V_N = V_SINK + HEADS
C_ID, C_ONE, C_IOTA, C_SLOPE, C_MASK = 0, 128, 256, 384, 400
C_DIST = C_MASK + LEVELS * P
C_N = C_DIST + 3 * P
C_KEEP = C_MASK

BLOCKS = []
for g0, g1 in ((0, T_PROMPT // P), (T_PROMPT // P, TT)):
    for q in range(g0, g1):
        k0, k1 = max(g0, q - 1), min(g1 - 1, q + 1)
        BLOCKS.append((q, k0, k1 - k0 + 1, (k0 - q + 1) * P))
B_OFF = [P * sum(b[2] for b in BLOCKS[:i]) for i in range(TT + 1)]
N_KT = sum(b[2] for b in BLOCKS)


def encoder_kernel(nc, x_t, vecs, consts, w_mod, w_str, keys_t, u_late, u_early, v_t, out):
    with ExitStack() as ctx:
        def sb(name, shape, dt=F32):
            return ctx.enter_context(nc.sbuf_tensor(name, shape, dt))

        def sem(name):
            return ctx.enter_context(nc.semaphore(name))

        acts_a = sb("acts_a", [P, 2, DC, T], F32R)
        w_split = sb("w_split", [P, 2, 2, DC, P], F32R)
        w_raw = sb("w_raw", [P, 2, DC, P])
        cst = sb("cst", [P, C_KEEP])
        vec = sb("vec", [P, V_N])
        mod = sb("mod", [P, 6 * DC, 2])
        lb = sb("lb", [P, 2, 2, H_HEADS])
        ARENA = 19200
        arena = sb("arena", [P, ARENA])
        psum = ctx.enter_context(nc.psum_tensor("psum", [P, 8, 512], F32))

        class Room:
            def __init__(self):
                self.stack = ExitStack()

            def take(self, *tensors):
                self.stack.close()
                return [self.stack.enter_context(nc.sbuf_tensor(*t))[:] for t in tensors]
        room = Room()
        m_dram = nc.dram_tensor("m_scratch", (DC, P, T), F32, kind="Internal").ap()
        x1_dram = nc.dram_tensor("x1_scratch", (P, DC * T), F32, kind="Internal").ap()

        class Arena:
            def __init__(self):
                self.at = 0

            def take(self, *shape):
                n = int(np.prod(shape))
                ap = arena[:, self.at:self.at + n]
                self.at += n
                assert self.at <= ARENA, self.at
                if len(shape) == 2:
                    ap = ap.rearrange("p (a b) -> p a b", a=shape[0])
                elif len(shape) == 3:
                    ap = ap.rearrange("p (a b c) -> p a b c", a=shape[0], b=shape[1])
                return ap

        ident, ones = cst[:, C_ID:C_ID + P], cst[:, C_ONE:C_ONE + P]
        iota = cst[:, C_IOTA:C_IOTA + P]

        def modcol(which, d, g):
            return mod[:, which * DC + d, g:g + 1]
        SHIFT1, SCALE1, GATE1, SHIFT2, SCALE2, GATE2 = range(6)

        raw_ready = [sem("raw_ready0"), sem("raw_ready1")]
        hi_ready, lo_ready = sem("hi_ready"), sem("lo_ready")
        w_used = sem("w_used")
        proj_free = [sem("proj_free0"), sem("proj_free1")]

        def load_unit(sp, n, s):
            sp.dma_start(w_raw[:, s], w_str[ds(n, 1)].rearrange("o p (c k) -> p (o c) k", c=DC)
                         ).then_inc(raw_ready[s], 16)

        def load_ahead(sp, n, u):
            sp.wait_ge(lo_ready, n + 3)
            load_unit(sp, n + LEAD, u % 2)

        def split_lo(dve, n, u):
            dve.wait_ge(hi_ready, n + 3)
            nc.vector.tensor_tensor(w_split[:, u % 2, 1], w_raw[:, u % 2],
                                    w_split[:, u % 2, 0].bitcast(F32), ALU.subtract).then_inc(lo_ready, 1)

        class Unit:
            def __init__(self, base, it=None, per=0):
                assert base % 2 == 0 and per % 2 == 0
                self.base, self.it, self.per = base, it, per

            def at(self, u):
                return self.base + u if self.it is None else self.it * self.per + (self.base + u)

            def half(self, u):
                h = (self.base + u) // 2
                return h if self.it is None else self.it * (self.per // 2) + h

        def do_load(sp, U, u):
            load_ahead(sp, U.at(u), u)

        def do_hi(act, U, u):
            act.wait_ge(raw_ready[u % 2], U.half(u) * 16 + 32)
            act.wait_ge(w_used, U.at(u) + 1)
            nc.scalar.activation(w_split[:, u % 2, 0], w_raw[:, u % 2], ACT.Copy).then_inc(hi_ready, 1)

        def do_lo(dve, U, u):
            split_lo(dve, U.at(u), u)

        def project(pe, U, u, a, tokens_out=False, halves=(0, 1)):
            s = u % 2
            if 0 in halves:
                pe.wait_ge(lo_ready, U.at(u) + 1)
                pe.wait_ge(proj_free[s], U.half(u) + 1)
            passes = ((0, 0), (0, 1), (1, 0))
            n_half = TT // 2 if tokens_out else 1
            for t in range(halves[0] * n_half, (halves[-1] + 1) * n_half):
                for d in range(DC):
                    for i, (wh, ah) in enumerate(passes):
                        if tokens_out:
                            o = psum[:, 2 * s + t // 3, t % 3 * P:t % 3 * P + P]
                            l, r = a[:, ah, d, t * P:(t + 1) * P], w_split[:, s, wh, d, :]
                        else:
                            o = psum[:, 2 * s + t, 0:HALF]
                            l, r = w_split[:, s, wh, d, :], a[:, ah, d, t * HALF:(t + 1) * HALF]
                        last = nc.tensor.matmul(o, l, r, start=(d == 0 and i == 0),
                                                stop=(d == DC - 1 and i == 2))
            if 1 in halves:
                last.then_inc(w_used, 1)

        def proj_out(u, parts=slice(0, P)):
            return psum[parts, 2 * (u % 2):2 * (u % 2) + 2, 0:HALF]

        def two(ap):
            return ap.rearrange("p (a b) -> p a b", a=2)

        class Norm:
            def __init__(self, name, x, scale_of, shift_of, dest, work):
                self.x, self.scale_of, self.shift_of, self.dest = x, scale_of, shift_of, dest
                self.sq, self.r, self.hx, self.hf = work
                (self.n_sq, self.n_ps, self.n_r, self.n_root, self.n_hx, self.n_hf, self.n_hi, self.n_lo) = (
                    sem(name + k) for k in ("_sq", "_ps", "_r", "_root", "_hx", "_hf", "_hi", "_lo"))

            def stats_act(self, act):
                for d in range(DC):
                    if d >= 2:
                        act.wait_ge(self.n_ps, d - 1)
                    nc.scalar.activation(self.sq[:, d % 2], self.x[:, d], ACT.Square).then_inc(self.n_sq, 1)
                act.wait_ge(self.n_r, 1)
                nc.scalar.activation(self.r, self.r, ACT.Sqrt).then_inc(self.n_root, 1)

            def stats_pe(self, pe):
                for d in range(DC):
                    pe.wait_ge(self.n_sq, d + 1)
                    for t in range(2):
                        m = nc.tensor.matmul(psum[:, 4 + t, 0:HALF], ones, self.sq[:, d % 2, t * HALF:(t + 1) * HALF],
                                             start=(d == 0), stop=(d == DC - 1))
                    m.then_inc(self.n_ps, 1)

            def stats_dve(self, dve):
                dve.wait_ge(self.n_ps, DC)
                nc.vector.tensor_scalar(two(self.r), psum[:, 4:6, 0:HALF], 1.0 / D, EPS, ALU.mult, ALU.add
                                        ).then_inc(self.n_r, 1)
                dve.wait_ge(self.n_root, 1)
                nc.vector.reciprocal(self.r, self.r).then_inc(self.n_r, 1)

            def apply_act(self, act):
                for d in range(DC):
                    act.wait_ge(self.n_hf, 2 * d + 2)
                    nc.scalar.activation(self.dest[:, 0, d], self.hf[:, d % 2], ACT.Copy).then_inc(self.n_hi, 1)

            def apply_dve(self, dve):
                hf, hx, dest, n_hx, n_hf = self.hf, self.hx, self.dest, self.n_hx, self.n_hf

                def rest(d):
                    dve.wait_ge(self.n_hi, d + 1)
                    nc.vector.tensor_tensor(dest[:, 1, d], hf[:, d % 2], dest[:, 0, d].bitcast(F32), ALU.subtract
                                            ).then_inc(self.n_lo, 1)
                dve.wait_ge(self.n_r, 2)
                for d in range(DC):
                    if d >= 2:
                        dve.wait_ge(n_hf, 2 * d - 2)
                    nc.vector.tensor_tensor(hx[:, d % 2], self.x[:, d], self.r, ALU.mult).then_inc(n_hx, 1)
                    if dest is not None and d >= 2:
                        rest(d - 2)
                        dve.wait_ge(self.n_lo, d - 1)
                    dve.wait_ge(n_hx, d + 1)
                    for g, (t0, t1) in enumerate(GROUPS):
                        o = self.x[:, d, t0:t1] if dest is None else hf[:, d % 2, t0:t1]
                        if self.shift_of is None:
                            m = nc.vector.tensor_scalar(o, hx[:, d % 2, t0:t1], self.scale_of(d, g), None, ALU.mult)
                        else:
                            m = nc.vector.tensor_scalar(o, hx[:, d % 2, t0:t1], self.scale_of(d, g), self.shift_of(d, g),
                                                        ALU.mult, ALU.add)
                        m.then_inc(n_hf, 1)
                if dest is not None:
                    for d in range(DC - 2, DC):
                        rest(d)

        def norm_work(A):
            return A.take(2, T), A.take(T), A.take(2, T), A.take(2, T)

        A = Arena()
        MOD_SLOTS = 4
        wm = A.take(MOD_SLOTS * MOD_LOT, D).rearrange("p (s u) k -> p s u k", s=MOD_SLOTS)
        cs, cg = A.take(16), A.take(16)
        lbt = A.take(4, 8)
        x_sb, spare = room.take(("x_sb", [P, DC, T], F32), ("n1_work", [P, 7, T], F32))
        n1 = Norm("n1", x_sb, lambda d, g: modcol(SCALE1, d, g), lambda d, g: modcol(SHIFT1, d, g), acts_a,
                  (spare[:, 0:2], spare[:, 2], spare[:, 3:5], spare[:, 5:7]))
        LOTS_1, LOTS_ALL = 2 * DC // MOD_LOT, N_MOD // MOD_LOT
        d_vec, d_x, d_cst, d_wm = sem("d_vec"), sem("d_x"), sem("d_cst"), [sem("d_wm%d" % k) for k in range(MOD_SLOTS)]
        mod_a, mod_v, mod_used, mod_done = sem("mod_a"), sem("mod_v"), sem("mod_used"), sem("mod_done")

        def load_mod(eng, lot):
            if lot >= MOD_SLOTS:
                eng.wait_ge(mod_used, lot - MOD_SLOTS + 1)
            eng.dma_start(wm[:, lot % MOD_SLOTS], w_mod[lot * MOD_LOT:(lot + 1) * MOD_LOT]
                          .rearrange("u p k -> p u k")).then_inc(d_wm[lot % MOD_SLOTS], 16)

        def mod_products(pe, lots):
            for lot in lots:
                pe.wait_ge(d_wm[lot % MOD_SLOTS], 16 * (lot // MOD_SLOTS + 1))
                for k in range(MOD_LOT):
                    n = lot * MOD_LOT + k
                    for d in range(DC):
                        last = nc.tensor.matmul(psum[:, 0, 2 * n:2 * n + 2], wm[:, lot % MOD_SLOTS, k, d * P:(d + 1) * P],
                                                cs[:, 2 * d:2 * d + 2], start=(d == 0), stop=(d == DC - 1))
                last.then_inc(mod_used, 1)

        def mod_out(dve, lots, scale_which, v, count):
            dve.wait_ge(mod_used, lots[-1] + 1)
            n0, n1_ = lots[0] * MOD_LOT, (lots[-1] + 1) * MOD_LOT
            for g in range(2):
                m = nc.vector.tensor_tensor(mod[:, n0:n1_, g],
                                            psum[:, 0, 0:2 * N_MOD].rearrange("p (n g) -> p n g", g=2)[:, n0:n1_, g],
                                            vec[:, V_BMOD + n0:V_BMOD + n1_], ALU.add)
            m.then_inc(mod_v, 1)
            dve.wait_ge(mod_v, count + 1)
            for g in range(2):
                col = mod[:, scale_which * DC:(scale_which + 1) * DC, g]
                nc.vector.scalar_tensor_tensor(out=col, in0=col, scalar=1.0, in1=vec[:, v:v + DC],
                                               op0=ALU.add, op1=ALU.mult).then_inc(mod_done, 1)

        with nc.Block() as block:
            @block.sync
            def _(sp):
                sp.dma_start(vec[:], vecs).then_inc(d_vec, 16)
                sp.dma_start(cst[:], consts[:, 0:C_KEEP]).then_inc(d_cst, 16)
                for lot in range(0, MOD_SLOTS, 2):
                    load_mod(sp, lot)
                for n in range(2):
                    load_unit(sp, n, n)
                for lot in range(MOD_SLOTS, LOTS_1 + MOD_SLOTS, 2):
                    load_mod(sp, lot)

            @block.scalar
            def _(act):
                act.dma_start(x_sb, x_t.rearrange("p (a b) -> p a b", a=DC)).then_inc(d_x, 16)
                for lot in range(1, MOD_SLOTS, 2):
                    load_mod(act, lot)
                act.wait_ge(d_vec, 16)
                nc.scalar.activation(cg, vec[:, V_C:V_C + 16], ACT.Sigmoid).then_inc(mod_a, 1)
                act.wait_ge(mod_v, 2)
                nc.scalar.activation(lbt, lbt, ACT.Exp).then_inc(mod_a, 1)
                act.wait_ge(d_x, 16)
                n1.stats_act(act)
                for lot in range(MOD_SLOTS + 1, LOTS_1 + MOD_SLOTS, 2):
                    load_mod(act, lot)

            @block.vector
            def _(dve):
                p_lb = vec[:, V_LB:V_LB + 32].rearrange("p (d l h) -> p d l h", d=2, l=2)
                e_lb = lbt.rearrange("p (d l) h -> p d l h", d=2)
                dve.wait_ge(d_vec, 16)
                nc.vector.tensor_tensor(lb[:, 0], p_lb[:, :, 0], p_lb[:, :, 1], ALU.max).then_inc(mod_v, 1)
                dve.wait_ge(mod_v, 1)
                for l in range(2):
                    m = nc.vector.tensor_tensor(e_lb[:, :, l], p_lb[:, :, l], lb[:, 0], ALU.subtract)
                m.then_inc(mod_v, 1)
                dve.wait_ge(mod_a, 1)
                nc.vector.tensor_tensor(cs, cg, vec[:, V_C:V_C + 16], ALU.mult).then_inc(mod_v, 1)
                dve.wait_ge(mod_a, 2)
                nc.vector.tensor_tensor(lb[:, 1], e_lb[:, :, 0], e_lb[:, :, 1], ALU.add).then_inc(mod_v, 1)
                dve.wait_ge(mod_v, 4)
                nc.vector.reciprocal(lb[:, 1], lb[:, 1]).then_inc(mod_v, 1)
                dve.wait_ge(mod_v, 5)
                nc.vector.tensor_tensor(lb[:, 0], e_lb[:, :, 0], lb[:, 1], ALU.mult).then_inc(mod_v, 1)
                dve.wait_ge(mod_v, 6)
                nc.vector.tensor_scalar(lb[:, 1], lb[:, 0], -1.0, 1.0, ALU.mult, ALU.add).then_inc(mod_v, 1)
                n1.stats_dve(dve)
                mod_out(dve, range(LOTS_1), SCALE1, V_G1, 7)

            @block.tensor
            def _(pe):
                pe.wait_ge(mod_v, 3)
                pe.wait_ge(d_cst, 16)
                n1.stats_pe(pe)
                mod_products(pe, range(LOTS_1))

        with nc.Block() as block:
            @block.sync
            def _(sp):
                for lot in range(LOTS_1 + MOD_SLOTS, LOTS_ALL):
                    load_mod(sp, lot)
                for n in range(2, 4):
                    sp.wait_ge(lo_ready, n - 1)
                    load_unit(sp, n, n % 2)

            @block.tensor
            def _(pe):
                mod_products(pe, range(LOTS_1, LOTS_ALL))

            @block.scalar
            def _(act):
                for s in range(2):
                    act.wait_ge(raw_ready[s], 16)
                    nc.scalar.activation(w_split[:, s, 0], w_raw[:, s], ACT.Copy).then_inc(hi_ready, 1)
                n1.apply_act(act)

            @block.vector
            def _(dve):
                for s in range(2):
                    dve.wait_ge(hi_ready, s + 1)
                    nc.vector.tensor_tensor(w_split[:, s, 1], w_raw[:, s], w_split[:, s, 0].bitcast(F32),
                                            ALU.subtract).then_inc(lo_ready, 1)
                for s in range(2):
                    dve.sem_inc(proj_free[s], 1)
                dve.wait_ge(mod_done, 2)
                n1.apply_dve(dve)
                mod_out(dve, range(LOTS_1, LOTS_ALL), SCALE2, V_G2, 8)


        acts_b, hg_more = room.take(("acts_b", [P, 2, DC, T], F32R),
                                    ("hg_more", [P, 3, T], F32))
        A = Arena()
        dist = A.take(3 * P)
        kT, vT, qT = A.take(2, T), A.take(T), A.take(2, T)
        vN = A.take(2, TT, HD)
        sc = A.take(2, 2, N_KT * P)
        pT = A.take(2, N_KT, P)
        st = A.take(4, 6 * TT)
        d_dist = sem("d_dist")
        kv_ready, q_ready, v_ready = sem("kv_ready"), sem("q_ready"), sem("v_ready")
        score_ready, work_free = sem("score_ready"), [sem("work_free0"), sem("work_free1")]
        max_done, nmax_ready, sinkd_ready, exp_ready = sem("max_done"), sem("nmax_ready"), sem("sinkd_ready"), sem("exp_ready")
        den_step, prob_ready = sem("den_step"), sem("prob_ready")
        tr_ready, tr_taken, pv_ready, pv_hi = sem("tr_ready"), sem("tr_taken"), sem("pv_ready"), sem("pv_hi")
        TRIPS = KV_HEADS // 2
        PAIR_UNIT = (1, 2, 4, 5)
        SEQ = ["P0", "P1", "V0", "S0", "P2", "S1", "F0", "P3", "F1", "T0", "V1", "P4", "S2", "T1", "P5", "S3",
               "F2", "F3", "T2", "T3"]
        W_PAIR, W_TRIP = 2 * TT + 4, 4 * (2 * TT + 4)
        TR_GROUPS = [(a, min(a + 4, N_KT)) for a in range(0, N_KT, 4)]
        TR_TRIP = 2 + 4 * 2 * len(TR_GROUPS)
        PV_PARTS = ((0, T_PROMPT), (T_PROMPT, T))

        def walk(it):
            w = t = 0
            for step in SEQ:
                kind, k = step[0], int(step[1:])
                yield kind, k, w, t
                w += {"S": 2 * TT, "T": 4}.get(kind, 0)
                t += {"V": 1, "T": 2 * len(TR_GROUPS)}.get(kind, 0)
            assert w == W_TRIP and t == TR_TRIP

        def stat(p, e, k, n=TT):
            return st[:, (p % 2) * 2 + e, k * TT:k * TT + n]

        with nc.Block() as block:
            @block.sync
            def _(sp):
                sp.dma_start(dist, consts[:, C_DIST:C_DIST + 3 * P]).then_inc(d_dist, 16)
                with sp.Fori(0, TRIPS) as it:
                    U = Unit(U_ATT, it, 6)
                    for u in range(6):
                        do_load(sp, U, u)

            @block.tensor
            def _(pe):
                with pe.Fori(0, TRIPS) as it:
                    U = Unit(U_ATT, it, 6)
                    for kind, k, w, t in walk(it):
                        if kind == "P":
                            project(pe, U, k, acts_a)
                        elif kind == "V":
                            pe.wait_ge(kv_ready, it * 2 + (k + 1))
                            pe.wait_ge(tr_taken, it * TR_TRIP + (t + 1))
                            for i in range(TT):
                                m = nc.tensor.matmul(psum[:, 6 + t % 2, i * HD:(i + 1) * HD], vT[:, i * P:(i + 1) * P],
                                                     ident[:, HD:P], start=True, stop=True)
                            m.then_inc(tr_ready, 1)
                        elif kind == "S":
                            kv = k // 2
                            pe.wait_ge(kv_ready, it * 2 + (kv + 1))
                            pe.wait_ge(q_ready, it * 4 + (k + 1))
                            for e in range(2):
                                for i, (q, k0, nk, _) in enumerate(BLOCKS):
                                    wi = w + e * TT + i
                                    pe.wait_ge(work_free[wi % 2], it * (W_TRIP // 2) + (wi // 2 + 1))
                                    hd = slice(e * HD, (e + 1) * HD)
                                    nc.tensor.matmul(psum[:, 4 + wi % 2, 0:nk * P], qT[hd, k % 2, q * P:(q + 1) * P],
                                                     kT[hd, kv, k0 * P:(k0 + nk) * P], start=True, stop=True
                                                     ).then_inc(score_ready, 1)
                        elif kind == "T":
                            kv = k // 2
                            pe.wait_ge(v_ready, it * 2 + (kv + 1))
                            for e in range(2):
                                pe.wait_ge(prob_ready, it * 8 + (2 * k + e + 1))
                                for j, (a, b) in enumerate(TR_GROUPS):
                                    ti = t + e * len(TR_GROUPS) + j
                                    pe.wait_ge(tr_taken, it * TR_TRIP + (ti + 1))
                                    for c in range(a, b):
                                        m = nc.tensor.transpose(psum[:, 6 + ti % 2, (c - a) * P:(c - a + 1) * P],
                                                                sc[:, k % 2, e, c * P:(c + 1) * P], ident)
                                    m.then_inc(tr_ready, 1)
                            for e in range(2):
                                pe.wait_ge(tr_taken, it * TR_TRIP + (t + (e + 1) * len(TR_GROUPS) + 2))
                                for g, (t0, t1) in enumerate(PV_PARTS):
                                    wi = w + 2 * e + g
                                    pe.wait_ge(work_free[wi % 2], it * (W_TRIP // 2) + (wi // 2 + 1))
                                    for i, (q, k0, nk, _) in enumerate(BLOCKS):
                                        if not t0 <= q * P < t1:
                                            continue
                                        for j in range(nk):
                                            m = nc.tensor.matmul(
                                                psum[e * HD:(e + 1) * HD, 4 + wi % 2, q * P - t0:(q + 1) * P - t0],
                                                vN[:, kv, k0 + j, :], pT[:, e, B_OFF[i] // P + j, :],
                                                start=(j == 0), stop=(j == nk - 1))
                                    m.then_inc(pv_ready, 1)

            @block.scalar
            def _(act):
                act.sem_inc(tr_taken, 2)
                with act.Fori(0, TRIPS) as it:
                    U = Unit(U_ATT, it, 6)
                    for kind, k, w, t in walk(it):
                        if kind == "P":
                            act.wait_ge(w_used, U.at(k) + 1)
                            if k in (0, 3):
                                kv = k // 3
                                nc.scalar.activation(two(kT[0:HD, kv]), proj_out(k, slice(0, HD)), ACT.Copy)
                                nc.scalar.activation(two(kT[HD:P, kv]), proj_out(k, slice(0, HD)), ACT.Copy)
                                nc.scalar.activation(two(vT), proj_out(k), ACT.Copy
                                                     ).then_inc(proj_free[k % 2], 1)
                                act.wait_ge(proj_free[k % 2], U.half(k) + 2)
                                act.sem_inc(kv_ready, 1)
                            else:
                                p = PAIR_UNIT.index(k)
                                nc.scalar.activation(two(qT[:, p % 2]), proj_out(k), ACT.Copy, scale=HD ** -0.5
                                                     ).then_inc(proj_free[k % 2], 1)
                                act.wait_ge(proj_free[k % 2], U.half(k) + 2)
                                act.sem_inc(q_ready, 1)
                            do_hi(act, U, k)
                        elif kind == "V":
                            act.wait_ge(tr_ready, it * TR_TRIP + (t + 1))
                            nc.scalar.activation(vN[:, k].rearrange("p a b -> p (a b)"), psum[:, 6 + t % 2, 0:TT * HD],
                                                 ACT.Copy).then_inc(tr_taken, 1)
                            act.wait_ge(tr_taken, it * TR_TRIP + (t + 3))
                            act.sem_inc(v_ready, 1)
                        elif kind == "S":
                            for e in range(2):
                                act.wait_ge(sinkd_ready, it * 8 + (2 * k + e + 1))
                                for i, (q, k0, nk, _) in enumerate(BLOCKS):
                                    s = sc[:, k % 2, e, B_OFF[i]:B_OFF[i + 1]]
                                    nc.scalar.activation(s, s, ACT.Exp, bias=stat(k, e, 1)[:, i:i + 1],
                                                         accum_out=stat(k, e, 3)[:, i:i + 1])
                                nc.scalar.activation(stat(k, e, 4), stat(k, e, 2), ACT.Exp).then_inc(exp_ready, 1)
                        elif kind == "T":
                            for e in range(2):
                                for j, (a, b) in enumerate(TR_GROUPS):
                                    ti = t + e * len(TR_GROUPS) + j
                                    act.wait_ge(tr_ready, it * TR_TRIP + (ti + 1))
                                    nc.scalar.activation(pT[:, e, a:b].rearrange("p a b -> p (a b)"),
                                                         psum[:, 6 + ti % 2, 0:(b - a) * P], ACT.Copy).then_inc(tr_taken, 1)
                            for e in range(2):
                                for g, (t0, t1) in enumerate(PV_PARTS):
                                    wi = w + 2 * e + g
                                    act.wait_ge(pv_ready, it * 16 + (4 * k + 2 * e + g + 1))
                                    dst = acts_b[e * HD:(e + 1) * HD, 0, ds(it * 4 + k, 1), t0:t1]
                                    nc.scalar.activation(dst.rearrange("p o n -> p (o n)"),
                                                         psum[e * HD:(e + 1) * HD, 4 + wi % 2, 0:t1 - t0], ACT.Copy
                                                         ).then_inc(pv_hi, 1)

            @block.vector
            def _(dve):
                for b in range(2):
                    dve.sem_inc(work_free[b], 1)
                dve.wait_ge(d_dist, 16)
                with dve.Fori(0, TRIPS) as it:
                    U = Unit(U_ATT, it, 6)
                    steps = 0
                    for kind, k, w, t in walk(it):
                        if kind == "P":
                            do_lo(dve, U, k)
                        elif kind == "S":
                            for e in range(2):
                                head = it * 8 + (2 * k + e)
                                for i, (q, k0, nk, wc) in enumerate(BLOCKS):
                                    wi = w + e * TT + i
                                    dve.wait_ge(score_ready, it * (8 * TT) + ((2 * k + e) * TT + i + 1))
                                    nc.vector.scalar_tensor_tensor(
                                        out=sc[:, k % 2, e, B_OFF[i]:B_OFF[i + 1]], in0=dist[:, wc:wc + nk * P],
                                        scalar=cst[:, ds(head + C_SLOPE, 1)], in1=psum[:, 4 + wi % 2, 0:nk * P],
                                        op0=ALU.mult, op1=ALU.add).then_inc(work_free[wi % 2], 1)
                                for b in range(2):
                                    dve.wait_ge(work_free[b], it * (W_TRIP // 2) + ((w + e * TT + TT) // 2 + 1))
                                for i in range(TT):
                                    m = nc.vector.reduce_max(stat(k, e, 0)[:, i:i + 1],
                                                             sc[:, k % 2, e, B_OFF[i]:B_OFF[i + 1]], AX_X)
                                m.then_inc(max_done, 1)
                                sink = vec[:, ds(head + V_SINK, 1)]
                                dve.wait_ge(max_done, head + 1)
                                nc.vector.tensor_scalar(stat(k, e, 1), stat(k, e, 0), sink, -1.0, ALU.max, ALU.mult
                                                        ).then_inc(nmax_ready, 1)
                                dve.wait_ge(nmax_ready, head + 1)
                                nc.vector.tensor_scalar(stat(k, e, 2), stat(k, e, 1), sink, None, ALU.add
                                                        ).then_inc(sinkd_ready, 1)
                        elif kind == "F":
                            for e in range(2):
                                dve.wait_ge(exp_ready, it * 8 + (2 * k + e + 1))
                                nc.vector.tensor_tensor(stat(k, e, 5), stat(k, e, 3), stat(k, e, 4), ALU.add
                                                        ).then_inc(den_step, 1)
                                dve.wait_ge(den_step, it * 16 + (steps + 1))
                                nc.vector.reciprocal(stat(k, e, 5), stat(k, e, 5)).then_inc(den_step, 1)
                                dve.wait_ge(den_step, it * 16 + (steps + 2))
                                steps += 2
                                for i in range(TT):
                                    s = sc[:, k % 2, e, B_OFF[i]:B_OFF[i + 1]]
                                    m = nc.vector.tensor_scalar(s, s, stat(k, e, 5)[:, i:i + 1], None, ALU.mult)
                                m.then_inc(prob_ready, 1)
                        elif kind == "T":
                            for e in range(2):
                                for g, (t0, t1) in enumerate(PV_PARTS):
                                    wi = w + 2 * e + g
                                    dve.wait_ge(pv_hi, it * 16 + (4 * k + 2 * e + g + 1))
                                    hd = slice(e * HD, (e + 1) * HD)
                                    hi = acts_b[hd, 0, ds(it * 4 + k, 1), t0:t1].rearrange("p o n -> p (o n)")
                                    lo = acts_b[hd, 1, ds(it * 4 + k, 1), t0:t1].rearrange("p o n -> p (o n)")
                                    nc.vector.tensor_tensor(lo, psum[hd, 4 + wi % 2, 0:t1 - t0], hi.bitcast(F32),
                                                            ALU.subtract).then_inc(work_free[wi % 2], 1)

        def gate_phase(name, u0, last_phase):
            A = Arena()
            sg, m_sb, y = A.take(DC, T), A.take(DC, T), A.take(2, T)
            g_m, g_st, g_y, g_sum, g_hi = (sem(name + k) for k in ("_m", "_st", "_y", "_sum", "_hi"))
            with nc.Block() as block:
                @block.sync
                def _(sp):
                    if last_phase:
                        sp.dma_start(m_sb, m_dram.rearrange("c p t -> p c t")).then_inc(g_m, 16)
                    with sp.Fori(0, DC // 2) as it:
                        for u in range(2):
                            do_load(sp, Unit(u0, it, 2), u)
                    with sp.Fori(0, DC // 2) as it:
                        for u in range(2):
                            do_load(sp, Unit(u0 + DC, it, 2), u)
                            if not last_phase:
                                sp.wait_ge(g_y, it * 2 + (u + 1))
                                sp.dma_start(m_dram[ds(it * 2 + u, 1)].rearrange("o p t -> p (o t)"),
                                             m_sb[:, ds(it * 2 + u, 1)].rearrange("p o t -> p (o t)")
                                             ).then_inc(g_st, 16)
                    if not last_phase:
                        sp.wait_ge(g_st, 16 * DC)

                @block.tensor
                def _(pe):
                    for base, a in ((u0, acts_a), (u0 + DC, acts_b)):
                        with pe.Fori(0, DC // 2) as it:
                            for u in range(2):
                                project(pe, Unit(base, it, 2), u, a)

                @block.scalar
                def _(act):
                    with act.Fori(0, DC // 2) as it:
                        U = Unit(u0, it, 2)
                        for u in range(2):
                            act.wait_ge(w_used, U.at(u) + 1)
                            nc.scalar.activation(sg[:, ds(it * 2 + u, 1)].rearrange("p o (a b) -> p (o a) b", a=2),
                                                 proj_out(u), ACT.Sigmoid).then_inc(proj_free[u], 1)
                            do_hi(act, U, u)
                    with act.Fori(0, DC // 2) as it:
                        U = Unit(u0 + DC, it, 2)
                        for u in range(2):
                            do_hi(act, U, u)
                            if last_phase:
                                act.wait_ge(g_sum, it * 2 + (u + 1))
                                nc.scalar.activation(acts_a[:, 0, ds(it * 2 + u, 1)].rearrange("p o t -> p (o t)"),
                                                     y[:, u], ACT.Copy).then_inc(g_hi, 1)

                @block.vector
                def _(dve):
                    with dve.Fori(0, DC // 2) as it:
                        for u in range(2):
                            do_lo(dve, Unit(u0, it, 2), u)
                    if last_phase:
                        dve.wait_ge(g_m, 16)
                    with dve.Fori(0, DC // 2) as it:
                        U = Unit(u0 + DC, it, 2)
                        for u in range(2):
                            c = it * 2 + u
                            dve.wait_ge(w_used, U.at(u) + 1)
                            dve.wait_ge(proj_free[u], (u0 + DC) // 2 + 1)
                            gate = sg[:, ds(c, 1)].rearrange("p o (a b) -> p (o a) b", a=2)
                            if not last_phase:
                                nc.vector.tensor_tensor(m_sb[:, ds(c, 1)].rearrange("p o (a b) -> p (o a) b", a=2),
                                                        proj_out(u), gate, ALU.mult).then_inc(proj_free[u], 1)
                                dve.wait_ge(proj_free[u], U.half(u) + 2)
                                dve.sem_inc(g_y, 1)
                            else:
                                nc.vector.tensor_tensor(two(y[:, u]), proj_out(u), gate, ALU.mult
                                                        ).then_inc(proj_free[u], 1)
                                dve.wait_ge(proj_free[u], U.half(u) + 2)
                                nc.vector.tensor_tensor(y[:, u], y[:, u], m_sb[:, ds(c, 1)].rearrange("p o t -> p (o t)"),
                                                        ALU.add).then_inc(g_sum, 1)
                            do_lo(dve, U, u)
                            if last_phase:
                                dve.wait_ge(g_hi, c + 1)
                                hi, lo = (acts_a[:, k, ds(c, 1)].rearrange("p o t -> p (o t)") for k in range(2))
                                nc.vector.tensor_tensor(lo, y[:, u], hi.bitcast(F32), ALU.subtract
                                                        ).then_inc(g_y, 1)

        gate_phase("ga", U_GATT, False)

        A = Arena()
        hq, hv, gs = A.take(2, T), A.take(2, T), A.take(2, T)
        Pf, Pb, kf, kb = (A.take(2, T) for _ in range(4))
        Xf, Xb = A.take(T), A.take(T)
        Qs, Ks = A.take(2, T), A.take(2, T)
        kx, S = A.take(2, 4, P), A.take(2, 4, P)
        masks = A.take(LEVELS, P)
        pad = A.take(2)
        tots = A.take(2, TT)
        At0 = A.take(T)
        Qe = hg_more[:, 0:2]
        At = (At0, hg_more[:, 2])
        o_sb, rr = Qe[:, 0], Qe[:, 1]
        ENTER = ({1: 0, 2: 1, 3: 2, 5: 3}, {2: 0, 1: 1, 0: 2, 4: 3})
        MAKE = ((0, 1, 2, 4), (3, 2, 1, 5))
        names = """d_mask z_ready f_ready sum_ready lev_ready qkb_ready lev_done updf_step updb_step endf_ready
                   endb_ready kx_tr kx_ready kv_done st_ready o_ready sq_ready ss_ready ms_ready root_ready r_step
                   of_ready oh_ready ol_ready pad_ready""".split()
        (d_mask, z_ready, f_ready, sum_ready, lev_ready, qkb_ready, lev_done, updf_step, updb_step, endf_ready,
         endb_ready, kx_tr, kx_ready, kv_done, st_ready, o_ready, sq_ready, ss_ready, ms_ready, root_ready, r_step,
         of_ready, oh_ready, ol_ready, pad_ready) = (sem(n) for n in names)
        bank_taken = [sem("bank_taken0"), sem("bank_taken1")]
        HU = 5
        ZF, ZB, QH, GH, IH = range(HU)
        DIAG = LEVELS
        PROD = LEVELS + 1
        UPD = 1 + 2 * LEVELS
        SEQ_PE = "H0 L0 H1 L1 o H2 L2 H3 L3 n H4 L4 H5 L5 H6 L6 H7 L7 H8 T H9 V".split()
        SEQ_ACT = "L0 o U0 U1 n U2 f U3 T U4".split()
        SEQ_DVE = "Q1 s Q2 K1 Q3 U0 K2 Q4 K3 Q5 n U1 K4 Q6 m K5 f U2 K6 Z K7 U3 Q0 U4".split()
        SEQ_POOL = "B1 B2 B3 B4 B5 B6 Q7 Z B0".split()

        def halves(ap, B):
            return ap.rearrange("p (n h b) -> p n h b", h=2, b=B)

        def tot(Pr, B, half, direction):
            j = B - 1 if direction == 0 else 0
            a = halves(Pr, B)[:, :, half, j:j + 1]
            return a.broadcast_to([P, T // (2 * B), B]) if B > 1 else a

        def in_unit_act(act, U, u, i, b):
            do_hi(act, U, u)
            s = u % 2
            if i in (ZF, ZB):
                Pr, kr = (Pf, kf) if i == ZF else (Pb, kb)
                nc.scalar.activation(two(Pr[:, b]), proj_out(u), ACT.Sigmoid)
                nc.scalar.activation(two(kr[:, b]), proj_out(u), ACT.Sigmoid, scale=-1.0).then_inc(proj_free[s], 1)
            elif i == IH:
                nc.scalar.activation(two(hv[:, b]), proj_out(u), ACT.Copy).then_inc(proj_free[s], 1)
            else:
                nc.scalar.activation(two((hq if i == QH else gs)[:, b]), proj_out(u), ACT.Sigmoid).then_inc(z_ready, 1)

        def in_unit_dve(dve, U, u, i, b, hd):
            s = u % 2
            do_lo(dve, U, u)
            if i in (ZF, ZB):
                Pr, kr = (Pf, kf) if i == ZF else (Pb, kb)
                lbc, omc = (lb[:, k, i, ds(hd, 1)] for k in range(2))
                dve.wait_ge(proj_free[s], U.half(u) + 2)
                nc.vector.tensor_scalar(Pr[:, b], Pr[:, b], omc, lbc, ALU.mult, ALU.add).then_inc(f_ready, 1)
                nc.vector.tensor_scalar(kr[:, b], kr[:, b], omc, None, ALU.mult).then_inc(f_ready, 1)
            elif i in (QH, GH):
                dst = (hq if i == QH else gs)[:, b]
                dve.wait_ge(z_ready, hd * 2 + (1 if i == QH else 2))
                nc.vector.tensor_tensor(two(dst), two(dst), proj_out(u), ALU.mult).then_inc(proj_free[s], 1)

        BANKS = ((4, 0, T_PROMPT), (5, T_PROMPT, T))

        def head_pe(pe, hd, b, kind, k, first):
            if kind == "L":
                if k == DIAG:
                    pe.wait_ge(sum_ready, hd + 1)
                    l, r = Ks[:, 1], hq[:, b]
                else:
                    pe.wait_ge(lev_ready, hd * LEVELS + (k + 1))
                    l, r = Ks[:, k % 2], Qs[:, k % 2]
                for bank, (bk, t0, t1) in enumerate(BANKS):
                    pe.wait_ge(bank_taken[bank], hd * PROD + (k + 1))
                    for t in range(t0, t1, P):
                        m = nc.tensor.matmul(psum[:, bk, t - t0:t - t0 + P], l[:, t:t + P], r[:, t:t + P],
                                             start=True, stop=True)
                    m.then_inc(lev_done, 1)
            elif kind == "T":
                pe.wait_ge(endf_ready, hd + 1)
                pe.wait_ge(endb_ready, hd + 1)
                pe.wait_ge(ms_ready, hd + 1)
                for d in range(2):
                    for j, c in enumerate(MAKE[d]):
                        m = nc.tensor.transpose(psum[:, 6 + d, j * P:(j + 1) * P], Ks[:, d, c * P:(c + 1) * P], ident)
                    m.then_inc(kx_tr, 1)
            elif kind == "V":
                for d in range(2):
                    pe.wait_ge(kx_ready, hd * 2 + (d + 1))
                    for j, c in enumerate(MAKE[d]):
                        m = nc.tensor.matmul(psum[:, 6 + d, j * P:(j + 1) * P], kx[:, d, j], hv[:, b, c * P:(c + 1) * P],
                                             start=True, stop=True)
                    m.then_inc(kv_done, 1)
            elif kind == "o":
                pe.wait_ge(st_ready, hd * 6 + 6)
                for bank, (bk, t0, t1) in enumerate(BANKS):
                    pe.wait_ge(bank_taken[bank], (hd + 1) * PROD + 1)
                    for t in range(t0, t1, P):
                        c = t // P
                        o = psum[:, bk + 2, t - t0:t - t0 + P]
                        parts = [(hv[:, b, t:t + P], At[b][:, t:t + P])]
                        parts += [(S[:, d, ENTER[d][c]], Qe[:, d, t:t + P]) for d in range(2) if c in ENTER[d]]
                        for n, (l, r) in enumerate(parts):
                            m = nc.tensor.matmul(o, l, r, start=(n == 0), stop=(n == len(parts) - 1))
                    m.then_inc(o_ready, 1)
            else:
                for bank, (bk, t0, t1) in enumerate(BANKS):
                    pe.wait_ge(sq_ready, hd * 2 + (bank + 1))
                    nc.tensor.matmul(psum[:, bk + 2, 0:t1 - t0], ones, rr[:, t0:t1], start=True, stop=True
                                     ).then_inc(ss_ready, 1)

        def head_act(act, hd, b, kind, k, first):
            if kind == "L":
                for bank, (bk, t0, t1) in enumerate(BANKS):
                    act.wait_ge(lev_done, hd * (2 * PROD) + (bank + 1))
                    nc.scalar.activation(At[b][:, t0:t1], psum[:, bk, 0:t1 - t0], ACT.Copy).then_inc(bank_taken[bank], 1)
            elif kind == "T":
                for d in range(2):
                    act.wait_ge(kx_tr, hd * 2 + (d + 1))
                    nc.scalar.activation(kx[:, d].rearrange("p a b -> p (a b)"), psum[:, 6 + d, :], ACT.Copy
                                         ).then_inc(kx_ready, 1)
            elif kind == "o":
                act.wait_ge(o_ready, hd * 2 + 2)
                for bank, (bk, t0, t1) in enumerate(BANKS):
                    nc.scalar.activation(o_sb[:, t0:t1], psum[:, bk + 2, 0:t1 - t0], ACT.Copy)
                    nc.scalar.activation(rr[:, t0:t1], psum[:, bk + 2, 0:t1 - t0], ACT.Square).then_inc(sq_ready, 1)
            elif kind == "n":
                act.wait_ge(ms_ready, hd + 2)
                nc.scalar.activation(rr, rr, ACT.Sqrt).then_inc(root_ready, 1)
            elif kind == "f":
                act.wait_ge(of_ready, hd + 1)
                nc.scalar.activation(acts_b[:, 0, ds(hd, 1)].rearrange("p o t -> p (o t)"), At[b], ACT.Copy
                                     ).then_inc(oh_ready, 1)

        def operands(hd, k, directions):
            B = 1 << k
            Q, K = halves(Qs[:, k % 2], B), halves(Ks[:, k % 2], B)
            for o, a, x, h in directions:
                o = Q if o == "q" else K
                m = nc.vector.tensor_tensor(o[:, :, h], halves(a, B)[:, :, h], halves(x, B)[:, :, h], ALU.mult)
            return m

        def update(eng, tt, hd, k, Pr, X, d, step):
            B = 1 << k
            xv, pv = halves(X, B)[:, :, d], halves(Pr, B)[:, :, 1 - d]
            tt(xv, xv, tot(Pr, B, 1 - d, d), ALU.mult).then_inc(step, 1)
            eng.wait_ge(step, hd * UPD + (2 + 2 * k))
            tt(pv, pv, tot(Pr, B, d, d), ALU.mult).then_inc(step, 1)

        def head_dve(dve, hd, b, kind, k, first):
            q, pf, pb, kf_, kb_ = hq[:, b], Pf[:, b], Pb[:, b], kf[:, b], kb[:, b]
            if kind == "Q":
                if k == 0:
                    if not first:
                        dve.wait_ge(endf_ready, hd)
                        dve.wait_ge(endb_ready, hd)
                        dve.wait_ge(kx_tr, hd * 2)
                    nc.vector.memset(Xf, 1.0).then_inc(updf_step, 1)
                    nc.vector.memset(Xb, 1.0).then_inc(updb_step, 1)
                    dve.wait_ge(f_ready, hd * 4 + 4)
                elif k >= 2:
                    dve.wait_ge(lev_done, hd * (2 * PROD) + 2 * (k - 1))
                dve.wait_ge(updb_step, hd * UPD + (1 + 2 * k))
                operands(hd, k, (("q", q, pb, 0), ("k", kb_, Xb, 1))).then_inc(qkb_ready, 1)
                dve.wait_ge(updf_step, hd * UPD + (1 + 2 * k))
                operands(hd, k, (("q", q, pf, 1), ("k", kf_, Xf, 0))).then_inc(lev_ready, 1)
                dve.wait_ge(lev_ready, hd * LEVELS + (k + 1))
                update(dve, nc.vector.tensor_tensor, hd, k, pf, Xf, 0, updf_step)
            elif kind == "K":
                dve.wait_ge(lev_done, hd * (2 * PROD) + 2 * (k + 1))
                nc.vector.tensor_copy(pad[:, 0:1], pad[:, 1:2])
                for bank, (bk, t0, t1) in enumerate(BANKS):
                    n = (t1 - t0) // P
                    mask = ident.rearrange("p (o b) -> p o b", o=1) if k == DIAG else masks[:, k:k + 1]
                    nc.vector.copy_predicated(At[b][:, t0:t1].rearrange("p (n b) -> p n b", n=n),
                                              mask.bitcast(U32).broadcast_to([P, n, P]),
                                              psum[:, bk, 0:t1 - t0].rearrange("p (n b) -> p n b", n=n)
                                              ).then_inc(bank_taken[bank], 1)
            elif kind == "Z":
                dve.wait_ge(lev_done, hd * (2 * PROD) + 2 * LEVELS)
                dve.wait_ge(updf_step, (hd + 1) * UPD)
                nc.vector.tensor_tensor(Ks[:, 0], kf_, Xf, ALU.mult)
                nc.vector.tensor_tensor(Qe[:, 0], q, pf, ALU.mult)
                nc.vector.tensor_copy(tots[:, 0], pf[:, P - 1:T:P])
                dve.wait_ge(updb_step, (hd + 1) * UPD)
                nc.vector.tensor_copy(tots[:, 1], pb[:, 0:T:P]).then_inc(endf_ready, 1)
            elif kind == "s":
                n = hd * 6
                for d in range(2):
                    dve.wait_ge(kv_done, hd * 2 + (d + 1))
                    D4 = psum[:, 6 + d, :].rearrange("p (a b) -> p a b", a=4)
                    nc.vector.tensor_copy(S[:, d, 0:4:3], D4[:, 0:4:3]).then_inc(st_ready, 1)
                    for j in (1, 2):
                        c = MAKE[d][j]
                        dve.wait_ge(st_ready, n + 3 * d + j)
                        nc.vector.scalar_tensor_tensor(out=S[:, d, j], in0=S[:, d, j - 1], scalar=tots[:, d, c:c + 1],
                                                       in1=D4[:, j], op0=ALU.mult, op1=ALU.add).then_inc(st_ready, 1)
            elif kind == "n":
                for bank, (bk, t0, t1) in enumerate(BANKS):
                    dve.wait_ge(ss_ready, hd * 2 + (bank + 1))
                    m = nc.vector.tensor_scalar(rr[:, t0:t1], psum[:, bk + 2, 0:t1 - t0], 1.0 / P, EPS, ALU.mult, ALU.add)
                m.then_inc(ms_ready, 1)
            elif kind == "m":
                dve.wait_ge(root_ready, hd + 1)
                nc.vector.reciprocal(rr, rr).then_inc(r_step, 1)
                dve.wait_ge(r_step, hd * 2 + 1)
                nc.vector.tensor_tensor(rr, rr, o_sb, ALU.mult).then_inc(r_step, 1)
                dve.wait_ge(r_step, hd * 2 + 2)
                nc.vector.scalar_tensor_tensor(out=At[b], in0=rr, scalar=vec[:, ds(hd + V_GH, 1)],
                                               in1=gs[:, b], op0=ALU.mult, op1=ALU.mult).then_inc(of_ready, 1)
            elif kind == "f":
                dve.wait_ge(oh_ready, hd + 1)
                hi, lo = (acts_b[:, j, ds(hd, 1)].rearrange("p o t -> p (o t)") for j in range(2))
                nc.vector.tensor_tensor(lo, At[b], hi.bitcast(F32), ALU.subtract).then_inc(ol_ready, 1)

        def head_pool(pool, hd, b, kind, k, first):
            if kind == "B":
                pool.wait_ge(qkb_ready, hd * LEVELS + (k + 1))
                update(pool, nc.gpsimd.tensor_tensor, hd, k, Pb[:, b], Xb, 1, updb_step)
            elif kind == "Q":
                pool.wait_ge(lev_done, hd * (2 * PROD) + 2 * (LEVELS - 1))
                nc.gpsimd.tensor_tensor(Ks[:, 1], kf[:, b], kb[:, b], ALU.add).then_inc(sum_ready, 1)
            else:
                pool.wait_ge(updb_step, (hd + 1) * UPD)
                pool.wait_ge(lev_done, hd * (2 * PROD) + 2 * LEVELS)
                nc.gpsimd.tensor_tensor(Qe[:, 1], hq[:, b], Pb[:, b], ALU.mult)
                pool.wait_ge(lev_done, (hd + 1) * (2 * PROD))
                nc.gpsimd.tensor_tensor(Ks[:, 1], kb[:, b], Xb, ALU.mult).then_inc(endb_ready, 1)

        def run_heads(eng, seq, head_fn, unit_fn, starts="Q0 B0".split()):
            def body(hd, b, U, next_u, prev=True, nxt=True):
                for step in seq:
                    kind, k = step[0], int(step[1:] or 0)
                    if kind in "HU":
                        if nxt:
                            i = k // 2 if kind == "H" else k
                            unit_fn(U, next_u + i, i, 1 - b, hd + 1, k)
                    elif step in starts:
                        if nxt:
                            head_fn(eng, hd + 1, 1 - b, kind, k, False)
                    elif kind.islower():
                        if prev:
                            head_fn(eng, hd - 1, 1 - b, kind, k, False)
                    else:
                        head_fn(eng, hd, b, kind, k, False)
            for step in seq:
                if step[0] in "HU":
                    k = int(step[1:])
                    i = k // 2 if step[0] == "H" else k
                    unit_fn(Unit(U_HG), i, i, 0, 0, k)
            for step in seq:
                if step in starts:
                    head_fn(eng, 0, 0, step[0], 0, True)
            body(0, 0, Unit(U_HG), HU, prev=False)
            with eng.Fori(0, H_HEADS // 2 - 1) as it:
                for b in (1, 0):
                    body(it * 2 + (2 - b), b, Unit(U_HG, it, 2 * HU), (3 - b) * HU)
            body(H_HEADS - 1, 1, None, None, nxt=False)
            for step in seq:
                if step[0].islower():
                    head_fn(eng, H_HEADS - 1, 1, step[0], 0, False)

        with nc.Block() as block:
            @block.sync
            def _(sp):
                sp.dma_start(masks, consts[:, C_MASK:C_MASK + LEVELS * P].rearrange("p (a b) -> p a b", a=LEVELS)
                             ).then_inc(d_mask, 16)
                with sp.Fori(0, N_HG // 2) as it:
                    for u in range(2):
                        do_load(sp, Unit(U_HG, it, 2), u)

            @block.tensor
            def _(pe):
                run_heads(pe, SEQ_PE, head_pe, lambda U, u, i, b, h, k: project(
                    pe, U, u, acts_a, tokens_out=(i == IH), halves=(k % 2,)))

            @block.scalar
            def _(act):
                run_heads(act, SEQ_ACT, head_act, lambda U, u, i, b, h, k: in_unit_act(act, U, u, i, b))

            @block.vector
            def _(dve):
                for b in range(2):
                    dve.sem_inc(bank_taken[b], 1)
                dve.sem_inc(ms_ready, 1)
                nc.vector.memset(pad, 0.0).then_inc(pad_ready, 1)
                dve.wait_ge(pad_ready, 1)
                dve.wait_ge(d_mask, 16)
                run_heads(dve, SEQ_DVE, head_dve, lambda U, u, i, b, h, k: in_unit_dve(dve, U, u, i, b, h))

            @block.gpsimd
            def _(pool):
                run_heads(pool, SEQ_POOL, head_pool, None)

        gate_phase("gb", U_GHG, True)

        A = Arena()
        x1 = A.take(DC, T)
        x1_flat = arena[:, 0:DC * T]
        d_x1, x1_done = sem("d_x1"), sem("x1_done")
        PIECES = ((0, 0, HALF, 0), (1, HALF, T_PROMPT, 0), (1, T_PROMPT, T, 1))
        with nc.Block() as block:
            @block.sync
            def _(sp):
                sp.dma_start(x1_flat, x_t).then_inc(d_x1, 16)
                with sp.Fori(0, DC // 2) as it:
                    for u in range(2):
                        do_load(sp, Unit(U_OUT, it, 2), u)

            @block.tensor
            def _(pe):
                with pe.Fori(0, DC // 2) as it:
                    for u in range(2):
                        project(pe, Unit(U_OUT, it, 2), u, acts_a)

            @block.scalar
            def _(act):
                with act.Fori(0, DC // 2) as it:
                    for u in range(2):
                        do_hi(act, Unit(U_OUT, it, 2), u)

            @block.vector
            def _(dve):
                dve.wait_ge(d_x1, 16)
                with dve.Fori(0, DC // 2) as it:
                    U = Unit(U_OUT, it, 2)
                    for u in range(2):
                        dve.wait_ge(w_used, U.at(u) + 1)
                        for bank, t0, t1, g in PIECES:
                            x = x1[:, ds(it * 2 + u, 1), t0:t1].rearrange("p o t -> p (o t)")
                            gate = mod[:, ds(it * 2 + (GATE1 * DC + u), 1), g:g + 1].rearrange("p o t -> p (o t)")
                            m = nc.vector.scalar_tensor_tensor(
                                out=x, in0=psum[:, 2 * u + bank, t0 - bank * HALF:t1 - bank * HALF], scalar=gate,
                                in1=x, op0=ALU.mult, op1=ALU.add)
                        m.then_inc(proj_free[u], 1)
                        do_lo(dve, U, u)
        n2 = Norm("n2", x1, lambda d, g: modcol(SCALE2, d, g), lambda d, g: modcol(SHIFT2, d, g), acts_a,
                  norm_work(A))
        x1_stored = sem("x1_stored")
        with nc.Block() as block:
            @block.sync
            def _(sp):
                sp.dma_start(x1_dram, x1_flat).then_inc(x1_stored, 16)
                sp.wait_ge(x1_stored, 16)

            @block.scalar
            def _(act):
                n2.stats_act(act)
                n2.apply_act(act)

            @block.tensor
            def _(pe):
                n2.stats_pe(pe)

            @block.vector
            def _(dve):
                n2.stats_dve(dve)
                n2.apply_dve(dve)

        RING = 16
        e_split, e_raw, e_gl, oh_j = room.take(
            ("e_split", [P, 2, 2, DC, P], F32R), ("e_raw", [P, 2, DC, P], F32), ("e_gl", [P, 2, T], F32),
            ("oh_j", [P, RING, NKEYS], F32))
        gl_dram = nc.dram_tensor("gelu_scratch", (EARLY, P, T), F32, kind="Internal").ap()
        e_in, e_out = [sem("e_in0"), sem("e_in1")], [sem("e_out0"), sem("e_out1")]
        e_hi, e_lo, e_done, e_gelu = sem("e_hi"), sem("e_lo"), sem("e_done"), sem("e_gelu")

        def e_load(sp, e, s):
            sp.dma_start(e_raw[:, s], u_early[ds(e, 1)].rearrange("o p (c k) -> p (o c) k", c=DC)
                         ).then_inc(e_in[s], 16)

        def early_sync(sp, E, u):
            sp.wait_ge(e_lo, E.at(u) + 1)
            e_load(sp, E.at(u) + EARLY_LEAD, u % 2)
            sp.wait_ge(e_gelu, E.at(u) * 2 + 4)
            sp.dma_start(gl_dram[ds(E.at(u), 1)].rearrange("o p t -> p (o t)"), e_gl[:, u % 2]
                         ).then_inc(e_out[u % 2], 16)

        def early_hi(act, s):
            nc.scalar.activation(e_split[:, s, 0], e_raw[:, s], ACT.Copy).then_inc(e_hi, 1)

        def early_act(act, E, u, t):
            act.wait_ge(e_done, E.at(u) * 2 + (t + 1))
            if t == 0:
                act.wait_ge(e_out[u % 2], E.half(u) * 16 + 16)
            nc.scalar.activation(e_gl[:, u % 2, t * HALF:(t + 1) * HALF], psum[:, 6 + t, 0:HALF], ACT.Gelu
                                 ).then_inc(e_gelu, 1)
            if t == 1:
                act.wait_ge(e_in[u % 2], E.half(u) * 16 + 32)
                early_hi(act, u % 2)

        def early_lo(pool, e, s):
            pool.wait_ge(e_hi, e + 1)
            nc.gpsimd.tensor_tensor(e_split[:, s, 1], e_raw[:, s], e_split[:, s, 0].bitcast(F32), ALU.subtract
                                    ).then_inc(e_lo, 1)

        def early_pe(pe, E, u, t):
            pe.wait_ge(e_lo, E.at(u) + 1)
            pe.wait_ge(e_gelu, E.at(u) * 2 + (t + 1))
            for d in range(DC):
                for i, (wh, ah) in enumerate(((0, 0), (0, 1), (1, 0))):
                    m = nc.tensor.matmul(psum[:, 6 + t, 0:HALF], e_split[:, u % 2, wh, d, :],
                                         acts_a[:, ah, d, t * HALF:(t + 1) * HALF],
                                         start=(d == 0 and i == 0), stop=(d == DC - 1 and i == 2))
            m.then_inc(e_done, 1)

        A = Arena()
        KH = TOPK // 2
        keys = A.take(2 * PH * NKEYS)
        qh_sb, s_sb, s_cut = A.take(2, T), A.take(2, TT, NKEYS), A.take(TT, NKEYS)
        sv = A.take(2, TT, TOPK)
        si = A.take(2, TT, TOPK).bitcast(U32)
        sf = A.take(2, TT, TOPK)
        cv, cid, cv_cut = A.take(TT, CAND), A.take(TT, CAND), A.take(TT, CAND)
        tv = A.take(TT, TOPK)
        tp = A.take(TT, TOPK).bitcast(U32)
        tpf, te, tsum = A.take(TT, TOPK), A.take(TT, TOPK), A.take(TT)
        onehot = A.take(TOPK, CAND)
        eid, gate = A.take(TT, PH * TOPK), A.take(TT, PH * TOPK)
        ei = A.take(TT, PH * TOPK).bitcast(U32)
        te_ji, te_j = A.take(TT, PH * TOPK).bitcast(U32), A.take(TT, PH * TOPK)
        pad = A.take(2)
        gate_t, i_t = w_raw[:].rearrange("p a b c -> p (a b c)")[:, 0:T], w_raw[:].rearrange("p a b c -> p (a b c)")[:, T:2 * T]
        j_t = arena[:, ARENA - T:ARENA]
        d_keys, qh_ready, s_done, s_ready = sem("d_keys"), sem("qh_ready"), sem("s_done"), sem("s_ready")
        s_bank = [sem("s_bank0"), sem("s_bank1")]
        k_step, sf_ready, cid_ready, ts_ready, te_ready, head_done = (
            sem(n) for n in ("k_step", "sf_ready", "cid_ready", "ts_ready", "te_ready", "head_done"))
        tab_tr, tab_done, slot_free = sem("tab_tr"), sem("tab_done"), sem("slot_free")
        STEPS = 35
        rows = []
        at = 0
        for a in range(TOPK):
            rows.append((a, at, ROW_LEN[a]))
            at += ROW_LEN[a]
        SINGLE = TOPK // 2

        def pair_sums(eng_tt, out, first, second):
            for a, o, n in rows[:SINGLE]:
                m = eng_tt(out[:, :, o:o + n], second[:, :, 0:n], first[:, :, a:a + 1].broadcast_to([P, TT, n]), ALU.add)
            o = rows[SINGLE][1]
            return eng_tt(out[:, :, o:o + TOPK - SINGLE], first[:, :, SINGLE:TOPK],
                          second[:, :, 0:1].broadcast_to([P, TT, TOPK - SINGLE]), ALU.add)

        with nc.Block() as block:
            @block.sync
            def _(sp):
                for e in range(EARLY_LEAD):
                    e_load(sp, e, e)
                sp.dma_start(keys, keys_t).then_inc(d_keys, 16)
                with sp.Fori(0, PH // 2) as it:
                    for hh in range(2):
                        for u in range(2):
                            do_load(sp, Unit(U_PQ, it, 4), 2 * hh + u)
                        for k in range(EARLY_PQ):
                            early_sync(sp, Unit(0, it, 2 * EARLY_PQ), hh * EARLY_PQ + k)

            @block.tensor
            def _(pe):
                def scores(n, u, hp):
                    pe.wait_ge(qh_ready, n + 1)
                    pe.wait_ge(s_bank[0], n + 1)
                    for t in range(TT):
                        m = nc.tensor.matmul(psum[:, 4 + t // 4, t % 4 * P:t % 4 * P + P],
                                             qh_sb[:, u, t * P:(t + 1) * P], keys[:, ds(hp, NKEYS)],
                                             start=True, stop=True)
                    m.then_inc(s_done, 1)
                pe.wait_ge(d_keys, 16)
                with pe.Fori(0, PH // 2) as it:
                    U, E = Unit(U_PQ, it, 4), Unit(0, it, 2 * EARLY_PQ)

                    def early(k):
                        for t in range(2):
                            early_pe(pe, E, k, t)
                    for hh in range(2):
                        for u in range(2):
                            project(pe, U, 2 * hh + u, acts_a)
                        for u in range(2):
                            n = it * 4 + (2 * hh + u)
                            scores(n, u, n * NKEYS)
                            early(hh * EARLY_PQ + u)
                        for k in range(2, EARLY_PQ):
                            early(hh * EARLY_PQ + k)
                pe.wait_ge(tab_done, 1)
                for k, tab in enumerate((gate, eid, te_j)):
                    for t in range(TT):
                        m = nc.tensor.transpose(psum[:, 2 * k + t // 4, t % 4 * P:t % 4 * P + P], tab[:, t], ident)
                    m.then_inc(tab_tr, 1)

            @block.scalar
            def _(act):
                act.sem_inc(e_gelu, 2)
                for e in range(EARLY_LEAD):
                    act.sem_inc(e_out[e], 16)
                    act.wait_ge(e_in[e], 16)
                    early_hi(act, e)
                with act.Fori(0, PH // 2) as it:
                    U, E = Unit(U_PQ, it, 4), Unit(0, it, 2 * EARLY_PQ)

                    def early(k):
                        for t in range(2):
                            early_act(act, E, k, t)
                    for hh in range(2):
                        for u in range(2):
                            v = 2 * hh + u
                            act.wait_ge(w_used, U.at(v) + 1)
                            nc.scalar.activation(two(qh_sb[:, u]), proj_out(v), ACT.Copy).then_inc(proj_free[u], 1)
                            act.wait_ge(proj_free[u], U.half(v) + 2)
                            act.sem_inc(qh_ready, 1)
                            do_hi(act, U, v)
                        for u in range(2):
                            n = it * 4 + (2 * hh + u)
                            act.wait_ge(s_done, n + 1)
                            act.wait_ge(slot_free, n + 1)
                            flat = s_sb[:, u].rearrange("p a b -> p (a b)")
                            nc.scalar.activation(flat[:, 0:512], psum[:, 4, :], ACT.Copy)
                            nc.scalar.activation(flat[:, 512:T], psum[:, 5, 0:T - 512], ACT.Copy).then_inc(s_bank[0], 1)
                            early(hh * EARLY_PQ + u)
                        for k in range(2, EARLY_PQ):
                            early(hh * EARLY_PQ + k)
                        act.wait_ge(ts_ready, it * 2 + (hh + 1))
                        nc.scalar.activation(te, te, ACT.Exp).then_inc(te_ready, 1)
                for s in range(2):
                    act.wait_ge(raw_ready[s], 16 * (UNITS + LEAD) // 2)
                for k, dst in enumerate((gate_t, i_t, j_t)):
                    act.wait_ge(tab_tr, k + 1)
                    nc.scalar.activation(dst[:, 0:512], psum[:, 2 * k, :], ACT.Copy)
                    nc.scalar.activation(dst[:, 512:T], psum[:, 2 * k + 1, 0:T - 512], ACT.Copy).then_inc(te_ready, 1)

            @block.gpsimd
            def _(pool):
                for e in range(EARLY_LEAD):
                    early_lo(pool, e, e)
                with pool.Fori(0, PH // 2) as it:
                    E = Unit(0, it, 2 * EARLY_PQ)
                    for hh in range(2):
                        for k in range(EARLY_PQ):
                            if k == EARLY_PQ - 2:
                                pool.wait_ge(sf_ready, it * 2 + (hh + 1))
                                pair_sums(nc.gpsimd.tensor_tensor, cid, sf[:, 0], sf[:, 1]).then_inc(cid_ready, 1)
                            e = hh * EARLY_PQ + k
                            early_lo(pool, E.at(e) + EARLY_LEAD, e % 2)

            @block.vector
            def _(dve):
                dve.sem_inc(s_bank[0], 1)
                dve.sem_inc(slot_free, 2)
                nc.vector.memset(pad, 0.0).then_inc(k_step, 1)
                dve.wait_ge(k_step, 1)
                with dve.Fori(0, PH // 2) as it:
                    U = Unit(U_PQ, it, 4)
                    count = [0]

                    def step(ins):
                        count[0] += 1
                        ins.then_inc(k_step, 1)
                        dve.wait_ge(k_step, it * (2 * STEPS) + (count[0] + 1))

                    def carry():
                        nc.vector.tensor_copy(pad[:, 0:1], pad[:, 1:2])

                    def best16(src, cut, val, idx):
                        for t in range(TT):
                            m = nc.vector.max(val[:, t, 0:KH], src[:, t])
                        step(m)
                        carry()
                        for t in range(TT):
                            nc.vector.max_index(idx[:, t, 0:KH], val[:, t, 0:KH], src[:, t])
                            m = nc.vector.match_replace(cut[:, t], val[:, t, 0:KH], src[:, t], -3.0e38)
                        step(m)
                        carry()
                        for t in range(TT):
                            m = nc.vector.max(val[:, t, KH:TOPK], cut[:, t])
                        step(m)
                        carry()
                        for t in range(TT):
                            m = nc.vector.max_index(idx[:, t, KH:TOPK], val[:, t, KH:TOPK], cut[:, t])
                        step(m)
                    for hh in range(2):
                        head = it * 2 + hh
                        for u in range(2):
                            do_lo(dve, U, 2 * hh + u)
                        for u in range(2):
                            dve.wait_ge(s_bank[0], it * 4 + (2 * hh + u + 2))
                            carry()
                            best16(s_sb[:, u], s_cut, sv[:, u], si[:, u])
                            dve.sem_inc(slot_free, 1)
                            if u == 0:
                                step(nc.vector.tensor_scalar(sf[:, 0], si[:, 0], float(NKEYS), None, ALU.mult))
                            else:
                                nc.vector.tensor_copy(sf[:, 1], si[:, 1]).then_inc(sf_ready, 1)
                        step(pair_sums(nc.vector.tensor_tensor, cv, sv[:, 0], sv[:, 1]))
                        carry()
                        best16(cv, cv_cut, tv, tp)
                        nc.vector.tensor_copy(tpf, tp).then_inc(k_step, 1)
                        nc.vector.tensor_tensor(te, tv, tv[:, :, 0:1].broadcast_to([P, TT, TOPK]), ALU.subtract
                                                ).then_inc(ts_ready, 1)
                        count[0] += 1
                        dve.wait_ge(k_step, it * (2 * STEPS) + (count[0] + 1))
                        dve.wait_ge(cid_ready, head + 1)
                        for t in range(TT):
                            step(nc.vector.tensor_tensor(onehot, iota[:, 0:CAND].rearrange("p (o c) -> p o c", o=1)
                                                         .broadcast_to([P, TOPK, CAND]),
                                                         tpf[:, t].rearrange("p (k o) -> p k o", o=1)
                                                         .broadcast_to([P, TOPK, CAND]), ALU.is_equal))
                            step(nc.vector.tensor_tensor(onehot, onehot, cid[:, t:t + 1].broadcast_to([P, TOPK, CAND]),
                                                         ALU.mult))
                            step(nc.vector.reduce_sum(eid[:, t, ds(head * TOPK, TOPK)], onehot, AX_X))
                        dve.wait_ge(te_ready, head + 1)
                        step(nc.vector.reduce_sum(tsum, te, AX_X))
                        step(nc.vector.reciprocal(tsum, tsum))
                        nc.vector.tensor_tensor(gate[:, :, ds(head * TOPK, TOPK)], te,
                                                tsum.rearrange("p (t o) -> p t o", o=1).broadcast_to([P, TT, TOPK]),
                                                ALU.mult).then_inc(head_done, 1)
                        assert count[0] == STEPS * (hh + 1), count
                dve.wait_ge(head_done, PH)
                nc.vector.tensor_copy(ei, eid).then_inc(head_done, 1)
                dve.wait_ge(head_done, PH + 1)
                nc.vector.tensor_scalar(te_ji, ei, NKEYS - 1, None, ALU.bitwise_and)
                nc.vector.tensor_scalar(ei, ei, 7, None, ALU.logical_shift_right).then_inc(head_done, 1)
                dve.wait_ge(head_done, PH + 2)
                nc.vector.tensor_copy(eid, ei)
                nc.vector.tensor_copy(te_j, te_ji).then_inc(tab_done, 1)


        TB = 64
        NB = T // TB
        c_dram = nc.dram_tensor("gates_scratch", (NB, P, NKEYS * TB), F32, kind="Internal").ap()
        A = Arena()
        c_sb = A.take(2, NKEYS, TB)
        oh_i = A.take(RING, NKEYS)
        onehot_ready, onehot_used, c_bank, c_stored = sem("onehot_ready"), sem("onehot_used"), sem("c_bank"), [sem("c_stored0"), sem("c_stored1")]
        Q4 = 4
        QUADS, HALVES = 2 * TB // Q4, 8
        assert HALVES * RING == 2 * TB and EARLY == PH * EARLY_PQ + NB // 2 * HALVES // 2
        with nc.Block() as block:
            @block.vector
            def _(dve):
                dve.sem_inc(onehot_used, RING // Q4)
                with dve.Fori(0, T // RING) as it:
                    for q in range(RING // Q4):
                        dve.wait_ge(onehot_used, it * (RING // Q4) + (q + 1))
                        for k in range(q * Q4, (q + 1) * Q4):
                            t = it * RING + k
                            nc.vector.tensor_scalar(oh_i[:, k], iota, i_t[:, ds(t, 1)], None, ALU.is_equal)
                            m = nc.vector.tensor_scalar(oh_j[:, k], iota, j_t[:, ds(t, 1)], gate_t[:, ds(t, 1)],
                                                        ALU.is_equal, ALU.mult)
                        m.then_inc(onehot_ready, 1)

            @block.tensor
            def _(pe):
                with pe.Fori(0, NB // 2) as blk:
                    E = Unit(PH * EARLY_PQ, blk, HALVES // 2)
                    for half in range(HALVES):
                        for q in range(RING // Q4):
                            n = blk * QUADS + (half * (RING // Q4) + q + 1)
                            pe.wait_ge(onehot_ready, n)
                            pe.wait_ge(c_bank, n)
                            for k in range(Q4):
                                m = nc.tensor.matmul(psum[:, q % 2, k * P:(k + 1) * P], oh_i[:, q * Q4 + k],
                                                     oh_j[:, q * Q4 + k], start=True, stop=True)
                            m.then_inc(onehot_used, 1)
                        early_pe(pe, E, half // 2, half % 2)

            @block.gpsimd
            def _(pool):
                with pool.Fori(0, NB // 2) as blk:
                    E = Unit(PH * EARLY_PQ, blk, HALVES // 2)
                    for k in range(HALVES // 2):
                        early_lo(pool, E.at(k) + EARLY_LEAD, k % 2)

            @block.scalar
            def _(act):
                act.sem_inc(c_bank, 2)
                for s in range(2):
                    act.sem_inc(c_stored[s], 16)
                with act.Fori(0, NB // 2) as blk:
                    E = Unit(PH * EARLY_PQ, blk, HALVES // 2)
                    for half in range(HALVES):
                        s, part = half // (HALVES // 2), half % (HALVES // 2)
                        if part == 0:
                            act.wait_ge(c_stored[s], blk * 16 + 16)
                        for q in range(RING // Q4):
                            act.wait_ge(onehot_used, blk * QUADS + (half * (RING // Q4) + q + RING // Q4 + 1))
                            t = part * RING + q * Q4
                            nc.scalar.activation(c_sb[:, s, :, t:t + Q4].rearrange("p j t -> p t j"),
                                                 psum[:, q % 2, :].rearrange("p (t j) -> p t j", t=Q4), ACT.Copy
                                                 ).then_inc(c_bank, 1)
                        early_act(act, E, half // 2, half % 2)

            @block.sync
            def _(sp):
                with sp.Fori(0, NB // 2) as blk:
                    E = Unit(PH * EARLY_PQ, blk, HALVES // 2)
                    for s in range(2):
                        for k in range(HALVES // 4):
                            early_sync(sp, E, s * (HALVES // 4) + k)
                        sp.wait_ge(c_bank, blk * QUADS + ((s + 1) * (TB // Q4) + 2))
                        sp.dma_start(c_dram[ds(blk * 2 + s, 1)].rearrange("o p n -> p (o n)"),
                                     c_sb[:, s].rearrange("p j t -> p (j t)")).then_inc(c_stored[s], 16)
                for s in range(2):
                    sp.wait_ge(c_stored[s], 16 * (NB // 2 + 1))
                    sp.wait_ge(e_out[s], 16 * (EARLY // 2 + 1))

        A = Arena()
        LATE, EARLY_LOT = 0, 1
        y_sb = A.take(TT, D)
        v_raw = A.take(4, D).rearrange("p (b s) n -> p b s n", b=2)
        c_lot = A.take(4, T).rearrange("p (b s) t -> p b s t", b=2)
        gl_early, gl_late = A.take(2, T), A.take(T)
        v_split, g_split = room.take(("v_split", [P, 2, 2, 2, D], F32R), ("g_split", [P, 2, 2, 2, T], F32R))
        PAIRS = EARLY
        u_in, pair_in = ([sem(n + str(s)) for s in range(2)] for n in ("u_in", "pair_in"))
        PAIR_LOADS = 16 * 5
        uh, ul, vh, vl = sem("uh"), sem("ul"), sem("vh"), sem("vl")
        act_done, gelu_done, g_mul, gh_done, gl_done = (sem(n) for n in ("act_done", "gelu_done", "g_mul", "gh_done", "gl_done"))
        y_done, y_free, y_zero = sem("y_done"), [sem("y_free%d" % k) for k in range(4)], sem("y_zero")
        Y_N = 2 * TT

        with nc.Block() as block:
            @block.gpsimd
            def _(pool):
                nc.gpsimd.memset(y_sb, 0.0).then_inc(y_zero, 1)

            @block.sync
            def _(sp):
                def load_u(p, b):
                    sp.dma_start(w_raw[:, b], u_late[ds(p, 1)].rearrange("o p (c k) -> p (o c) k", c=DC)).then_inc(u_in[b], 16)

                def load_pair(p, b):
                    for s in (EARLY_LOT, LATE):
                        j = p * 2 + s
                        sp.dma_start(v_raw[:, b, s], v_t[ds(j, 1)].rearrange("o p n -> p (o n)")).then_inc(pair_in[b], 16)
                        sp.dma_start(c_lot[:, b, s].rearrange("p (b t) -> p b t", b=NB),
                                     c_dram[:, :, ds(j * TB, TB)].rearrange("b p t -> p b t")).then_inc(pair_in[b], 16)
                    sp.dma_start(gl_early[:, b], gl_dram[ds(p, 1)].rearrange("o p t -> p (o t)")).then_inc(pair_in[b], 16)

                def step(p, b, with_u=True):
                    sp.wait_ge(gl_done, p * 2 + 2)
                    sp.wait_ge(vl, p * 2 + 2)
                    load_pair(p + 2, b)
                    if with_u:
                        sp.wait_ge(ul, p + 2)
                        load_u(p + 3, 1 - b)
                load_u(0, 0)
                load_u(1, 1)
                load_pair(0, 0)
                sp.wait_ge(ul, 1)
                load_u(2, 0)
                load_pair(1, 1)
                with sp.Fori(0, PAIRS // 2 - 2) as it:
                    for b in range(2):
                        step(it * 2 + b, b)
                step(PAIRS - 4, 0)
                step(PAIRS - 3, 1, False)

            @block.tensor
            def _(pe):
                def late(p, b):
                    pe.wait_ge(ul, p + 1)
                    pe.wait_ge(gelu_done, p + 1)
                    for t in range(2):
                        for d in range(DC):
                            for i, (wh, ah) in enumerate(((0, 0), (0, 1), (1, 0))):
                                m = nc.tensor.matmul(psum[:, 2 * b + t, 0:HALF], w_split[:, b, wh, d, :],
                                                     acts_a[:, ah, d, t * HALF:(t + 1) * HALF],
                                                     start=(d == 0 and i == 0), stop=(d == DC - 1 and i == 2))
                    m.then_inc(act_done, 1)

                def y_pair(p, b):
                    pe.wait_ge(gl_done, p * 2 + 2)
                    pe.wait_ge(vl, p * 2 + 2)
                    for n in range(Y_N):
                        t, c = n // 2, n % 2
                        pe.wait_ge(y_free[n % 4], p * (Y_N // 4) + (n // 4 + 1))
                        k = 0
                        for j in range(2):
                            for gh, vh_ in ((0, 0), (0, 1), (1, 0)):
                                m = nc.tensor.matmul(psum[:, 4 + n % 4, :], g_split[:, b, j, gh, t * P:(t + 1) * P],
                                                     v_split[:, b, j, vh_, c * 512:(c + 1) * 512],
                                                     start=(k == 0), stop=(k == 5))
                                k += 1
                        m.then_inc(y_done, 1)
                late(0, 0)
                with pe.Fori(0, PAIRS // 2 - 1) as it:
                    for b in range(2):
                        late(it * 2 + (b + 1), 1 - b)
                        y_pair(it * 2 + b, b)
                late(PAIRS - 1, 1)
                y_pair(PAIRS - 2, 0)
                y_pair(PAIRS - 1, 1)

            @block.scalar
            def _(act):
                def u_hi(p, b, h, first=False):
                    act.wait_ge(u_in[b], h * 16 + 16)
                    if not first:
                        act.wait_ge(act_done, p - 1)
                    nc.scalar.activation(w_split[:, b, 0], w_raw[:, b], ACT.Copy).then_inc(uh, 1)

                def heads(p, b, h):
                    act.wait_ge(pair_in[b], h * PAIR_LOADS + PAIR_LOADS)
                    act.wait_ge(y_done, p * Y_N + 1)
                    for s in range(2):
                        nc.scalar.activation(v_split[:, b, s, 0], v_raw[:, b, s], ACT.Copy).then_inc(vh, 1)
                    act.wait_ge(g_mul, p * 2 + 1)
                    nc.scalar.activation(g_split[:, b, EARLY_LOT, 0], gl_early[:, b], ACT.Copy).then_inc(gh_done, 1)

                def gelu_late(p, b, first=False):
                    act.wait_ge(act_done, p + 1)
                    if not first:
                        act.wait_ge(gl_done, p * 2)
                    nc.scalar.activation(two(gl_late), psum[:, 2 * b:2 * b + 2, 0:HALF], ACT.Gelu).then_inc(gelu_done, 1)
                    act.wait_ge(g_mul, p * 2 + 2)
                    nc.scalar.activation(g_split[:, b, LATE, 0], gl_late, ACT.Copy).then_inc(gh_done, 1)
                act.sem_inc(gelu_done, 2)
                act.sem_inc(y_done, Y_N + 1)
                u_hi(0, 0, 0, True)
                u_hi(1, 1, 0, True)
                heads(0, 0, 0)
                gelu_late(0, 0, True)
                with act.Fori(0, PAIRS // 2 - 1) as it:
                    for b in range(2):
                        heads(it * 2 + (b + 1), 1 - b, it + b)
                        u_hi(it * 2 + (b + 2), b, it + 1)
                        gelu_late(it * 2 + (b + 1), 1 - b)
                heads(PAIRS - 1, 1, PAIRS // 2 - 1)
                gelu_late(PAIRS - 1, 1)

            @block.vector
            def _(dve):
                def u_lo(p, b):
                    dve.wait_ge(uh, p + 1)
                    nc.vector.tensor_tensor(w_split[:, b, 1], w_raw[:, b], w_split[:, b, 0].bitcast(F32), ALU.subtract
                                            ).then_inc(ul, 1)

                def g_lo(p, b, lot, gl, count):
                    dve.wait_ge(gh_done, p * 2 + count)
                    nc.vector.tensor_tensor(g_split[:, b, lot, 1], gl, g_split[:, b, lot, 0].bitcast(F32), ALU.subtract
                                            ).then_inc(gl_done, 1)

                def rests(p, b, h):
                    dve.wait_ge(pair_in[b], h * PAIR_LOADS + PAIR_LOADS)
                    nc.vector.tensor_tensor(gl_early[:, b], gl_early[:, b], c_lot[:, b, EARLY_LOT], ALU.mult).then_inc(g_mul, 1)
                    for s in range(2):
                        dve.wait_ge(vh, p * 2 + (s + 1))
                        nc.vector.tensor_tensor(v_split[:, b, s, 1], v_raw[:, b, s], v_split[:, b, s, 0].bitcast(F32),
                                                ALU.subtract).then_inc(vl, 1)
                    g_lo(p, b, EARLY_LOT, gl_early[:, b], 1)

                def times_gates(p, b):
                    dve.wait_ge(gelu_done, p + 3)
                    nc.vector.tensor_tensor(gl_late, gl_late, c_lot[:, b, LATE], ALU.mult).then_inc(g_mul, 1)

                def adds(p, n0, n1):
                    for n in range(n0, n1):
                        t, c = n // 2, n % 2
                        dve.wait_ge(y_done, p * Y_N + (n + Y_N + 2))
                        dve.wait_ge(y_free[n % 4], p * (Y_N // 4) + (n // 4 + 1))
                        y = y_sb[:, t, c * 512:(c + 1) * 512]
                        nc.vector.tensor_tensor(y, y, psum[:, 4 + n % 4, :], ALU.add).then_inc(y_free[n % 4], 1)
                for k in range(4):
                    dve.sem_inc(y_free[k], 1)
                dve.wait_ge(y_zero, 1)
                u_lo(0, 0)
                u_lo(1, 1)
                rests(0, 0, 0)
                times_gates(0, 0)
                g_lo(0, 0, LATE, gl_late, 2)

                def step(p, b, h, last=False):
                    rests(p + 1, 1 - b, h)
                    if not last:
                        u_lo(p + 2, b)
                    times_gates(p + 1, 1 - b)
                    adds(p, 0, 2)
                    g_lo(p + 1, 1 - b, LATE, gl_late, 2)
                    adds(p, 2, Y_N)
                with dve.Fori(0, PAIRS // 2 - 1) as it:
                    for b in range(2):
                        step(it * 2 + b, b, it + b)
                step(PAIRS - 2, 0, PAIRS // 2 - 1, True)
                adds(PAIRS - 1, 0, Y_N)

        A = Arena()
        y_in = A.take(TT, D)
        x2 = A.take(DC, T)
        d_x2, yt_done, yt_free = sem("d_x2"), sem("yt_done"), sem("yt_free")
        with nc.Block() as block:
            @block.sync
            def _(sp):
                sp.dma_start(arena[:, TT * D:TT * D + DC * T], x1_dram).then_inc(d_x2, 16)

            @block.tensor
            def _(pe):
                for d in range(DC):
                    if d >= 2:
                        pe.wait_ge(yt_free, d - 1)
                    for t in range(TT):
                        b = 2 * (d % 2) + t // 4
                        m = nc.tensor.transpose(psum[:, b, t % 4 * P:t % 4 * P + P], y_in[:, t, d * P:(d + 1) * P], ident)
                    m.then_inc(yt_done, 1)

            @block.vector
            def _(dve):
                dve.wait_ge(d_x2, 16)
                for d in range(DC):
                    dve.wait_ge(yt_done, d + 1)
                    for g, (t0, t1) in enumerate(GROUPS):
                        x = x2[:, d, t0:t1]
                        m = nc.vector.scalar_tensor_tensor(out=x, in0=psum[:, 2 * (d % 2) + g, 0:t1 - t0],
                                                           scalar=modcol(GATE2, d, g), in1=x, op0=ALU.mult, op1=ALU.add)
                    m.then_inc(yt_free, 1)
        n3 = Norm("n3", x2, lambda d, g: vec[:, V_GF + d:V_GF + d + 1], None, None, norm_work(A))
        out_stored = sem("out_stored")
        with nc.Block() as block:
            @block.sync
            def _(sp):
                for d in range(DC):
                    sp.wait_ge(n3.n_hf, 2 * d + 2)
                    sp.dma_start(out[:, d * T:(d + 1) * T], x2[:, d]).then_inc(out_stored, 16)
                sp.wait_ge(out_stored, 16 * DC)

            @block.scalar
            def _(act):
                n3.stats_act(act)

            @block.tensor
            def _(pe):
                n3.stats_pe(pe)

            @block.vector
            def _(dve):
                n3.stats_dve(dve)
                n3.apply_dve(dve)
        room.take()


def _constants():
    c = np.zeros((P, C_N), np.float32)
    row, col = np.arange(P)[:, None], np.arange(P)[None, :]
    c[:, C_ID:C_ID + P] = row == col
    c[:, C_ONE:C_ONE + P] = 1.0
    c[:, C_IOTA:C_IOTA + P] = col
    c[:, C_SLOPE:C_SLOPE + HEADS] = np.exp2(-8.0 * np.arange(1, HEADS + 1) / HEADS)
    for l in range(LEVELS):
        m = (((row ^ col) >> l) == 1).astype(np.uint32)
        c[:, C_MASK + l * P:C_MASK + (l + 1) * P] = m.view(np.float32)
    d = np.abs(row - np.arange(3 * P)[None, :] + P)
    c[:, C_DIST:C_DIST + 3 * P] = np.where(d <= P, -d, -1e30)
    return c


def _columns(v):
    return np.reshape(v, (-1, P)).T


def _units(w):
    k, n = w.shape
    return w.reshape(DC, P, n // P, P).transpose(2, 1, 0, 3).reshape(n // P, P, D)


def arrays_of(i):
    i = {k: np.asarray(v) for k, v in i.items()}
    x = np.concatenate([i["x_prompt"][0], i["x_sample"][0]], 0)
    x_t = x.T.reshape(DC, P, T).transpose(1, 0, 2)
    c = np.stack([_columns(i["c_prompt"][0]), _columns(i["c_sample"][0])], -1).reshape(P, 16)
    vecs = np.concatenate(
        [_columns(i["b_mod"][0]), _columns(i["g_norm1"][0]), _columns(i["g_norm2"][0]), _columns(i["g_final"]),
         _columns(i["g_hnorm"][0]), _columns(i["p_lb_fwd"][0]), _columns(i["p_lb_fwd"][1]),
         _columns(i["p_lb_bwd"][0]), _columns(i["p_lb_bwd"][1]), c,
         np.broadcast_to(i["att_sink"][0][None, :], (P, HEADS))], 1)
    w = i["w_in"][0]
    qa, kv = _units(w[:, 0:D]), w[:, D:D + 512]
    n0 = D + 512
    qh, zf, zb, ih, gh, ga, gb = (_units(w[:, n0 + k * D:n0 + (k + 1) * D]) for k in range(7))
    order = []
    for g in range(KV_HEADS):
        pair = np.concatenate([kv[:, g * HD:(g + 1) * HD], kv[:, 256 + g * HD:256 + (g + 1) * HD]], 1)
        order += [_units(pair)[0], qa[2 * g], qa[2 * g + 1]]
    order += list(ga) + list(_units(i["w_o_att"][0]))
    for h in range(H_HEADS):
        order += [zf[h], zb[h], qh[h], gh[h], ih[h]]
    order += list(gb) + list(_units(i["w_o_hgrn"][0])) + list(_units(i["w_out"][0])) + list(_units(i["w_pq"][0]))
    order += [order[k] for k in range(LEAD)]
    keys_t = i["peer_keys"][0].reshape(2 * PH, NKEYS, P).transpose(2, 0, 1).reshape(P, 2 * PH * NKEYS)
    u_t = i["peer_u"][0].reshape(NKEYS, NKEYS, DC, P).transpose(1, 3, 2, 0).reshape(NKEYS, P, D)
    u_early = np.concatenate([u_t[1::2], u_t[1:1 + 2 * EARLY_LEAD:2]], 0)
    v_t = i["peer_v"][0].reshape(NKEYS, NKEYS, D).transpose(1, 0, 2)
    return {"x_t": x_t.reshape(P, DC * T), "vecs": vecs, "consts": _constants(), "w_mod": _units(i["w_mod"][0]),
            "w_str": np.stack(order), "keys_t": keys_t, "u_late": u_t[0::2],
            "u_early": u_early, "v_t": v_t}


def kernel(**inputs):
    import concourse.bacc as _bacc
    from concourse.bass_utils import run_bass_kernel_spmd as _run

    nc = _bacc.Bacc("TRN2", target_bir_lowering=False, num_devices=1)
    arrays = {k: np.ascontiguousarray(v) for k, v in arrays_of(inputs).items()}
    args = [nc.dram_tensor(k, v.shape, F32, kind="ExternalInput").ap() for k, v in arrays.items()]
    out = nc.dram_tensor("y_t", (P, DC * T), F32, kind="ExternalOutput").ap()
    encoder_kernel(nc, *args, out)
    y = _run(nc, [arrays], core_ids=[0]).results[0]["y_t"]
    y = np.asarray(y).reshape(P, DC, T).transpose(2, 1, 0).reshape(T, D)
    return y[None, 0:T_PROMPT], y[None, T_PROMPT:T]
```

```python
from contextlib import ExitStack

import concourse.bass as bass
import numpy as np
from concourse import mybir

F32 = mybir.dt.float32
F32R = mybir.dt.float32r
U32 = mybir.dt.uint32
ALU = mybir.AluOpType
ACT = mybir.ActivationFunctionType
AX_X = mybir.AxisListType.X
ds = bass.ds

P = 128
D = 1024
DC = D // P
T_PROMPT, T_SAMPLE = 512, 256
T = T_PROMPT + T_SAMPLE
TT = T // P
HALF = T // 2
GROUPS = ((0, T_PROMPT), (T_PROMPT, T))
EPS = 1e-6
KV_HEADS, Q_PER_KV, HD = 4, 4, 64
HEADS = KV_HEADS * Q_PER_KV
H_HEADS = 8
LEVELS = 7
PH, NKEYS, TOPK = 8, 128, 16
EXPERTS = NKEYS * NKEYS
ROW_LEN = [TOPK // (a + 1) for a in range(TOPK)]
CAND = sum(ROW_LEN)

N_ATT = KV_HEADS * 3
N_GATT = 2 * DC
N_HG = H_HEADS * 5
N_GHG = 2 * DC
N_OUT = DC
N_PQ = 2 * PH
U_ATT = 0
U_GATT = U_ATT + N_ATT
U_HG = U_GATT + N_GATT
U_GHG = U_HG + N_HG
U_OUT = U_GHG + N_GHG
U_PQ = U_OUT + N_OUT
UNITS = U_PQ + N_PQ
GATES_AHEAD = 4
LEAD = 4
EARLY = EXPERTS // P // 2
EARLY_PQ = 5
EARLY_LEAD = 2
N_MOD = 6 * DC
MOD_LOT = 4

V_BMOD, V_G1, V_G2, V_GF, V_GH = 0, 48, 56, 64, 72
V_LB = 80
V_C = 112
V_SINK = 128
V_N = V_SINK + HEADS
C_ID, C_ONE, C_IOTA, C_SLOPE, C_MASK = 0, 128, 256, 384, 400
C_DIST = C_MASK + LEVELS * P
C_N = C_DIST + 3 * P
C_KEEP = C_MASK

BLOCKS = []
for g0, g1 in ((0, T_PROMPT // P), (T_PROMPT // P, TT)):
    for q in range(g0, g1):
        k0, k1 = max(g0, q - 1), min(g1 - 1, q + 1)
        BLOCKS.append((q, k0, k1 - k0 + 1, (k0 - q + 1) * P))
B_OFF = [P * sum(b[2] for b in BLOCKS[:i]) for i in range(TT + 1)]
N_KT = sum(b[2] for b in BLOCKS)


def encoder_kernel(nc, x_t, vecs, consts, w_mod, w_str, keys_t, u_late, u_early, v_t, out):
    with ExitStack() as ctx:
        def sb(name, shape, dt=F32):
            return ctx.enter_context(nc.sbuf_tensor(name, shape, dt))

        def sem(name):
            return ctx.enter_context(nc.semaphore(name))

        acts_a = sb("acts_a", [P, 2, DC, T], F32R)
        w_split = sb("w_split", [P, 2, 2, DC, P], F32R)
        w_raw = sb("w_raw", [P, 2, DC, P])
        cst = sb("cst", [P, C_KEEP])
        vec = sb("vec", [P, V_N])
        mod = sb("mod", [P, 6 * DC, 2])
        lb = sb("lb", [P, 2, 2, H_HEADS])
        ARENA = 19200
        arena = sb("arena", [P, ARENA])
        psum = ctx.enter_context(nc.psum_tensor("psum", [P, 8, 512], F32))

        class Room:
            def __init__(self):
                self.stack = ExitStack()

            def take(self, *tensors):
                self.stack.close()
                return [self.stack.enter_context(nc.sbuf_tensor(*t))[:] for t in tensors]
        room = Room()
        ctx.callback(room.take)
        m_dram = nc.dram_tensor("m_scratch", (DC, P, T), F32, kind="Internal").ap()
        x1_dram = nc.dram_tensor("x1_scratch", (P, DC * T), F32, kind="Internal").ap()

        class Arena:
            def __init__(self):
                self.at = 0

            def take(self, *shape):
                n = int(np.prod(shape))
                ap = arena[:, self.at:self.at + n]
                self.at += n
                assert self.at <= ARENA, self.at
                if len(shape) == 2:
                    ap = ap.rearrange("p (a b) -> p a b", a=shape[0])
                elif len(shape) == 3:
                    ap = ap.rearrange("p (a b c) -> p a b c", a=shape[0], b=shape[1])
                return ap

        ident, ones = cst[:, C_ID:C_ID + P], cst[:, C_ONE:C_ONE + P]
        iota = cst[:, C_IOTA:C_IOTA + P]

        def modcol(which, d, g):
            return mod[:, which * DC + d, g:g + 1]
        SHIFT1, SCALE1, GATE1, SHIFT2, SCALE2, GATE2 = range(6)

        raw_ready = [sem("raw_ready0"), sem("raw_ready1")]
        hi_ready, lo_ready = sem("hi_ready"), sem("lo_ready")
        w_used = sem("w_used")
        proj_free = [sem("proj_free0"), sem("proj_free1")]

        def load_unit(sp, n, s):
            sp.dma_start(w_raw[:, s], w_str[ds(n, 1)].rearrange("o p (c k) -> p (o c) k", c=DC)
                         ).then_inc(raw_ready[s], 16)

        def load_ahead(sp, n, u):
            sp.wait_ge(lo_ready, n + 3)
            load_unit(sp, n + LEAD, u % 2)

        def split_lo(dve, n, u):
            dve.wait_ge(hi_ready, n + 3)
            nc.vector.tensor_tensor(w_split[:, u % 2, 1], w_raw[:, u % 2],
                                    w_split[:, u % 2, 0].bitcast(F32), ALU.subtract).then_inc(lo_ready, 1)

        class Unit:
            def __init__(self, base, it=None, per=0):
                assert base % 2 == 0 and per % 2 == 0
                self.base, self.it, self.per = base, it, per

            def at(self, u):
                return self.base + u if self.it is None else self.it * self.per + (self.base + u)

            def half(self, u):
                h = (self.base + u) // 2
                return h if self.it is None else self.it * (self.per // 2) + h

        def do_load(sp, U, u):
            load_ahead(sp, U.at(u), u)

        def do_hi(act, U, u):
            act.wait_ge(raw_ready[u % 2], U.half(u) * 16 + 32)
            act.wait_ge(w_used, U.at(u) + 1)
            nc.scalar.activation(w_split[:, u % 2, 0], w_raw[:, u % 2], ACT.Copy).then_inc(hi_ready, 1)

        def do_lo(dve, U, u):
            split_lo(dve, U.at(u), u)

        def project(pe, U, u, a, tokens_out=False, halves=(0, 1)):
            s = u % 2
            if 0 in halves:
                pe.wait_ge(lo_ready, U.at(u) + 1)
                pe.wait_ge(proj_free[s], U.half(u) + 1)
            passes = ((0, 0), (0, 1), (1, 0))
            n_half = TT // 2 if tokens_out else 1
            for t in range(halves[0] * n_half, (halves[-1] + 1) * n_half):
                for d in range(DC):
                    for i, (wh, ah) in enumerate(passes):
                        if tokens_out:
                            o = psum[:, 2 * s + t // 3, t % 3 * P:t % 3 * P + P]
                            l, r = a[:, ah, d, t * P:(t + 1) * P], w_split[:, s, wh, d, :]
                        else:
                            o = psum[:, 2 * s + t, 0:HALF]
                            l, r = w_split[:, s, wh, d, :], a[:, ah, d, t * HALF:(t + 1) * HALF]
                        last = nc.tensor.matmul(o, l, r, start=(d == 0 and i == 0),
                                                stop=(d == DC - 1 and i == 2))
            if 1 in halves:
                last.then_inc(w_used, 1)

        def proj_out(u, parts=slice(0, P)):
            return psum[parts, 2 * (u % 2):2 * (u % 2) + 2, 0:HALF]

        def two(ap):
            return ap.rearrange("p (a b) -> p a b", a=2)

        class Norm:
            def __init__(self, name, x, scale_of, shift_of, dest, work):
                self.x, self.scale_of, self.shift_of, self.dest = x, scale_of, shift_of, dest
                self.sq, self.r, self.hx, self.hf = work
                (self.n_sq, self.n_ps, self.n_r, self.n_root, self.n_hx, self.n_hf, self.n_hi, self.n_lo) = (
                    sem(name + k) for k in ("_sq", "_ps", "_r", "_root", "_hx", "_hf", "_hi", "_lo"))

            def square(self, act, d, at=None):
                n = d if at is None else at
                if at is not None or d >= 2:
                    act.wait_ge(self.n_ps, n - 1)
                x = self.x[:, d] if at is None else self.x[:, ds(at, 1)].rearrange("p o t -> p (o t)")
                nc.scalar.activation(self.sq[:, d % 2], x, ACT.Square).then_inc(self.n_sq, 1)

            def sums(self, pe, d, at=None):
                pe.wait_ge(self.n_sq, (d if at is None else at) + 1)
                for t in range(2):
                    m = nc.tensor.matmul(psum[:, 4 + t, 0:HALF], ones, self.sq[:, d % 2, t * HALF:(t + 1) * HALF],
                                         start=(d == 0), stop=(d == DC - 1))
                m.then_inc(self.n_ps, 1)

            def root(self, act):
                act.wait_ge(self.n_r, 1)
                nc.scalar.activation(self.r, self.r, ACT.Sqrt).then_inc(self.n_root, 1)

            def stats_dve(self, dve):
                dve.wait_ge(self.n_ps, DC)
                nc.vector.tensor_scalar(two(self.r), psum[:, 4:6, 0:HALF], 1.0 / D, EPS, ALU.mult, ALU.add
                                        ).then_inc(self.n_r, 1)
                dve.wait_ge(self.n_root, 1)
                nc.vector.reciprocal(self.r, self.r).then_inc(self.n_r, 1)

            def apply_act(self, act, d):
                act.wait_ge(self.n_hf, 2 * d + 2)
                nc.scalar.activation(self.dest[:, 0, d], self.hf[:, d % 2], ACT.Copy).then_inc(self.n_hi, 1)

            def apply_dve(self, dve):
                hf, hx, dest, n_hx, n_hf = self.hf, self.hx, self.dest, self.n_hx, self.n_hf

                def rest(d):
                    dve.wait_ge(self.n_hi, d + 1)
                    nc.vector.tensor_tensor(dest[:, 1, d], hf[:, d % 2], dest[:, 0, d].bitcast(F32), ALU.subtract
                                            ).then_inc(self.n_lo, 1)
                dve.wait_ge(self.n_r, 2)
                for d in range(DC):
                    if d >= 2:
                        dve.wait_ge(n_hf, 2 * d - 2)
                    nc.vector.tensor_tensor(hx[:, d % 2], self.x[:, d], self.r, ALU.mult).then_inc(n_hx, 1)
                    if dest is not None and d >= 2:
                        rest(d - 2)
                        dve.wait_ge(self.n_lo, d - 1)
                    dve.wait_ge(n_hx, d + 1)
                    for g, (t0, t1) in enumerate(GROUPS):
                        o = self.x[:, d, t0:t1] if dest is None else hf[:, d % 2, t0:t1]
                        if self.shift_of is None:
                            m = nc.vector.tensor_scalar(o, hx[:, d % 2, t0:t1], self.scale_of(d, g), None, ALU.mult)
                        else:
                            m = nc.vector.tensor_scalar(o, hx[:, d % 2, t0:t1], self.scale_of(d, g), self.shift_of(d, g),
                                                        ALU.mult, ALU.add)
                        m.then_inc(n_hf, 1)
                if dest is not None:
                    for d in range(DC - 2, DC):
                        rest(d)

        def norm_work(A):
            return A.take(2, T), A.take(T), A.take(2, T), A.take(2, T)

        A = Arena()
        MOD_SLOTS = 4
        ROW_BANKS = (1, 2, 3, 6)
        wm = A.take(MOD_SLOTS * MOD_LOT, D).rearrange("p (s u) k -> p s u k", s=MOD_SLOTS)
        rows = A.take(MOD_SLOTS, MOD_LOT * P)
        cs, cg = A.take(16), A.take(16)
        lbt = A.take(4, 8)
        x_sb, spare = room.take(("x_sb", [P, DC, T], F32), ("n1_work", [P, 7, T], F32))
        n1 = Norm("n1", x_sb, lambda d, g: modcol(SCALE1, d, g), lambda d, g: modcol(SHIFT1, d, g), acts_a,
                  (spare[:, 0:2], spare[:, 2], spare[:, 3:5], spare[:, 5:7]))
        LOTS_1, LOTS_ALL = 2 * DC // MOD_LOT, N_MOD // MOD_LOT
        d_vec, d_x, d_cst, d_wm = sem("d_vec"), sem("d_x"), sem("d_cst"), [sem("d_wm%d" % k) for k in range(MOD_SLOTS)]
        mod_a, mod_v, mod_used, mod_done = sem("mod_a"), sem("mod_v"), sem("mod_used"), sem("mod_done")
        row_ready, row_turned = sem("row_ready"), sem("row_turned")

        def load_mod(eng, lot):
            if lot >= MOD_SLOTS:
                eng.wait_ge(mod_used, lot - MOD_SLOTS + 1)
            eng.dma_start(wm[:, lot % MOD_SLOTS], w_mod[lot * MOD_LOT:(lot + 1) * MOD_LOT]
                          .rearrange("u p k -> p u k")).then_inc(d_wm[lot % MOD_SLOTS], 16)

        def mod_products(pe, lots):
            for lot in lots:
                pe.wait_ge(d_wm[lot % MOD_SLOTS], 16 * (lot // MOD_SLOTS + 1))
                if lot >= MOD_SLOTS:
                    pe.wait_ge(row_ready, lot - MOD_SLOTS + 1)
                for d in range(DC):
                    last = nc.tensor.matmul(psum[0:2, ROW_BANKS[lot % MOD_SLOTS], :], cs[:, 2 * d:2 * d + 2],
                                            wm[:, lot % MOD_SLOTS, :, d * P:(d + 1) * P],
                                            start=(d == 0), stop=(d == DC - 1))
                last.then_inc(mod_used, 1)

        def mod_rows(act, lots):
            for lot in lots:
                act.wait_ge(mod_used, lot + 1)
                if lot >= MOD_SLOTS:
                    act.wait_ge(row_turned, lot - MOD_SLOTS + 1)
                nc.scalar.activation(rows[0:2, lot % MOD_SLOTS], psum[0:2, ROW_BANKS[lot % MOD_SLOTS], :], ACT.Copy
                                     ).then_inc(row_ready, 1)

        def mod_turn(pe, lots):
            for lot in lots:
                pe.wait_ge(row_ready, lot + 1)
                for k in range(MOD_LOT):
                    n = lot * MOD_LOT + k
                    last = nc.tensor.matmul(psum[:, 0, 2 * n:2 * n + 2], rows[0:2, lot % MOD_SLOTS, k * P:(k + 1) * P],
                                            ident[0:2, 0:2], start=True, stop=True)
                last.then_inc(row_turned, 1)

        def mod_out(dve, lots, scale_which, v, count):
            dve.wait_ge(row_turned, lots[-1] + 1)
            n0, n1_ = lots[0] * MOD_LOT, (lots[-1] + 1) * MOD_LOT
            for g in range(2):
                m = nc.vector.tensor_tensor(mod[:, n0:n1_, g],
                                            psum[:, 0, 0:2 * N_MOD].rearrange("p (n g) -> p n g", g=2)[:, n0:n1_, g],
                                            vec[:, V_BMOD + n0:V_BMOD + n1_], ALU.add)
            m.then_inc(mod_v, 1)
            dve.wait_ge(mod_v, count + 1)
            for g in range(2):
                col = mod[:, scale_which * DC:(scale_which + 1) * DC, g]
                nc.vector.scalar_tensor_tensor(out=col, in0=col, scalar=1.0, in1=vec[:, v:v + DC],
                                               op0=ALU.add, op1=ALU.mult).then_inc(mod_done, 1)

        with nc.Block() as block:
            @block.sync
            def _(sp):
                sp.dma_start(vec[:], vecs).then_inc(d_vec, 16)
                load_mod(sp, 0)
                sp.dma_start(cst[:], consts[:, 0:C_KEEP]).then_inc(d_cst, 16)
                load_mod(sp, 1)
                sp.dma_start(x_sb, x_t.rearrange("p (a b) -> p a b", a=DC)).then_inc(d_x, 16)
                for lot in range(2, MOD_SLOTS):
                    load_mod(sp, lot)
                for n in range(2):
                    load_unit(sp, n, n)
                for lot in range(MOD_SLOTS, LOTS_1 + MOD_SLOTS):
                    load_mod(sp, lot)

            @block.scalar
            def _(act):
                act.wait_ge(d_vec, 16)
                nc.scalar.activation(cg, vec[:, V_C:V_C + 16], ACT.Sigmoid).then_inc(mod_a, 1)
                act.wait_ge(mod_v, 2)
                nc.scalar.activation(lbt, lbt, ACT.Exp).then_inc(mod_a, 1)
                act.wait_ge(d_x, 16)
                for d in range(DC):
                    n1.square(act, d)
                n1.root(act)
                mod_rows(act, range(LOTS_1))

            @block.vector
            def _(dve):
                p_lb = vec[:, V_LB:V_LB + 32].rearrange("p (d l h) -> p d l h", d=2, l=2)
                e_lb = lbt.rearrange("p (d l) h -> p d l h", d=2)
                dve.wait_ge(d_vec, 16)
                nc.vector.tensor_tensor(lb[:, 0], p_lb[:, :, 0], p_lb[:, :, 1], ALU.max).then_inc(mod_v, 1)
                dve.wait_ge(mod_v, 1)
                for l in range(2):
                    m = nc.vector.tensor_tensor(e_lb[:, :, l], p_lb[:, :, l], lb[:, 0], ALU.subtract)
                m.then_inc(mod_v, 1)
                dve.wait_ge(mod_a, 1)
                nc.vector.tensor_tensor(cs, cg, vec[:, V_C:V_C + 16], ALU.mult).then_inc(mod_v, 1)
                dve.wait_ge(mod_a, 2)
                nc.vector.tensor_tensor(lb[:, 1], e_lb[:, :, 0], e_lb[:, :, 1], ALU.add).then_inc(mod_v, 1)
                dve.wait_ge(mod_v, 4)
                nc.vector.reciprocal(lb[:, 1], lb[:, 1]).then_inc(mod_v, 1)
                dve.wait_ge(mod_v, 5)
                nc.vector.tensor_tensor(lb[:, 0], e_lb[:, :, 0], lb[:, 1], ALU.mult).then_inc(mod_v, 1)
                dve.wait_ge(mod_v, 6)
                nc.vector.tensor_scalar(lb[:, 1], lb[:, 0], -1.0, 1.0, ALU.mult, ALU.add).then_inc(mod_v, 1)
                n1.stats_dve(dve)
                mod_out(dve, range(LOTS_1), SCALE1, V_G1, 7)

            @block.tensor
            def _(pe):
                pe.wait_ge(mod_v, 3)
                pe.wait_ge(d_cst, 16)
                mod_products(pe, range(LOTS_1 // 2))
                for d in range(DC):
                    n1.sums(pe, d)
                mod_products(pe, range(LOTS_1 // 2, LOTS_1))
                mod_turn(pe, range(LOTS_1))

        with nc.Block() as block:
            @block.sync
            def _(sp):
                for lot in range(LOTS_1 + MOD_SLOTS, LOTS_ALL):
                    load_mod(sp, lot)
                for n in range(2, 4):
                    sp.wait_ge(lo_ready, n - 1)
                    load_unit(sp, n, n % 2)

            @block.tensor
            def _(pe):
                for lot in range(LOTS_1, LOTS_ALL):
                    mod_products(pe, (lot,))
                    if lot > LOTS_1:
                        mod_turn(pe, (lot - 1,))
                mod_turn(pe, (LOTS_ALL - 1,))

            @block.scalar
            def _(act):
                for s in range(2):
                    act.wait_ge(raw_ready[s], 16)
                    nc.scalar.activation(w_split[:, s, 0], w_raw[:, s], ACT.Copy).then_inc(hi_ready, 1)
                for d in range(DC):
                    n1.apply_act(act, d)
                    if d in (3, 5, 7):
                        mod_rows(act, (LOTS_1 + (d - 3) // 2,))
                mod_rows(act, range(LOTS_1 + 3, LOTS_ALL))

            @block.vector
            def _(dve):
                for s in range(2):
                    dve.wait_ge(hi_ready, s + 1)
                    nc.vector.tensor_tensor(w_split[:, s, 1], w_raw[:, s], w_split[:, s, 0].bitcast(F32),
                                            ALU.subtract).then_inc(lo_ready, 1)
                for s in range(2):
                    dve.sem_inc(proj_free[s], 1)
                dve.wait_ge(mod_done, 2)
                n1.apply_dve(dve)
                mod_out(dve, range(LOTS_1, LOTS_ALL), SCALE2, V_G2, 8)


        acts_b, hg_more = room.take(("acts_b", [P, 2, DC, T], F32R),
                                    ("hg_more", [P, 3, T], F32))
        A = Arena()
        dist = A.take(3 * P)
        kT, vT, qT = A.take(2, T), A.take(T), A.take(2, T)
        vN = A.take(2, TT, HD)
        sc = A.take(2, 2, N_KT * P)
        pT = A.take(2, N_KT, P)
        st = A.take(4, 6 * TT)
        d_dist = sem("d_dist")
        kv_ready, q_ready, v_ready = sem("kv_ready"), sem("q_ready"), sem("v_ready")
        score_ready, work_free = sem("score_ready"), [sem("work_free0"), sem("work_free1")]
        max_done, nmax_ready, sinkd_ready, exp_ready = sem("max_done"), sem("nmax_ready"), sem("sinkd_ready"), sem("exp_ready")
        den_step, prob_ready = sem("den_step"), sem("prob_ready")
        tr_ready, tr_taken, pv_ready, pv_hi = sem("tr_ready"), sem("tr_taken"), sem("pv_ready"), sem("pv_hi")
        TRIPS = KV_HEADS // 2
        PAIR_UNIT = (1, 2, 4, 5)
        SEQ_PE = """P0a P0b P1a P1b V0 S0 P2a S1 P2b T0 S2 v0 P3a T1 S3 v1 P3b T2 P4a V1 P4b v2 S4 P5a T3
                    S5 v3 P5b T4 S6 v4 T5 S7 v5 T6 v6 T7 v7""".split()
        SEQ_ACT = """C0 W0 C1 W1 V0 E0 E1 C2 T0 W2 v0 E2 T1 v1 E3 T2 C3 W3 V1 C4 v2 W4 E4 T3 v3 E5 C5 T4 W5
                     v4 E6 T5 v5 E7 T6 v6 T7 v7""".split()
        SEQ_DVE = """D0 D1 S0 S1 F0 D2 S2 v0 F1 S3 v1 F2 D3 v2 S4 F3 D4 S5 v3 F4 D5 S6 v4 F5 S7 v5 F6 F7
                     v6 v7""".split()
        TR_GROUPS = [(a, min(a + 4, N_KT)) for a in range(0, N_KT, 4)]
        PV_PARTS = ((0, T_PROMPT), (T_PROMPT, T))
        uses = {}
        W_TRIP = TR_TRIP = 0
        for step in SEQ_PE:
            uses[step] = W_TRIP if step[0] in "Sv" else TR_TRIP
            W_TRIP += {"S": TT, "v": len(PV_PARTS)}.get(step[0], 0)
            TR_TRIP += {"V": 1, "T": len(TR_GROUPS)}.get(step[0], 0)
        assert W_TRIP % 2 == 0 and TR_TRIP % 2 == 0

        def walk(seq):
            for step in seq:
                yield step, step[0], int(step[1]), uses.get(step)

        def stat(h, k):
            return st[:, h % 4, k * TT:(k + 1) * TT]

        def scores_of(h, a, b):
            return sc[:, h // 2 % 2, h % 2, a:b]

        with nc.Block() as block:
            @block.sync
            def _(sp):
                sp.dma_start(dist, consts[:, C_DIST:C_DIST + 3 * P]).then_inc(d_dist, 16)
                with sp.Fori(0, TRIPS) as it:
                    U = Unit(U_ATT, it, 6)
                    for u in range(6):
                        do_load(sp, U, u)

            @block.tensor
            def _(pe):
                with pe.Fori(0, TRIPS) as it:
                    U = Unit(U_ATT, it, 6)
                    for step, kind, h, n in walk(SEQ_PE):
                        kv, e, hd = h // 4, h % 2, slice(h % 2 * HD, (h % 2 + 1) * HD)
                        if kind == "P":
                            project(pe, U, h, acts_a, halves=("ab".index(step[2]),))
                        elif kind == "V":
                            pe.wait_ge(kv_ready, it * 2 + (h + 1))
                            pe.wait_ge(tr_taken, it * TR_TRIP + (n + 1))
                            for i in range(TT):
                                m = nc.tensor.matmul(psum[:, 6 + n % 2, i * HD:(i + 1) * HD], vT[:, i * P:(i + 1) * P],
                                                     ident[:, HD:P], start=True, stop=True)
                            m.then_inc(tr_ready, 1)
                        elif kind == "S":
                            pe.wait_ge(kv_ready, it * 2 + (kv + 1))
                            pe.wait_ge(q_ready, it * 4 + (h // 2 + 1))
                            for i, (q, k0, nk, _) in enumerate(BLOCKS):
                                pe.wait_ge(work_free[(n + i) % 2], it * (W_TRIP // 2) + ((n + i) // 2 + 1))
                                nc.tensor.matmul(psum[:, 4 + (n + i) % 2, 0:nk * P], qT[hd, h // 2 % 2, q * P:(q + 1) * P],
                                                 kT[hd, kv, k0 * P:(k0 + nk) * P], start=True, stop=True
                                                 ).then_inc(score_ready, 1)
                        elif kind == "T":
                            pe.wait_ge(prob_ready, it * 8 + (h + 1))
                            for j, (a, b) in enumerate(TR_GROUPS):
                                pe.wait_ge(tr_taken, it * TR_TRIP + (n + j + 1))
                                for c in range(a, b):
                                    m = nc.tensor.transpose(psum[:, 6 + (n + j) % 2, (c - a) * P:(c - a + 1) * P],
                                                            scores_of(h, c * P, (c + 1) * P), ident)
                                m.then_inc(tr_ready, 1)
                        else:
                            pe.wait_ge(v_ready, it * 2 + (kv + 1))
                            pe.wait_ge(tr_taken, it * TR_TRIP + (uses["T%d" % h] + len(TR_GROUPS) + 2))
                            for g, (t0, t1) in enumerate(PV_PARTS):
                                pe.wait_ge(work_free[(n + g) % 2], it * (W_TRIP // 2) + ((n + g) // 2 + 1))
                                for i, (q, k0, nk, _) in enumerate(BLOCKS):
                                    if not t0 <= q * P < t1:
                                        continue
                                    for j in range(nk):
                                        m = nc.tensor.matmul(
                                            psum[hd, 4 + (n + g) % 2, q * P - t0:(q + 1) * P - t0],
                                            vN[:, kv, k0 + j, :], pT[:, e, B_OFF[i] // P + j, :],
                                            start=(j == 0), stop=(j == nk - 1))
                                m.then_inc(pv_ready, 1)

            @block.scalar
            def _(act):
                act.sem_inc(tr_taken, 2)
                with act.Fori(0, TRIPS) as it:
                    U = Unit(U_ATT, it, 6)
                    for step, kind, h, n in walk(SEQ_ACT):
                        hd = slice(h % 2 * HD, (h % 2 + 1) * HD)
                        if kind == "C":
                            act.wait_ge(w_used, U.at(h) + 1)
                            if h in (0, 3):
                                kv = h // 3
                                nc.scalar.activation(two(kT[0:HD, kv]), proj_out(h, slice(0, HD)), ACT.Copy)
                                nc.scalar.activation(two(kT[HD:P, kv]), proj_out(h, slice(0, HD)), ACT.Copy)
                                nc.scalar.activation(two(vT), proj_out(h), ACT.Copy
                                                     ).then_inc(proj_free[h % 2], 1)
                                act.wait_ge(proj_free[h % 2], U.half(h) + 2)
                                act.sem_inc(kv_ready, 1)
                            else:
                                p = PAIR_UNIT.index(h)
                                nc.scalar.activation(two(qT[:, p % 2]), proj_out(h), ACT.Copy, scale=HD ** -0.5
                                                     ).then_inc(proj_free[h % 2], 1)
                                act.wait_ge(proj_free[h % 2], U.half(h) + 2)
                                act.sem_inc(q_ready, 1)
                        elif kind == "W":
                            do_hi(act, U, h)
                        elif kind == "V":
                            act.wait_ge(tr_ready, it * TR_TRIP + (n + 1))
                            nc.scalar.activation(vN[:, h].rearrange("p a b -> p (a b)"), psum[:, 6 + n % 2, 0:TT * HD],
                                                 ACT.Copy).then_inc(tr_taken, 1)
                            act.wait_ge(tr_taken, it * TR_TRIP + (n + 3))
                            act.sem_inc(v_ready, 1)
                        elif kind == "E":
                            act.wait_ge(sinkd_ready, it * 8 + (h + 1))
                            for i in range(TT):
                                s = scores_of(h, B_OFF[i], B_OFF[i + 1])
                                nc.scalar.activation(s, s, ACT.Exp, bias=stat(h, 1)[:, i:i + 1],
                                                     accum_out=stat(h, 3)[:, i:i + 1])
                            nc.scalar.activation(stat(h, 4), stat(h, 2), ACT.Exp).then_inc(exp_ready, 1)
                        elif kind == "T":
                            for j, (a, b) in enumerate(TR_GROUPS):
                                act.wait_ge(tr_ready, it * TR_TRIP + (n + j + 1))
                                nc.scalar.activation(pT[:, h % 2, a:b].rearrange("p a b -> p (a b)"),
                                                     psum[:, 6 + (n + j) % 2, 0:(b - a) * P], ACT.Copy).then_inc(tr_taken, 1)
                        else:
                            for g, (t0, t1) in enumerate(PV_PARTS):
                                act.wait_ge(pv_ready, it * 16 + (2 * h + g + 1))
                                dst = acts_b[hd, 0, ds(it * 4 + h // 2, 1), t0:t1]
                                nc.scalar.activation(dst.rearrange("p o n -> p (o n)"),
                                                     psum[hd, 4 + (n + g) % 2, 0:t1 - t0], ACT.Copy
                                                     ).then_inc(pv_hi, 1)

            @block.vector
            def _(dve):
                for b in range(2):
                    dve.sem_inc(work_free[b], 1)
                dve.wait_ge(d_dist, 16)
                with dve.Fori(0, TRIPS) as it:
                    U = Unit(U_ATT, it, 6)
                    for step, kind, h, n in walk(SEQ_DVE):
                        head = it * 8 + h
                        if kind == "D":
                            do_lo(dve, U, h)
                        elif kind == "S":
                            for i, (q, k0, nk, wc) in enumerate(BLOCKS):
                                dve.wait_ge(score_ready, it * (8 * TT) + (h * TT + i + 1))
                                nc.vector.scalar_tensor_tensor(
                                    out=scores_of(h, B_OFF[i], B_OFF[i + 1]), in0=dist[:, wc:wc + nk * P],
                                    scalar=cst[:, ds(head + C_SLOPE, 1)], in1=psum[:, 4 + (n + i) % 2, 0:nk * P],
                                    op0=ALU.mult, op1=ALU.add).then_inc(work_free[(n + i) % 2], 1)
                            for b in range(2):
                                dve.wait_ge(work_free[b], it * (W_TRIP // 2) + ((n + TT) // 2 + 1))
                            for i in range(TT):
                                m = nc.vector.reduce_max(stat(h, 0)[:, i:i + 1],
                                                         scores_of(h, B_OFF[i], B_OFF[i + 1]), AX_X)
                            m.then_inc(max_done, 1)
                            sink = vec[:, ds(head + V_SINK, 1)]
                            dve.wait_ge(max_done, head + 1)
                            nc.vector.tensor_scalar(stat(h, 1), stat(h, 0), sink, -1.0, ALU.max, ALU.mult
                                                    ).then_inc(nmax_ready, 1)
                            dve.wait_ge(nmax_ready, head + 1)
                            nc.vector.tensor_scalar(stat(h, 2), stat(h, 1), sink, None, ALU.add
                                                    ).then_inc(sinkd_ready, 1)
                        elif kind == "F":
                            dve.wait_ge(exp_ready, head + 1)
                            nc.vector.tensor_tensor(stat(h, 5), stat(h, 3), stat(h, 4), ALU.add
                                                    ).then_inc(den_step, 1)
                            dve.wait_ge(den_step, it * 16 + (2 * h + 1))
                            nc.vector.reciprocal(stat(h, 5), stat(h, 5)).then_inc(den_step, 1)
                            dve.wait_ge(den_step, it * 16 + (2 * h + 2))
                            for i in range(TT):
                                s = scores_of(h, B_OFF[i], B_OFF[i + 1])
                                m = nc.vector.tensor_scalar(s, s, stat(h, 5)[:, i:i + 1], None, ALU.mult)
                            m.then_inc(prob_ready, 1)
                        else:
                            hd = slice(h % 2 * HD, (h % 2 + 1) * HD)
                            for g, (t0, t1) in enumerate(PV_PARTS):
                                dve.wait_ge(pv_hi, it * 16 + (2 * h + g + 1))
                                hi, lo = (acts_b[hd, j, ds(it * 4 + h // 2, 1), t0:t1].rearrange("p o n -> p (o n)")
                                          for j in range(2))
                                nc.vector.tensor_tensor(lo, psum[hd, 4 + (n + g) % 2, 0:t1 - t0], hi.bitcast(F32),
                                                        ALU.subtract).then_inc(work_free[(n + g) % 2], 1)

        def gate_phase(name, u0, last_phase):
            A = Arena()
            y = A.take(2, T)
            A.take(4, T)
            both = A.take(DC, 2 * T)
            sg, m_sb = both[:, :, 0:T], both[:, :, T:2 * T]
            made = GATES_AHEAD if last_phase else 0
            g_m, g_st, g_y, g_sum, g_hi = (sem(name + k) for k in ("_m", "_st", "_y", "_sum", "_hi"))
            with nc.Block() as block:
                @block.sync
                def _(sp):
                    if last_phase:
                        sp.dma_start(m_sb, m_dram.rearrange("c p t -> p c t")).then_inc(g_m, 16)
                    with sp.Fori(0, (DC - made) // 2) as it:
                        for u in range(2):
                            do_load(sp, Unit(u0 + made, it, 2), u)
                    with sp.Fori(0, DC // 2) as it:
                        for u in range(2):
                            do_load(sp, Unit(u0 + DC, it, 2), u)
                            if not last_phase:
                                sp.wait_ge(g_y, it * 2 + (u + 1))
                                sp.dma_start(m_dram[ds(it * 2 + u, 1)].rearrange("o p t -> p (o t)"),
                                             m_sb[:, ds(it * 2 + u, 1)].rearrange("p o t -> p (o t)")
                                             ).then_inc(g_st, 16)
                    if not last_phase:
                        sp.wait_ge(g_st, 16 * DC)

                @block.tensor
                def _(pe):
                    for base, n, a in ((u0 + made, DC - made, acts_a), (u0 + DC, DC, acts_b)):
                        with pe.Fori(0, n // 2) as it:
                            for u in range(2):
                                project(pe, Unit(base, it, 2), u, a)

                @block.scalar
                def _(act):
                    with act.Fori(0, (DC - made) // 2) as it:
                        U = Unit(u0 + made, it, 2)
                        for u in range(2):
                            act.wait_ge(w_used, U.at(u) + 1)
                            nc.scalar.activation(sg[:, ds(it * 2 + (made + u), 1)].rearrange("p o (a b) -> p (o a) b", a=2),
                                                 proj_out(u), ACT.Sigmoid).then_inc(proj_free[u], 1)
                            do_hi(act, U, u)
                    with act.Fori(0, DC // 2) as it:
                        U = Unit(u0 + DC, it, 2)
                        for u in range(2):
                            do_hi(act, U, u)
                            if last_phase:
                                act.wait_ge(g_sum, it * 2 + (u + 1))
                                nc.scalar.activation(acts_a[:, 0, ds(it * 2 + u, 1)].rearrange("p o t -> p (o t)"),
                                                     y[:, u], ACT.Copy).then_inc(g_hi, 1)

                @block.vector
                def _(dve):
                    with dve.Fori(0, (DC - made) // 2) as it:
                        for u in range(2):
                            do_lo(dve, Unit(u0 + made, it, 2), u)
                    if last_phase:
                        dve.wait_ge(g_m, 16)
                    with dve.Fori(0, DC // 2) as it:
                        U = Unit(u0 + DC, it, 2)
                        for u in range(2):
                            c = it * 2 + u
                            dve.wait_ge(w_used, U.at(u) + 1)
                            dve.wait_ge(proj_free[u], (u0 + DC) // 2 + 1)
                            gate = sg[:, ds(c, 1)].rearrange("p o (a b) -> p (o a) b", a=2)
                            if not last_phase:
                                nc.vector.tensor_tensor(m_sb[:, ds(c, 1)].rearrange("p o (a b) -> p (o a) b", a=2),
                                                        proj_out(u), gate, ALU.mult).then_inc(proj_free[u], 1)
                                dve.wait_ge(proj_free[u], U.half(u) + 2)
                                dve.sem_inc(g_y, 1)
                            else:
                                nc.vector.tensor_tensor(two(y[:, u]), proj_out(u), gate, ALU.mult
                                                        ).then_inc(proj_free[u], 1)
                                dve.wait_ge(proj_free[u], U.half(u) + 2)
                                nc.vector.tensor_tensor(y[:, u], y[:, u], m_sb[:, ds(c, 1)].rearrange("p o t -> p (o t)"),
                                                        ALU.add).then_inc(g_sum, 1)
                            do_lo(dve, U, u)
                            if last_phase:
                                dve.wait_ge(g_hi, c + 1)
                                hi, lo = (acts_a[:, k, ds(c, 1)].rearrange("p o t -> p (o t)") for k in range(2))
                                nc.vector.tensor_tensor(lo, y[:, u], hi.bitcast(F32), ALU.subtract
                                                        ).then_inc(g_y, 1)

        gate_phase("ga", U_GATT, False)

        A = Arena()
        hq, hv, gs = A.take(2, T), A.take(2, T), A.take(2, T)
        Pf, Pb, kf, kb = (A.take(2, T) for _ in range(4))
        Xf, Xb = A.take(T), A.take(T)
        Qs, Ks = A.take(2, T), A.take(2, T)
        kx, S = A.take(2, 4, P), A.take(2, 4, P)
        masks = A.take(LEVELS, P)
        pad = A.take(2)
        tots = A.take(2, TT)
        At0 = A.take(T)
        Qe = hg_more[:, 0:2]
        At = (At0, hg_more[:, 2])
        o_sb, rr = Qe[:, 0], Qe[:, 1]
        ENTER = ({1: 0, 2: 1, 3: 2, 5: 3}, {2: 0, 1: 1, 0: 2, 4: 3})
        MAKE = ((0, 1, 2, 4), (3, 2, 1, 5))
        names = """d_mask z_ready f_ready sum_ready lev_ready qkb_ready lev_done updf_step updb_step endf_ready
                   endb_ready kx_tr kx_ready kv_done st_ready o_ready sq_ready ss_ready ms_ready root_ready r_step
                   of_ready oh_ready ol_ready pad_ready""".split()
        (d_mask, z_ready, f_ready, sum_ready, lev_ready, qkb_ready, lev_done, updf_step, updb_step, endf_ready,
         endb_ready, kx_tr, kx_ready, kv_done, st_ready, o_ready, sq_ready, ss_ready, ms_ready, root_ready, r_step,
         of_ready, oh_ready, ol_ready, pad_ready) = (sem(n) for n in names)
        bank_taken = [sem("bank_taken0"), sem("bank_taken1")]
        HU = 5
        ZF, ZB, QH, GH, IH = range(HU)
        DIAG = LEVELS
        PROD = LEVELS + 1
        UPD = 1 + 2 * LEVELS
        SEQ_PE = "H0 L0 H1 L1 o H2 L2 H3 L3 n H4 L4 H5 L5 H6 L6 H7 L7 H8 T H9 V".split()
        SEQ_ACT = "L0 o U0 U1 n U2 f U3 T U4".split()
        SEQ_DVE = "Q1 s Q2 K1 Q3 U0 K2 Q4 K3 Q5 n U1 K4 Q6 m0 K5 m1 m2 K6 U2 Z f K7 U3 Q0 U4".split()
        SEQ_POOL = "B1 B2 B3 B4 B5 B6 Q7 Z B0".split()

        def halves(ap, B):
            return ap.rearrange("p (n h b) -> p n h b", h=2, b=B)

        def tot(Pr, B, half, direction):
            j = B - 1 if direction == 0 else 0
            a = halves(Pr, B)[:, :, half, j:j + 1]
            return a.broadcast_to([P, T // (2 * B), B]) if B > 1 else a

        def in_unit_act(act, U, u, i, b):
            do_hi(act, U, u)
            s = u % 2
            if i in (ZF, ZB):
                Pr, kr = (Pf, kf) if i == ZF else (Pb, kb)
                nc.scalar.activation(two(Pr[:, b]), proj_out(u), ACT.Sigmoid)
                nc.scalar.activation(two(kr[:, b]), proj_out(u), ACT.Sigmoid, scale=-1.0).then_inc(proj_free[s], 1)
            elif i == IH:
                nc.scalar.activation(two(hv[:, b]), proj_out(u), ACT.Copy).then_inc(proj_free[s], 1)
            else:
                nc.scalar.activation(two((hq if i == QH else gs)[:, b]), proj_out(u), ACT.Sigmoid).then_inc(z_ready, 1)

        def in_unit_dve(dve, U, u, i, b, hd):
            s = u % 2
            do_lo(dve, U, u)
            if i in (ZF, ZB):
                Pr, kr = (Pf, kf) if i == ZF else (Pb, kb)
                lbc, omc = (lb[:, k, i, ds(hd, 1)] for k in range(2))
                dve.wait_ge(proj_free[s], U.half(u) + 2)
                nc.vector.tensor_scalar(Pr[:, b], Pr[:, b], omc, lbc, ALU.mult, ALU.add).then_inc(f_ready, 1)
                nc.vector.tensor_scalar(kr[:, b], kr[:, b], omc, None, ALU.mult).then_inc(f_ready, 1)
            elif i in (QH, GH):
                dst = (hq if i == QH else gs)[:, b]
                dve.wait_ge(z_ready, hd * 2 + (1 if i == QH else 2))
                nc.vector.tensor_tensor(two(dst), two(dst), proj_out(u), ALU.mult).then_inc(proj_free[s], 1)

        BANKS = ((4, 0, T_PROMPT), (5, T_PROMPT, T))

        def head_pe(pe, hd, b, kind, k, first):
            if kind == "L":
                if k == DIAG:
                    pe.wait_ge(sum_ready, hd + 1)
                    l, r = Ks[:, 1], hq[:, b]
                else:
                    pe.wait_ge(lev_ready, hd * LEVELS + (k + 1))
                    l, r = Ks[:, k % 2], Qs[:, k % 2]
                for bank, (bk, t0, t1) in enumerate(BANKS):
                    pe.wait_ge(bank_taken[bank], hd * PROD + (k + 1))
                    for t in range(t0, t1, P):
                        m = nc.tensor.matmul(psum[:, bk, t - t0:t - t0 + P], l[:, t:t + P], r[:, t:t + P],
                                             start=True, stop=True)
                    m.then_inc(lev_done, 1)
            elif kind == "T":
                pe.wait_ge(endf_ready, hd + 1)
                pe.wait_ge(endb_ready, hd + 1)
                pe.wait_ge(ms_ready, hd + 1)
                for d in range(2):
                    for j, c in enumerate(MAKE[d]):
                        m = nc.tensor.transpose(psum[:, 6 + d, j * P:(j + 1) * P], Ks[:, d, c * P:(c + 1) * P], ident)
                    m.then_inc(kx_tr, 1)
            elif kind == "V":
                for d in range(2):
                    pe.wait_ge(kx_ready, hd * 2 + (d + 1))
                    for j, c in enumerate(MAKE[d]):
                        m = nc.tensor.matmul(psum[:, 6 + d, j * P:(j + 1) * P], kx[:, d, j], hv[:, b, c * P:(c + 1) * P],
                                             start=True, stop=True)
                    m.then_inc(kv_done, 1)
            elif kind == "o":
                pe.wait_ge(st_ready, hd * 6 + 6)
                for bank, (bk, t0, t1) in enumerate(BANKS):
                    pe.wait_ge(bank_taken[bank], (hd + 1) * PROD + 1)
                    for t in range(t0, t1, P):
                        c = t // P
                        o = psum[:, bk + 2, t - t0:t - t0 + P]
                        parts = [(hv[:, b, t:t + P], At[b][:, t:t + P])]
                        parts += [(S[:, d, ENTER[d][c]], Qe[:, d, t:t + P]) for d in range(2) if c in ENTER[d]]
                        for n, (l, r) in enumerate(parts):
                            m = nc.tensor.matmul(o, l, r, start=(n == 0), stop=(n == len(parts) - 1))
                    m.then_inc(o_ready, 1)
            else:
                for bank, (bk, t0, t1) in enumerate(BANKS):
                    pe.wait_ge(sq_ready, hd * 2 + (bank + 1))
                    nc.tensor.matmul(psum[:, bk + 2, 0:t1 - t0], ones, rr[:, t0:t1], start=True, stop=True
                                     ).then_inc(ss_ready, 1)

        def head_act(act, hd, b, kind, k, first):
            if kind == "L":
                for bank, (bk, t0, t1) in enumerate(BANKS):
                    act.wait_ge(lev_done, hd * (2 * PROD) + (bank + 1))
                    nc.scalar.activation(At[b][:, t0:t1], psum[:, bk, 0:t1 - t0], ACT.Copy).then_inc(bank_taken[bank], 1)
            elif kind == "T":
                for d in range(2):
                    act.wait_ge(kx_tr, hd * 2 + (d + 1))
                    nc.scalar.activation(kx[:, d].rearrange("p a b -> p (a b)"), psum[:, 6 + d, :], ACT.Copy
                                         ).then_inc(kx_ready, 1)
            elif kind == "o":
                act.wait_ge(o_ready, hd * 2 + 2)
                for bank, (bk, t0, t1) in enumerate(BANKS):
                    nc.scalar.activation(o_sb[:, t0:t1], psum[:, bk + 2, 0:t1 - t0], ACT.Copy)
                    nc.scalar.activation(rr[:, t0:t1], psum[:, bk + 2, 0:t1 - t0], ACT.Square).then_inc(sq_ready, 1)
            elif kind == "n":
                act.wait_ge(ms_ready, hd + 2)
                nc.scalar.activation(rr, rr, ACT.Sqrt).then_inc(root_ready, 1)
            elif kind == "f":
                act.wait_ge(of_ready, hd + 1)
                nc.scalar.activation(acts_b[:, 0, ds(hd, 1)].rearrange("p o t -> p (o t)"), At[b], ACT.Copy
                                     ).then_inc(oh_ready, 1)

        def operands(hd, k, directions):
            B = 1 << k
            Q, K = halves(Qs[:, k % 2], B), halves(Ks[:, k % 2], B)
            for o, a, x, h in directions:
                o = Q if o == "q" else K
                m = nc.vector.tensor_tensor(o[:, :, h], halves(a, B)[:, :, h], halves(x, B)[:, :, h], ALU.mult)
            return m

        def update(eng, tt, hd, k, Pr, X, d, step):
            B = 1 << k
            xv, pv = halves(X, B)[:, :, d], halves(Pr, B)[:, :, 1 - d]
            tt(xv, xv, tot(Pr, B, 1 - d, d), ALU.mult).then_inc(step, 1)
            eng.wait_ge(step, hd * UPD + (2 + 2 * k))
            tt(pv, pv, tot(Pr, B, d, d), ALU.mult).then_inc(step, 1)

        def head_dve(dve, hd, b, kind, k, first):
            q, pf, pb, kf_, kb_ = hq[:, b], Pf[:, b], Pb[:, b], kf[:, b], kb[:, b]
            if kind == "Q":
                if k == 0:
                    if not first:
                        dve.wait_ge(endf_ready, hd)
                        dve.wait_ge(endb_ready, hd)
                        dve.wait_ge(kx_tr, hd * 2)
                    nc.vector.memset(Xf, 1.0).then_inc(updf_step, 1)
                    nc.vector.memset(Xb, 1.0).then_inc(updb_step, 1)
                    dve.wait_ge(f_ready, hd * 4 + 4)
                elif k >= 2:
                    dve.wait_ge(lev_done, hd * (2 * PROD) + 2 * (k - 1))
                dve.wait_ge(updb_step, hd * UPD + (1 + 2 * k))
                operands(hd, k, (("q", q, pb, 0), ("k", kb_, Xb, 1))).then_inc(qkb_ready, 1)
                dve.wait_ge(updf_step, hd * UPD + (1 + 2 * k))
                operands(hd, k, (("q", q, pf, 1), ("k", kf_, Xf, 0))).then_inc(lev_ready, 1)
                dve.wait_ge(lev_ready, hd * LEVELS + (k + 1))
                update(dve, nc.vector.tensor_tensor, hd, k, pf, Xf, 0, updf_step)
            elif kind == "K":
                dve.wait_ge(lev_done, hd * (2 * PROD) + 2 * (k + 1))
                nc.vector.tensor_copy(pad[:, 0:1], pad[:, 1:2])
                for bank, (bk, t0, t1) in enumerate(BANKS):
                    n = (t1 - t0) // P
                    mask = ident.rearrange("p (o b) -> p o b", o=1) if k == DIAG else masks[:, k:k + 1]
                    nc.vector.copy_predicated(At[b][:, t0:t1].rearrange("p (n b) -> p n b", n=n),
                                              mask.bitcast(U32).broadcast_to([P, n, P]),
                                              psum[:, bk, 0:t1 - t0].rearrange("p (n b) -> p n b", n=n)
                                              ).then_inc(bank_taken[bank], 1)
            elif kind == "Z":
                dve.wait_ge(lev_done, hd * (2 * PROD) + 2 * LEVELS)
                dve.wait_ge(updf_step, (hd + 1) * UPD)
                nc.vector.tensor_tensor(Ks[:, 0], kf_, Xf, ALU.mult)
                nc.vector.tensor_tensor(Qe[:, 0], q, pf, ALU.mult)
                nc.vector.tensor_copy(tots[:, 0], pf[:, P - 1:T:P])
                dve.wait_ge(updb_step, (hd + 1) * UPD)
                nc.vector.tensor_copy(tots[:, 1], pb[:, 0:T:P]).then_inc(endf_ready, 1)
            elif kind == "s":
                n = hd * 6
                for d in range(2):
                    dve.wait_ge(kv_done, hd * 2 + (d + 1))
                    D4 = psum[:, 6 + d, :].rearrange("p (a b) -> p a b", a=4)
                    nc.vector.tensor_copy(S[:, d, 0:4:3], D4[:, 0:4:3]).then_inc(st_ready, 1)
                    for j in (1, 2):
                        c = MAKE[d][j]
                        dve.wait_ge(st_ready, n + 3 * d + j)
                        nc.vector.scalar_tensor_tensor(out=S[:, d, j], in0=S[:, d, j - 1], scalar=tots[:, d, c:c + 1],
                                                       in1=D4[:, j], op0=ALU.mult, op1=ALU.add).then_inc(st_ready, 1)
            elif kind == "n":
                for bank, (bk, t0, t1) in enumerate(BANKS):
                    dve.wait_ge(ss_ready, hd * 2 + (bank + 1))
                    m = nc.vector.tensor_scalar(rr[:, t0:t1], psum[:, bk + 2, 0:t1 - t0], 1.0 / P, EPS, ALU.mult, ALU.add)
                m.then_inc(ms_ready, 1)
            elif kind == "m":
                if k < 2:
                    part = rr[:, k * HALF:(k + 1) * HALF]
                    dve.wait_ge(root_ready, hd + 1)
                    nc.vector.reciprocal(part, part).then_inc(r_step, 1)
                    return
                dve.wait_ge(r_step, hd * 3 + 2)
                nc.vector.tensor_tensor(rr, rr, o_sb, ALU.mult).then_inc(r_step, 1)
                dve.wait_ge(r_step, hd * 3 + 3)
                nc.vector.scalar_tensor_tensor(out=At[b], in0=rr, scalar=vec[:, ds(hd + V_GH, 1)],
                                               in1=gs[:, b], op0=ALU.mult, op1=ALU.mult).then_inc(of_ready, 1)
            elif kind == "f":
                dve.wait_ge(oh_ready, hd + 1)
                hi, lo = (acts_b[:, j, ds(hd, 1)].rearrange("p o t -> p (o t)") for j in range(2))
                nc.vector.tensor_tensor(lo, At[b], hi.bitcast(F32), ALU.subtract).then_inc(ol_ready, 1)

        def head_pool(pool, hd, b, kind, k, first):
            if kind == "B":
                pool.wait_ge(qkb_ready, hd * LEVELS + (k + 1))
                update(pool, nc.gpsimd.tensor_tensor, hd, k, Pb[:, b], Xb, 1, updb_step)
            elif kind == "Q":
                pool.wait_ge(lev_done, hd * (2 * PROD) + 2 * (LEVELS - 1))
                nc.gpsimd.tensor_tensor(Ks[:, 1], kf[:, b], kb[:, b], ALU.add).then_inc(sum_ready, 1)
            else:
                pool.wait_ge(updb_step, (hd + 1) * UPD)
                pool.wait_ge(lev_done, (hd + 1) * (2 * PROD))
                nc.gpsimd.tensor_tensor(Qe[:, 1], hq[:, b], Pb[:, b], ALU.mult)
                nc.gpsimd.tensor_tensor(Ks[:, 1], kb[:, b], Xb, ALU.mult).then_inc(endb_ready, 1)

        def gate_act(act, U, i):
            act.wait_ge(w_used, U.at(i) + 1)
            nc.scalar.activation(two((Pf, Pb, kf, kb)[i][:, 0]), proj_out(i), ACT.Sigmoid).then_inc(proj_free[i % 2], 1)
            do_hi(act, U, i)

        def run_heads(eng, seq, head_fn, unit_fn, gate_fn, starts="Q0 B0".split()):
            def body(hd, b, U, next_u, prev=True, nxt=True):
                for step in seq:
                    kind, k = step[0], int(step[1:] or 0)
                    if kind in "HU":
                        if not nxt:
                            i = k // 2 if kind == "H" else k
                            if i < GATES_AHEAD:
                                gate_fn(Unit(U_GHG), i, k)
                        else:
                            i = k // 2 if kind == "H" else k
                            unit_fn(U, next_u + i, i, 1 - b, hd + 1, k)
                    elif step in starts:
                        if nxt:
                            head_fn(eng, hd + 1, 1 - b, kind, k, False)
                    elif kind.islower():
                        if prev:
                            head_fn(eng, hd - 1, 1 - b, kind, k, False)
                    else:
                        head_fn(eng, hd, b, kind, k, False)
            for step in seq:
                if step[0] in "HU":
                    k = int(step[1:])
                    i = k // 2 if step[0] == "H" else k
                    unit_fn(Unit(U_HG), i, i, 0, 0, k)
            for step in seq:
                if step in starts:
                    head_fn(eng, 0, 0, step[0], 0, True)
            body(0, 0, Unit(U_HG), HU, prev=False)
            with eng.Fori(0, H_HEADS // 2 - 1) as it:
                for b in (1, 0):
                    body(it * 2 + (2 - b), b, Unit(U_HG, it, 2 * HU), (3 - b) * HU)
            body(H_HEADS - 1, 1, None, None, nxt=False)
            for step in seq:
                if step[0].islower():
                    head_fn(eng, H_HEADS - 1, 1, step[0], int(step[1:] or 0), False)

        with nc.Block() as block:
            @block.sync
            def _(sp):
                sp.dma_start(masks, consts[:, C_MASK:C_MASK + LEVELS * P].rearrange("p (a b) -> p a b", a=LEVELS)
                             ).then_inc(d_mask, 16)
                with sp.Fori(0, (N_HG + GATES_AHEAD) // 2) as it:
                    for u in range(2):
                        do_load(sp, Unit(U_HG, it, 2), u)

            @block.tensor
            def _(pe):
                run_heads(pe, SEQ_PE, head_pe, lambda U, u, i, b, h, k: project(
                    pe, U, u, acts_a, tokens_out=(i == IH), halves=(k % 2,)),
                          lambda U, i, k: project(pe, U, i, acts_a, halves=(k % 2,)))

            @block.scalar
            def _(act):
                run_heads(act, SEQ_ACT, head_act, lambda U, u, i, b, h, k: in_unit_act(act, U, u, i, b),
                          lambda U, i, k: gate_act(act, U, i))

            @block.vector
            def _(dve):
                for b in range(2):
                    dve.sem_inc(bank_taken[b], 1)
                dve.sem_inc(ms_ready, 1)
                nc.vector.memset(pad, 0.0).then_inc(pad_ready, 1)
                dve.wait_ge(pad_ready, 1)
                dve.wait_ge(d_mask, 16)
                run_heads(dve, SEQ_DVE, head_dve, lambda U, u, i, b, h, k: in_unit_dve(dve, U, u, i, b, h),
                          lambda U, i, k: do_lo(dve, U, i))

            @block.gpsimd
            def _(pool):
                run_heads(pool, SEQ_POOL, head_pool, None, None)

        gate_phase("gb", U_GHG, True)

        A = Arena()
        x1 = A.take(DC, T)
        x1_flat = arena[:, 0:DC * T]
        d_x1, x1_done = sem("d_x1"), sem("x1_done")
        PIECES = ((0, 0, HALF, 0), (1, HALF, T_PROMPT, 0), (1, T_PROMPT, T, 1))
        n2 = Norm("n2", x1, lambda d, g: modcol(SCALE2, d, g), lambda d, g: modcol(SHIFT2, d, g), acts_a,
                  norm_work(A))

        def out_units(eng, body):
            for u in range(2):
                body(Unit(U_OUT), u, u, u)
            with eng.Fori(0, DC // 2 - 1) as it:
                for u in range(2):
                    body(Unit(U_OUT, it, 2), u + 2, u + 2, it * 2 + (u + 2))

        with nc.Block() as block:
            @block.sync
            def _(sp):
                sp.dma_start(x1_flat, x_t).then_inc(d_x1, 16)
                out_units(sp, lambda U, u, d, at: do_load(sp, U, u))

            @block.tensor
            def _(pe):
                def body(U, u, d, at):
                    project(pe, U, u, acts_a)
                    if d == 1:
                        n2.sums(pe, 0)
                    elif d > 1:
                        n2.sums(pe, d - 1, at - 1)
                out_units(pe, body)
                n2.sums(pe, DC - 1)

            @block.scalar
            def _(act):
                def body(U, u, d, at):
                    do_hi(act, U, u)
                    act.wait_ge(proj_free[u % 2], U.half(u) + 2)
                    n2.square(act, d, None if d < 2 else at)
                out_units(act, body)

            @block.vector
            def _(dve):
                def body(U, u, d, at):
                    dve.wait_ge(w_used, U.at(u) + 1)
                    for bank, t0, t1, g in PIECES:
                        x = x1[:, ds(at, 1), t0:t1].rearrange("p o t -> p (o t)")
                        gate = mod[:, ds(at + GATE1 * DC, 1), g:g + 1].rearrange("p o t -> p (o t)")
                        m = nc.vector.scalar_tensor_tensor(
                            out=x, in0=psum[:, 2 * (u % 2) + bank, t0 - bank * HALF:t1 - bank * HALF], scalar=gate,
                            in1=x, op0=ALU.mult, op1=ALU.add)
                    m.then_inc(proj_free[u % 2], 1)
                    do_lo(dve, U, u)
                dve.wait_ge(d_x1, 16)
                out_units(dve, body)
        x1_stored = sem("x1_stored")
        with nc.Block() as block:
            @block.sync
            def _(sp):
                sp.dma_start(x1_dram, x1_flat).then_inc(x1_stored, 16)
                sp.wait_ge(x1_stored, 16)

            @block.scalar
            def _(act):
                n2.root(act)
                for d in range(DC):
                    n2.apply_act(act, d)

            @block.vector
            def _(dve):
                n2.stats_dve(dve)
                n2.apply_dve(dve)

        RING = 16
        e_split, e_raw, e_gl, oh_j, tables = room.take(
            ("e_split", [P, 2, 2, DC, P], F32R), ("e_raw", [P, 2, DC, P], F32), ("e_gl", [P, 2, T], F32),
            ("oh_j", [P, RING, NKEYS], F32), ("tables", [P, 2, T], F32))
        gl_dram = nc.dram_tensor("gelu_scratch", (EARLY, P, T), F32, kind="Internal").ap()
        e_in, e_out = [sem("e_in0"), sem("e_in1")], [sem("e_out0"), sem("e_out1")]
        e_hi, e_lo, e_done, e_gelu = sem("e_hi"), sem("e_lo"), sem("e_done"), sem("e_gelu")

        def e_load(sp, e, s):
            sp.dma_start(e_raw[:, s], u_early[ds(e, 1)].rearrange("o p (c k) -> p (o c) k", c=DC)
                         ).then_inc(e_in[s], 16)

        def early_sync(sp, E, u):
            sp.wait_ge(e_lo, E.at(u) + 1)
            e_load(sp, E.at(u) + EARLY_LEAD, u % 2)
            sp.wait_ge(e_gelu, E.at(u) * 2 + 4)
            sp.dma_start(gl_dram[ds(E.at(u), 1)].rearrange("o p t -> p (o t)"), e_gl[:, u % 2]
                         ).then_inc(e_out[u % 2], 16)

        def early_hi(act, s):
            nc.scalar.activation(e_split[:, s, 0], e_raw[:, s], ACT.Copy).then_inc(e_hi, 1)

        def early_act(act, E, u, t):
            act.wait_ge(e_done, E.at(u) * 2 + (t + 1))
            if t == 0:
                act.wait_ge(e_out[u % 2], E.half(u) * 16 + 16)
            nc.scalar.activation(e_gl[:, u % 2, t * HALF:(t + 1) * HALF], psum[:, 6 + t, 0:HALF], ACT.Gelu
                                 ).then_inc(e_gelu, 1)
            if t == 1:
                act.wait_ge(e_in[u % 2], E.half(u) * 16 + 32)
                early_hi(act, u % 2)

        def early_lo(pool, e, s):
            pool.wait_ge(e_hi, e + 1)
            nc.gpsimd.tensor_tensor(e_split[:, s, 1], e_raw[:, s], e_split[:, s, 0].bitcast(F32), ALU.subtract
                                    ).then_inc(e_lo, 1)

        def early_pe(pe, E, u, t):
            pe.wait_ge(e_lo, E.at(u) + 1)
            pe.wait_ge(e_gelu, E.at(u) * 2 + (t + 1))
            for d in range(DC):
                for i, (wh, ah) in enumerate(((0, 0), (0, 1), (1, 0))):
                    m = nc.tensor.matmul(psum[:, 6 + t, 0:HALF], e_split[:, u % 2, wh, d, :],
                                         acts_a[:, ah, d, t * HALF:(t + 1) * HALF],
                                         start=(d == 0 and i == 0), stop=(d == DC - 1 and i == 2))
            m.then_inc(e_done, 1)

        A = Arena()
        KH = TOPK // 2
        keys = A.take(2 * PH * NKEYS)
        qh_sb, s_sb, s_cut = A.take(2, T), A.take(2, TT, NKEYS), A.take(TT, NKEYS)
        sv = A.take(2, TT, TOPK)
        si = A.take(2, TT, TOPK).bitcast(U32)
        sf = A.take(2, TT, TOPK)
        cv, cid, cv_cut = A.take(TT, CAND), A.take(TT, CAND), A.take(TT, CAND)
        tv = A.take(TT, TOPK)
        tp = A.take(TT, TOPK).bitcast(U32)
        tpf, te, tsum = A.take(TT, TOPK), A.take(TT, TOPK), A.take(TT)
        onehot = A.take(TOPK, CAND)
        eid, gate = A.take(TT, PH * TOPK), A.take(TT, PH * TOPK)
        ei = A.take(TT, PH * TOPK).bitcast(U32)
        te_ji, te_j = A.take(TT, PH * TOPK).bitcast(U32), A.take(TT, PH * TOPK)
        pad = A.take(2)
        gate_t, i_t = tables[:, 0], tables[:, 1]
        j_t = arena[:, ARENA - T:ARENA]
        d_keys, qh_ready, s_done, s_ready = sem("d_keys"), sem("qh_ready"), sem("s_done"), sem("s_ready")
        s_bank = [sem("s_bank0"), sem("s_bank1")]
        k_step, sf_ready, cid_ready, ts_ready, te_ready, head_done = (
            sem(n) for n in ("k_step", "sf_ready", "cid_ready", "ts_ready", "te_ready", "head_done"))
        tab_tr, tab_done, slot_free = sem("tab_tr"), sem("tab_done"), sem("slot_free")
        STEPS = 35
        rows = []
        at = 0
        for a in range(TOPK):
            rows.append((a, at, ROW_LEN[a]))
            at += ROW_LEN[a]
        SINGLE = TOPK // 2

        def pair_sums(eng_tt, out, first, second):
            for a, o, n in rows[:SINGLE]:
                m = eng_tt(out[:, :, o:o + n], second[:, :, 0:n], first[:, :, a:a + 1].broadcast_to([P, TT, n]), ALU.add)
            o = rows[SINGLE][1]
            return eng_tt(out[:, :, o:o + TOPK - SINGLE], first[:, :, SINGLE:TOPK],
                          second[:, :, 0:1].broadcast_to([P, TT, TOPK - SINGLE]), ALU.add)

        with nc.Block() as block:
            @block.sync
            def _(sp):
                for e in range(EARLY_LEAD):
                    e_load(sp, e, e)
                sp.dma_start(keys, keys_t).then_inc(d_keys, 16)
                with sp.Fori(0, PH // 2) as it:
                    for hh in range(2):
                        for u in range(2):
                            do_load(sp, Unit(U_PQ, it, 4), 2 * hh + u)
                        for k in range(EARLY_PQ):
                            early_sync(sp, Unit(0, it, 2 * EARLY_PQ), hh * EARLY_PQ + k)

            @block.tensor
            def _(pe):
                def scores(n, u, hp):
                    pe.wait_ge(d_keys, 16)
                    pe.wait_ge(qh_ready, n + 1)
                    pe.wait_ge(s_bank[0], n + 1)
                    for t in range(TT):
                        m = nc.tensor.matmul(psum[:, 4 + t // 4, t % 4 * P:t % 4 * P + P],
                                             qh_sb[:, u, t * P:(t + 1) * P], keys[:, ds(hp, NKEYS)],
                                             start=True, stop=True)
                    m.then_inc(s_done, 1)
                with pe.Fori(0, PH // 2) as it:
                    U, E = Unit(U_PQ, it, 4), Unit(0, it, 2 * EARLY_PQ)

                    def early(k):
                        for t in range(2):
                            early_pe(pe, E, k, t)
                    for hh in range(2):
                        for u in range(2):
                            project(pe, U, 2 * hh + u, acts_a)
                        for u in range(2):
                            n = it * 4 + (2 * hh + u)
                            scores(n, u, n * NKEYS)
                            early(hh * EARLY_PQ + u)
                        for k in range(2, EARLY_PQ):
                            early(hh * EARLY_PQ + k)
                pe.wait_ge(tab_done, 1)
                for k, tab in enumerate((gate, eid, te_j)):
                    for t in range(TT):
                        m = nc.tensor.transpose(psum[:, 2 * k + t // 4, t % 4 * P:t % 4 * P + P], tab[:, t], ident)
                    m.then_inc(tab_tr, 1)

            @block.scalar
            def _(act):
                act.sem_inc(e_gelu, 2)
                for e in range(EARLY_LEAD):
                    act.sem_inc(e_out[e], 16)
                    act.wait_ge(e_in[e], 16)
                    early_hi(act, e)
                with act.Fori(0, PH // 2) as it:
                    U, E = Unit(U_PQ, it, 4), Unit(0, it, 2 * EARLY_PQ)

                    def early(k):
                        for t in range(2):
                            early_act(act, E, k, t)
                    for hh in range(2):
                        for u in range(2):
                            v = 2 * hh + u
                            act.wait_ge(w_used, U.at(v) + 1)
                            nc.scalar.activation(two(qh_sb[:, u]), proj_out(v), ACT.Copy).then_inc(proj_free[u], 1)
                            act.wait_ge(proj_free[u], U.half(v) + 2)
                            act.sem_inc(qh_ready, 1)
                            do_hi(act, U, v)
                        for u in range(2):
                            n = it * 4 + (2 * hh + u)
                            act.wait_ge(s_done, n + 1)
                            act.wait_ge(slot_free, n + 1)
                            flat = s_sb[:, u].rearrange("p a b -> p (a b)")
                            nc.scalar.activation(flat[:, 0:512], psum[:, 4, :], ACT.Copy)
                            nc.scalar.activation(flat[:, 512:T], psum[:, 5, 0:T - 512], ACT.Copy).then_inc(s_bank[0], 1)
                            early(hh * EARLY_PQ + u)
                        for k in range(2, EARLY_PQ):
                            early(hh * EARLY_PQ + k)
                        act.wait_ge(ts_ready, it * 2 + (hh + 1))
                        nc.scalar.activation(te, te, ACT.Exp).then_inc(te_ready, 1)
                for s in range(2):
                    act.wait_ge(raw_ready[s], 16 * (UNITS + LEAD) // 2)
                for k, dst in enumerate((gate_t, i_t, j_t)):
                    act.wait_ge(tab_tr, k + 1)
                    nc.scalar.activation(dst[:, 0:512], psum[:, 2 * k, :], ACT.Copy)
                    nc.scalar.activation(dst[:, 512:T], psum[:, 2 * k + 1, 0:T - 512], ACT.Copy).then_inc(te_ready, 1)

            @block.gpsimd
            def _(pool):
                for e in range(EARLY_LEAD):
                    early_lo(pool, e, e)
                with pool.Fori(0, PH // 2) as it:
                    E = Unit(0, it, 2 * EARLY_PQ)
                    for hh in range(2):
                        for k in range(EARLY_PQ):
                            if k == EARLY_PQ - 2:
                                pool.wait_ge(sf_ready, it * 2 + (hh + 1))
                                pair_sums(nc.gpsimd.tensor_tensor, cid, sf[:, 0], sf[:, 1]).then_inc(cid_ready, 1)
                            e = hh * EARLY_PQ + k
                            early_lo(pool, E.at(e) + EARLY_LEAD, e % 2)

            @block.vector
            def _(dve):
                dve.sem_inc(s_bank[0], 1)
                dve.sem_inc(slot_free, 2)
                nc.vector.memset(pad, 0.0).then_inc(k_step, 1)
                dve.wait_ge(k_step, 1)
                with dve.Fori(0, PH // 2) as it:
                    U = Unit(U_PQ, it, 4)
                    count = [0]

                    def step(ins):
                        count[0] += 1
                        ins.then_inc(k_step, 1)
                        dve.wait_ge(k_step, it * (2 * STEPS) + (count[0] + 1))

                    def carry():
                        nc.vector.tensor_copy(pad[:, 0:1], pad[:, 1:2])

                    def best16(src, cut, val, idx):
                        for t in range(TT):
                            m = nc.vector.max(val[:, t, 0:KH], src[:, t])
                        step(m)
                        carry()
                        for t in range(TT):
                            nc.vector.max_index(idx[:, t, 0:KH], val[:, t, 0:KH], src[:, t])
                            m = nc.vector.match_replace(cut[:, t], val[:, t, 0:KH], src[:, t], -3.0e38)
                        step(m)
                        carry()
                        for t in range(TT):
                            m = nc.vector.max(val[:, t, KH:TOPK], cut[:, t])
                        step(m)
                        carry()
                        for t in range(TT):
                            m = nc.vector.max_index(idx[:, t, KH:TOPK], val[:, t, KH:TOPK], cut[:, t])
                        step(m)
                    for hh in range(2):
                        head = it * 2 + hh
                        for u in range(2):
                            do_lo(dve, U, 2 * hh + u)
                        for u in range(2):
                            dve.wait_ge(s_bank[0], it * 4 + (2 * hh + u + 2))
                            carry()
                            best16(s_sb[:, u], s_cut, sv[:, u], si[:, u])
                            dve.sem_inc(slot_free, 1)
                            if u == 0:
                                step(nc.vector.tensor_scalar(sf[:, 0], si[:, 0], float(NKEYS), None, ALU.mult))
                            else:
                                nc.vector.tensor_copy(sf[:, 1], si[:, 1]).then_inc(sf_ready, 1)
                        step(pair_sums(nc.vector.tensor_tensor, cv, sv[:, 0], sv[:, 1]))
                        carry()
                        best16(cv, cv_cut, tv, tp)
                        nc.vector.tensor_copy(tpf, tp).then_inc(k_step, 1)
                        nc.vector.tensor_tensor(te, tv, tv[:, :, 0:1].broadcast_to([P, TT, TOPK]), ALU.subtract
                                                ).then_inc(ts_ready, 1)
                        count[0] += 1
                        dve.wait_ge(k_step, it * (2 * STEPS) + (count[0] + 1))
                        dve.wait_ge(cid_ready, head + 1)
                        for t in range(TT):
                            step(nc.vector.tensor_tensor(onehot, iota[:, 0:CAND].rearrange("p (o c) -> p o c", o=1)
                                                         .broadcast_to([P, TOPK, CAND]),
                                                         tpf[:, t].rearrange("p (k o) -> p k o", o=1)
                                                         .broadcast_to([P, TOPK, CAND]), ALU.is_equal))
                            step(nc.vector.tensor_tensor(onehot, onehot, cid[:, t:t + 1].broadcast_to([P, TOPK, CAND]),
                                                         ALU.mult))
                            step(nc.vector.reduce_sum(eid[:, t, ds(head * TOPK, TOPK)], onehot, AX_X))
                        dve.wait_ge(te_ready, head + 1)
                        step(nc.vector.reduce_sum(tsum, te, AX_X))
                        step(nc.vector.reciprocal(tsum, tsum))
                        nc.vector.tensor_tensor(gate[:, :, ds(head * TOPK, TOPK)], te,
                                                tsum.rearrange("p (t o) -> p t o", o=1).broadcast_to([P, TT, TOPK]),
                                                ALU.mult).then_inc(head_done, 1)
                        assert count[0] == STEPS * (hh + 1), count
                dve.wait_ge(head_done, PH)
                nc.vector.tensor_copy(ei, eid).then_inc(head_done, 1)
                dve.wait_ge(head_done, PH + 1)
                nc.vector.tensor_scalar(te_ji, ei, NKEYS - 1, None, ALU.bitwise_and)
                nc.vector.tensor_scalar(ei, ei, 7, None, ALU.logical_shift_right).then_inc(head_done, 1)
                dve.wait_ge(head_done, PH + 2)
                nc.vector.tensor_copy(eid, ei)
                nc.vector.tensor_copy(te_j, te_ji).then_inc(tab_done, 1)


        TB = 64
        NB = T // TB
        c_dram = nc.dram_tensor("gates_scratch", (NB, P, NKEYS * TB), F32, kind="Internal").ap()
        A = Arena()
        c_sb = A.take(2, NKEYS, TB)
        oh_i = A.take(RING, NKEYS)
        onehot_ready, onehot_used, c_bank, c_stored = sem("onehot_ready"), sem("onehot_used"), sem("c_bank"), [sem("c_stored0"), sem("c_stored1")]
        Q4 = 4
        u_in, uh, ul = [sem("u_in0"), sem("u_in1")], sem("uh"), sem("ul")

        def load_u(sp, p, b):
            sp.dma_start(w_raw[:, b], u_late[ds(p, 1)].rearrange("o p (c k) -> p (o c) k", c=DC)).then_inc(u_in[b], 16)

        QUADS, HALVES = 2 * TB // Q4, 8
        assert HALVES * RING == 2 * TB and EARLY == PH * EARLY_PQ + NB // 2 * HALVES // 2
        with nc.Block() as block:
            @block.vector
            def _(dve):
                dve.sem_inc(onehot_used, RING // Q4)
                with dve.Fori(0, T // RING) as it:
                    for q in range(RING // Q4):
                        dve.wait_ge(onehot_used, it * (RING // Q4) + (q + 1))
                        for k in range(q * Q4, (q + 1) * Q4):
                            t = it * RING + k
                            nc.vector.tensor_scalar(oh_i[:, k], iota, i_t[:, ds(t, 1)], None, ALU.is_equal)
                            m = nc.vector.tensor_scalar(oh_j[:, k], iota, j_t[:, ds(t, 1)], gate_t[:, ds(t, 1)],
                                                        ALU.is_equal, ALU.mult)
                        m.then_inc(onehot_ready, 1)

            @block.tensor
            def _(pe):
                with pe.Fori(0, NB // 2) as blk:
                    E = Unit(PH * EARLY_PQ, blk, HALVES // 2)
                    for half in range(HALVES):
                        for q in range(RING // Q4):
                            n = blk * QUADS + (half * (RING // Q4) + q + 1)
                            pe.wait_ge(onehot_ready, n)
                            pe.wait_ge(c_bank, n)
                            for k in range(Q4):
                                m = nc.tensor.matmul(psum[:, q, k * P:(k + 1) * P], oh_i[:, q * Q4 + k],
                                                     oh_j[:, q * Q4 + k], start=True, stop=True)
                            m.then_inc(onehot_used, 1)
                        early_pe(pe, E, half // 2, half % 2)

            @block.gpsimd
            def _(pool):
                for p in range(2):
                    pool.wait_ge(uh, p + 1)
                    nc.gpsimd.tensor_tensor(w_split[:, p, 1], w_raw[:, p], w_split[:, p, 0].bitcast(F32), ALU.subtract
                                            ).then_inc(ul, 1)
                with pool.Fori(0, NB // 2) as blk:
                    E = Unit(PH * EARLY_PQ, blk, HALVES // 2)
                    for k in range(HALVES // 2):
                        early_lo(pool, E.at(k) + EARLY_LEAD, k % 2)

            @block.scalar
            def _(act):
                act.sem_inc(c_bank, RING // Q4)
                for s in range(2):
                    act.sem_inc(c_stored[s], 16)
                for p in range(2):
                    act.wait_ge(u_in[p], 16)
                    nc.scalar.activation(w_split[:, p, 0], w_raw[:, p], ACT.Copy).then_inc(uh, 1)
                with act.Fori(0, NB // 2) as blk:
                    E = Unit(PH * EARLY_PQ, blk, HALVES // 2)
                    for half in range(HALVES):
                        s, part = half // (HALVES // 2), half % (HALVES // 2)
                        if part == 0:
                            act.wait_ge(c_stored[s], blk * 16 + 16)
                        for q in range(RING // Q4):
                            act.wait_ge(onehot_used, blk * QUADS + (half * (RING // Q4) + q + RING // Q4 + 1))
                            t = part * RING + q * Q4
                            nc.scalar.activation(c_sb[:, s, :, t:t + Q4].rearrange("p j t -> p t j"),
                                                 psum[:, q, :].rearrange("p (t j) -> p t j", t=Q4), ACT.Copy
                                                 ).then_inc(c_bank, 1)
                        early_act(act, E, half // 2, half % 2)

            @block.sync
            def _(sp):
                for p in range(2):
                    load_u(sp, p, p)
                with sp.Fori(0, NB // 2) as blk:
                    E = Unit(PH * EARLY_PQ, blk, HALVES // 2)
                    for s in range(2):
                        for k in range(HALVES // 4):
                            early_sync(sp, E, s * (HALVES // 4) + k)
                        sp.wait_ge(c_bank, blk * QUADS + ((s + 1) * (TB // Q4) + RING // Q4))
                        sp.dma_start(c_dram[ds(blk * 2 + s, 1)].rearrange("o p n -> p (o n)"),
                                     c_sb[:, s].rearrange("p j t -> p (j t)")).then_inc(c_stored[s], 16)
        A = Arena()
        LATE, EARLY_LOT = 0, 1
        y_sb = A.take(TT, D)
        v_raw = A.take(4, D).rearrange("p (b s) n -> p b s n", b=2)
        c_lot = A.take(4, T).rearrange("p (b s) t -> p b s t", b=2)
        gl_early = A.take(2, T)
        gl_late = arena[:, ARENA - T:ARENA]
        v_split, g_split = room.take(("v_split", [P, 2, 2, 2, D], F32R), ("g_split", [P, 2, 2, 2, T], F32R))
        PAIRS = EARLY
        pair_in = [sem("pair_in0"), sem("pair_in1")]
        PAIR_LOADS = 16 * 5
        vh, vl = sem("vh"), sem("vl")
        act_done, gelu_done, g_mul, gh_done, gl_done = (sem(n) for n in ("act_done", "gelu_done", "g_mul", "gh_done", "gl_done"))
        y_done, y_free, y_zero = sem("y_done"), [sem("y_free%d" % k) for k in range(4)], sem("y_zero")
        Y_N = 2 * TT

        with nc.Block() as block:
            @block.gpsimd
            def _(pool):
                for s in range(2):
                    pool.wait_ge(c_stored[s], 16 * (NB // 2 + 1))
                nc.gpsimd.memset(y_sb, 0.0).then_inc(y_zero, 1)

            @block.sync
            def _(sp):
                def load_pair(p, b):
                    for s in (EARLY_LOT, LATE):
                        j = p * 2 + s
                        sp.dma_start(v_raw[:, b, s], v_t[ds(j, 1)].rearrange("o p n -> p (o n)")).then_inc(pair_in[b], 16)
                        sp.dma_start(c_lot[:, b, s].rearrange("p (b t) -> p b t", b=NB),
                                     c_dram[:, :, ds(j * TB, TB)].rearrange("b p t -> p b t")).then_inc(pair_in[b], 16)
                    sp.dma_start(gl_early[:, b], gl_dram[ds(p, 1)].rearrange("o p t -> p (o t)")).then_inc(pair_in[b], 16)

                def step(p, b, with_u=True):
                    sp.wait_ge(gl_done, p * 2 + 2)
                    sp.wait_ge(vl, p * 2 + 2)
                    load_pair(p + 2, b)
                    if with_u:
                        sp.wait_ge(ul, p + 2)
                        load_u(sp, p + 3, 1 - b)
                for s in range(2):
                    sp.wait_ge(c_stored[s], 16 * (NB // 2 + 1))
                    sp.wait_ge(e_out[s], 16 * (EARLY // 2 + 1))
                load_pair(0, 0)
                load_u(sp, 2, 0)
                load_pair(1, 1)
                with sp.Fori(0, PAIRS // 2 - 2) as it:
                    for b in range(2):
                        step(it * 2 + b, b)
                step(PAIRS - 4, 0)
                step(PAIRS - 3, 1, False)

            @block.tensor
            def _(pe):
                def late(p, b):
                    pe.wait_ge(ul, p + 1)
                    pe.wait_ge(gelu_done, p + 1)
                    for t in range(2):
                        for d in range(DC):
                            for i, (wh, ah) in enumerate(((0, 0), (0, 1), (1, 0))):
                                m = nc.tensor.matmul(psum[:, 2 * b + t, 0:HALF], w_split[:, b, wh, d, :],
                                                     acts_a[:, ah, d, t * HALF:(t + 1) * HALF],
                                                     start=(d == 0 and i == 0), stop=(d == DC - 1 and i == 2))
                    m.then_inc(act_done, 1)

                def y_pair(p, b):
                    pe.wait_ge(gl_done, p * 2 + 2)
                    pe.wait_ge(vl, p * 2 + 2)
                    for n in range(Y_N):
                        t, c = n // 2, n % 2
                        pe.wait_ge(y_free[n % 4], p * (Y_N // 4) + (n // 4 + 1))
                        k = 0
                        for j in range(2):
                            for gh, vh_ in ((0, 0), (0, 1), (1, 0)):
                                m = nc.tensor.matmul(psum[:, 4 + n % 4, :], g_split[:, b, j, gh, t * P:(t + 1) * P],
                                                     v_split[:, b, j, vh_, c * 512:(c + 1) * 512],
                                                     start=(k == 0), stop=(k == 5))
                                k += 1
                        m.then_inc(y_done, 1)
                late(0, 0)
                with pe.Fori(0, PAIRS // 2 - 1) as it:
                    for b in range(2):
                        late(it * 2 + (b + 1), 1 - b)
                        y_pair(it * 2 + b, b)
                late(PAIRS - 1, 1)
                y_pair(PAIRS - 2, 0)
                y_pair(PAIRS - 1, 1)

            @block.scalar
            def _(act):
                def u_hi(p, b, h):
                    act.wait_ge(u_in[b], h * 16 + 16)
                    act.wait_ge(act_done, p - 1)
                    nc.scalar.activation(w_split[:, b, 0], w_raw[:, b], ACT.Copy).then_inc(uh, 1)

                def heads(p, b, h):
                    act.wait_ge(pair_in[b], h * PAIR_LOADS + PAIR_LOADS)
                    act.wait_ge(y_done, p * Y_N + 1)
                    for s in range(2):
                        nc.scalar.activation(v_split[:, b, s, 0], v_raw[:, b, s], ACT.Copy).then_inc(vh, 1)
                    act.wait_ge(g_mul, p * 2 + 1)
                    nc.scalar.activation(g_split[:, b, EARLY_LOT, 0], gl_early[:, b], ACT.Copy).then_inc(gh_done, 1)

                def gelu_late(p, b, first=False):
                    act.wait_ge(act_done, p + 1)
                    if not first:
                        act.wait_ge(gl_done, p * 2)
                    nc.scalar.activation(two(gl_late), psum[:, 2 * b:2 * b + 2, 0:HALF], ACT.Gelu).then_inc(gelu_done, 1)
                    act.wait_ge(g_mul, p * 2 + 2)
                    nc.scalar.activation(g_split[:, b, LATE, 0], gl_late, ACT.Copy).then_inc(gh_done, 1)
                act.sem_inc(gelu_done, 2)
                act.sem_inc(y_done, Y_N + 1)
                heads(0, 0, 0)
                gelu_late(0, 0, True)
                with act.Fori(0, PAIRS // 2 - 1) as it:
                    for b in range(2):
                        heads(it * 2 + (b + 1), 1 - b, it + b)
                        u_hi(it * 2 + (b + 2), b, it + 1)
                        gelu_late(it * 2 + (b + 1), 1 - b)
                heads(PAIRS - 1, 1, PAIRS // 2 - 1)
                gelu_late(PAIRS - 1, 1)

            @block.vector
            def _(dve):
                def u_lo(p, b):
                    dve.wait_ge(uh, p + 1)
                    nc.vector.tensor_tensor(w_split[:, b, 1], w_raw[:, b], w_split[:, b, 0].bitcast(F32), ALU.subtract
                                            ).then_inc(ul, 1)

                def g_lo(p, b, lot, gl, count):
                    dve.wait_ge(gh_done, p * 2 + count)
                    nc.vector.tensor_tensor(g_split[:, b, lot, 1], gl, g_split[:, b, lot, 0].bitcast(F32), ALU.subtract
                                            ).then_inc(gl_done, 1)

                def rests(p, b, h):
                    dve.wait_ge(pair_in[b], h * PAIR_LOADS + PAIR_LOADS)
                    nc.vector.tensor_tensor(gl_early[:, b], gl_early[:, b], c_lot[:, b, EARLY_LOT], ALU.mult).then_inc(g_mul, 1)
                    for s in range(2):
                        dve.wait_ge(vh, p * 2 + (s + 1))
                        nc.vector.tensor_tensor(v_split[:, b, s, 1], v_raw[:, b, s], v_split[:, b, s, 0].bitcast(F32),
                                                ALU.subtract).then_inc(vl, 1)
                    g_lo(p, b, EARLY_LOT, gl_early[:, b], 1)

                def times_gates(p, b):
                    dve.wait_ge(gelu_done, p + 3)
                    nc.vector.tensor_tensor(gl_late, gl_late, c_lot[:, b, LATE], ALU.mult).then_inc(g_mul, 1)

                def adds(p, n0, n1):
                    for n in range(n0, n1):
                        t, c = n // 2, n % 2
                        dve.wait_ge(y_done, p * Y_N + (n + Y_N + 2))
                        dve.wait_ge(y_free[n % 4], p * (Y_N // 4) + (n // 4 + 1))
                        y = y_sb[:, t, c * 512:(c + 1) * 512]
                        nc.vector.tensor_tensor(y, y, psum[:, 4 + n % 4, :], ALU.add).then_inc(y_free[n % 4], 1)
                for k in range(4):
                    dve.sem_inc(y_free[k], 1)
                dve.wait_ge(y_zero, 1)
                rests(0, 0, 0)
                times_gates(0, 0)
                g_lo(0, 0, LATE, gl_late, 2)

                def step(p, b, h, last=False):
                    rests(p + 1, 1 - b, h)
                    if not last:
                        u_lo(p + 2, b)
                    times_gates(p + 1, 1 - b)
                    adds(p, 0, 2)
                    g_lo(p + 1, 1 - b, LATE, gl_late, 2)
                    adds(p, 2, Y_N)
                with dve.Fori(0, PAIRS // 2 - 1) as it:
                    for b in range(2):
                        step(it * 2 + b, b, it + b)
                step(PAIRS - 2, 0, PAIRS // 2 - 1, True)
                adds(PAIRS - 1, 0, Y_N)

        A = Arena()
        y_in = A.take(TT, D)
        x2 = A.take(DC, T)
        d_x2, yt_done, yt_free, out_stored = sem("d_x2"), sem("yt_done"), sem("yt_free"), sem("out_stored")
        n3 = Norm("n3", x2, lambda d, g: vec[:, V_GF + d:V_GF + d + 1], None, None, norm_work(A))
        with nc.Block() as block:
            @block.sync
            def _(sp):
                sp.dma_start(arena[:, TT * D:TT * D + DC * T], x1_dram).then_inc(d_x2, 16)
                for d in range(DC):
                    sp.wait_ge(n3.n_hf, 2 * d + 2)
                    sp.dma_start(out[:, d * T:(d + 1) * T], x2[:, d]).then_inc(out_stored, 16)
                sp.wait_ge(out_stored, 16 * DC)

            @block.tensor
            def _(pe):
                for d in range(DC):
                    if d >= 2:
                        pe.wait_ge(yt_free, d - 1)
                    for t in range(TT):
                        b = 2 * (d % 2) + t // 4
                        m = nc.tensor.transpose(psum[:, b, t % 4 * P:t % 4 * P + P], y_in[:, t, d * P:(d + 1) * P], ident)
                    m.then_inc(yt_done, 1)
                    if d >= 2:
                        n3.sums(pe, d - 2)
                for d in range(DC - 2, DC):
                    n3.sums(pe, d)

            @block.scalar
            def _(act):
                for d in range(DC):
                    act.wait_ge(yt_free, d + 1)
                    n3.square(act, d)
                n3.root(act)

            @block.vector
            def _(dve):
                dve.wait_ge(d_x2, 16)
                for d in range(DC):
                    dve.wait_ge(yt_done, d + 1)
                    for g, (t0, t1) in enumerate(GROUPS):
                        x = x2[:, d, t0:t1]
                        m = nc.vector.scalar_tensor_tensor(out=x, in0=psum[:, 2 * (d % 2) + g, 0:t1 - t0],
                                                           scalar=modcol(GATE2, d, g), in1=x, op0=ALU.mult, op1=ALU.add)
                    m.then_inc(yt_free, 1)
                n3.stats_dve(dve)
                n3.apply_dve(dve)


def _constants():
    c = np.zeros((P, C_N), np.float32)
    row, col = np.arange(P)[:, None], np.arange(P)[None, :]
    c[:, C_ID:C_ID + P] = row == col
    c[:, C_ONE:C_ONE + P] = 1.0
    c[:, C_IOTA:C_IOTA + P] = col
    c[:, C_SLOPE:C_SLOPE + HEADS] = np.exp2(-8.0 * np.arange(1, HEADS + 1) / HEADS)
    for l in range(LEVELS):
        m = (((row ^ col) >> l) == 1).astype(np.uint32)
        c[:, C_MASK + l * P:C_MASK + (l + 1) * P] = m.view(np.float32)
    d = np.abs(row - np.arange(3 * P)[None, :] + P)
    c[:, C_DIST:C_DIST + 3 * P] = np.where(d <= P, -d, -1e30)
    return c


def _columns(v):
    return np.reshape(v, (-1, P)).T


def _units(w):
    k, n = w.shape
    return w.reshape(DC, P, n // P, P).transpose(2, 1, 0, 3).reshape(n // P, P, D)


def arrays_of(i):
    i = {k: np.asarray(v) for k, v in i.items()}
    x = np.concatenate([i["x_prompt"][0], i["x_sample"][0]], 0)
    x_t = x.T.reshape(DC, P, T).transpose(1, 0, 2)
    c = np.stack([_columns(i["c_prompt"][0]), _columns(i["c_sample"][0])], -1).reshape(P, 16)
    vecs = np.concatenate(
        [_columns(i["b_mod"][0]), _columns(i["g_norm1"][0]), _columns(i["g_norm2"][0]), _columns(i["g_final"]),
         _columns(i["g_hnorm"][0]), _columns(i["p_lb_fwd"][0]), _columns(i["p_lb_fwd"][1]),
         _columns(i["p_lb_bwd"][0]), _columns(i["p_lb_bwd"][1]), c,
         np.broadcast_to(i["att_sink"][0][None, :], (P, HEADS))], 1)
    w = i["w_in"][0]
    qa, kv = _units(w[:, 0:D]), w[:, D:D + 512]
    n0 = D + 512
    qh, zf, zb, ih, gh, ga, gb = (_units(w[:, n0 + k * D:n0 + (k + 1) * D]) for k in range(7))
    order = []
    for g in range(KV_HEADS):
        pair = np.concatenate([kv[:, g * HD:(g + 1) * HD], kv[:, 256 + g * HD:256 + (g + 1) * HD]], 1)
        order += [_units(pair)[0], qa[2 * g], qa[2 * g + 1]]
    order += list(ga) + list(_units(i["w_o_att"][0]))
    for h in range(H_HEADS):
        order += [zf[h], zb[h], qh[h], gh[h], ih[h]]
    order += list(gb) + list(_units(i["w_o_hgrn"][0])) + list(_units(i["w_out"][0])) + list(_units(i["w_pq"][0]))
    order += [order[k] for k in range(LEAD)]
    keys_t = i["peer_keys"][0].reshape(2 * PH, NKEYS, P).transpose(2, 0, 1).reshape(P, 2 * PH * NKEYS)
    u_t = i["peer_u"][0].reshape(NKEYS, NKEYS, DC, P).transpose(1, 3, 2, 0).reshape(NKEYS, P, D)
    u_early = np.concatenate([u_t[1::2], u_t[1:1 + 2 * EARLY_LEAD:2]], 0)
    v_t = i["peer_v"][0].reshape(NKEYS, NKEYS, D).transpose(1, 0, 2)
    return {"x_t": x_t.reshape(P, DC * T), "vecs": vecs, "consts": _constants(), "w_mod": _units(i["w_mod"][0]),
            "w_str": np.stack(order), "keys_t": keys_t, "u_late": u_t[0::2],
            "u_early": u_early, "v_t": v_t}


def kernel(**inputs):
    import concourse.bacc as _bacc
    from concourse.bass_utils import run_bass_kernel_spmd as _run

    nc = _bacc.Bacc("TRN2", target_bir_lowering=False, num_devices=1)
    arrays = {k: np.ascontiguousarray(v) for k, v in arrays_of(inputs).items()}
    args = [nc.dram_tensor(k, v.shape, F32, kind="ExternalInput").ap() for k, v in arrays.items()]
    out = nc.dram_tensor("y_t", (P, DC * T), F32, kind="ExternalOutput").ap()
    encoder_kernel(nc, *args, out)
    y = _run(nc, [arrays], core_ids=[0]).results[0]["y_t"]
    y = np.asarray(y).reshape(P, DC, T).transpose(2, 1, 0).reshape(T, D)
    return y[None, 0:T_PROMPT], y[None, T_PROMPT:T]
```
